# Optimizing a Trainium2 kernel written in Bass

```python
import math
import numpy as np
import jax
import jax.numpy as jnp
from jax import lax
import jax, jax.numpy as jnp

D_MODEL = 1024
BATCH = 1
SEQ = 256
DEPTH = 1

GRID_W = 64
CTX_LEN = 256
HEAD_DIM = 64
ROPE_THETA = 10000.0
NORM_EPS = 1e-6
F32 = jnp.float32

A_HEADS = 4
A_QK = HEAD_DIM
A_V = 2 * HEAD_DIM
A_QBLOCK = 128
B_HEADS = 4
B_DK = HEAD_DIM // 2
B_DV = HEAD_DIM
B_GATE_RANK = 16
B_GATE_TAU = 16.0
B_CHUNK = 64
C_HEADS = 4
C_DH = HEAD_DIM
NA_ROWS = 8
NA_COLS = 16

A_WIDTH = A_HEADS * A_V
B_WIDTH = B_HEADS * B_DV
C_WIDTH = C_HEADS * C_DH
MIX_WIDTH = A_WIDTH + B_WIDTH + C_WIDTH

IN_SIZES = (A_HEADS * 2 * A_QK, A_HEADS * 2 * A_QK, A_WIDTH,
            B_HEADS * B_DK, B_HEADS * B_DK, B_WIDTH, B_WIDTH, 2 * B_GATE_RANK,
            C_WIDTH, C_WIDTH, C_WIDTH)
IN_WIDTH = sum(IN_SIZES)

N_GROUPS = 4
EXPERTS_PER_GROUP = 8
N_EXPERTS = N_GROUPS * EXPERTS_PER_GROUP
TOP_K = 2
EXPERT_HIDDEN = 512
MOE_BLOCK = 128


def rms_norm(x, g):
    xf = x.astype(F32)
    y = xf * lax.rsqrt(jnp.mean(xf * xf, axis=-1, keepdims=True) + NORM_EPS)
    return (y * g.astype(F32)).astype(x.dtype)

def split_in(p):
    return jnp.split(p, np.cumsum(IN_SIZES)[:-1].tolist(), axis=-1)

def axial_rope_tables(n_tokens, dtype):
    t = jnp.arange(n_tokens)
    row = (t // GRID_W).astype(F32)
    col = (t % GRID_W).astype(F32)
    n_freq = HEAD_DIM // 4
    inv = ROPE_THETA ** (-jnp.arange(n_freq, dtype=F32) / n_freq)
    ang_r = row[:, None] * inv
    ang_c = col[:, None] * inv
    return (jnp.cos(ang_r).astype(dtype), jnp.sin(ang_r).astype(dtype),
            jnp.cos(ang_c).astype(dtype), jnp.sin(ang_c).astype(dtype))

def apply_axial_rope(x, tabs):
    cr, sr, cc, sc = (tb.reshape((tb.shape[0],) + (1,) * (x.ndim - 3) + (tb.shape[1],)) for tb in tabs)
    x1, x2, x3, x4 = jnp.split(x, 4, axis=-1)
    return jnp.concatenate([x1 * cr - x2 * sr, x2 * cr + x1 * sr,
                            x3 * cc - x4 * sc, x4 * cc + x3 * sc], axis=-1)

def diff_attention(q, k, v, qc, kc, vc, lam, lam_init, g_sub, need_ctx):
    B_, S = q.shape[:2]
    L = qc.shape[1]
    scale = A_QK ** -0.5
    k_all = jnp.concatenate([kc, k], axis=1)
    v_all = jnp.concatenate([vc, v], axis=1)

    def attend(qb, kb, vb):
        s = jnp.einsum('bqhmd,bkhmd->bhmqk', qb, kb).astype(F32) * scale
        p = jax.nn.softmax(s, axis=-1)
        d = p[:, :, 0] - lam * p[:, :, 1]
        return jnp.einsum('bhqk,bkhv->bqhv', d.astype(vb.dtype), vb)

    nb = S // A_QBLOCK
    qblocks = jnp.moveaxis(q.reshape((B_, nb, A_QBLOCK) + q.shape[2:]), 1, 0)
    o = lax.map(lambda qb: attend(qb, k_all, v_all), qblocks)
    o = jnp.moveaxis(o, 0, 1).reshape(B_, S, A_HEADS, A_V)
    out = (rms_norm(o, g_sub) * (1.0 - lam_init)).reshape(B_, S, A_WIDTH)
    out_c = None
    if need_ctx:
        oc = attend(qc, kc, vc)
        out_c = (rms_norm(oc, g_sub) * (1.0 - lam_init)).reshape(B_, L, A_WIDTH)
    return out, out_c

def gla_scan(q, k, v, log_a, s0):
    B_, H, T, dk = q.shape
    n = T // B_CHUNK

    def chunks(t):
        return jnp.moveaxis(t.reshape(B_, H, n, B_CHUNK, t.shape[-1]), 2, 0)

    causal = jnp.tril(jnp.ones((B_CHUNK, B_CHUNK), dtype=bool))

    def step(s, inp):
        qc, kc, vc, ac = inp
        b = jnp.cumsum(ac, axis=2)
        rel = jnp.where(causal[:, :, None], b[:, :, :, None, :] - b[:, :, None, :, :], -jnp.inf)
        a_intra = jnp.einsum('bhtsd,bhsd->bhts', qc[:, :, :, None, :] * jnp.exp(rel), kc)
        o = (jnp.einsum('bhts,bhsv->bhtv', a_intra, vc)
             + jnp.einsum('bhtd,bhdv->bhtv', qc * jnp.exp(b), s))
        b_end = b[:, :, -1, :]
        s = (jnp.exp(b_end)[..., None] * s
             + jnp.einsum('bhsd,bhsv->bhdv', kc * jnp.exp(b_end[:, :, None, :] - b), vc))
        return s, o

    s_final, o = lax.scan(step, s0, (chunks(q), chunks(k), chunks(v), chunks(log_a)))
    o = jnp.moveaxis(o, 0, 2).reshape(B_, H, T, v.shape[-1])
    return o, s_final

def gla_mixer(q, k, v, r, glow, qc, kc, vc, rc, glowc, w_dec, b_dec, g_out, need_ctx):
    B_ = q.shape[0]

    def heads(t, d):
        return jnp.transpose(t.reshape(t.shape[0], t.shape[1], -1, d), (0, 2, 1, 3)).astype(F32)

    def decay(gl, direction):
        z = gl[..., direction * B_GATE_RANK:(direction + 1) * B_GATE_RANK] @ w_dec[direction] + b_dec[direction]
        return heads(jax.nn.log_sigmoid(z.astype(F32)) / B_GATE_TAU, B_DK)

    def flip(t):
        return jnp.flip(t, axis=2)

    scale = B_DK ** -0.5
    ql, kl, vl = heads(q, B_DK) * scale, heads(k, B_DK), heads(v, B_DV)
    qx, kx, vx = heads(qc, B_DK) * scale, heads(kc, B_DK), heads(vc, B_DV)
    s0 = jnp.zeros((B_, B_HEADS, B_DK, B_DV), F32)
    ox_f, sx_f = gla_scan(qx, kx, vx, decay(glowc, 0), s0)
    ol_f, _ = gla_scan(ql, kl, vl, decay(glow, 0), sx_f)
    ox_b, sx_b = gla_scan(flip(qx), flip(kx), flip(vx), flip(decay(glowc, 1)), s0)
    ol_b, _ = gla_scan(flip(ql), flip(kl), flip(vl), flip(decay(glow, 1)), sx_b)

    def readout(o, gate):
        o = jnp.transpose(rms_norm(o, g_out), (0, 2, 1, 3)).reshape(gate.shape[0], gate.shape[1], B_WIDTH)
        return (o * jax.nn.silu(gate.astype(F32))).astype(gate.dtype)

    out = readout(ol_f + flip(ol_b), r)
    out_c = readout(ox_f + flip(ox_b), rc) if need_ctx else None
    return out, out_c

def neighborhood_attention(q, k, v, qc, kc, vc, rpb, need_ctx):
    B_, S, H, dh = q.shape
    L = qc.shape[1]
    rows = S // GRID_W
    wr = min(NA_ROWS, rows)
    scale = dh ** -0.5

    def grid(t):
        return jnp.transpose(t.reshape(B_, rows, GRID_W, H, dh), (0, 3, 1, 2, 4))

    qg, kg, vg = grid(q), grid(k), grid(v)
    r = jnp.arange(rows)
    row_idx = jnp.clip(r - wr // 2, 0, rows - wr)[:, None] + jnp.arange(wr)
    cq = jnp.arange(GRID_W)
    col_start = jnp.clip(cq - NA_COLS // 2, 0, GRID_W - NA_COLS)
    col_mask = (cq[None, :] >= col_start[:, None]) & (cq[None, :] < col_start[:, None] + NA_COLS)
    k_rows = kg[:, :, row_idx]
    v_rows = vg[:, :, row_idx]
    s_nb = jnp.einsum('bhrqd,bhrwkd->bhrqwk', qg, k_rows).astype(F32) * scale
    dr = row_idx - r[:, None] + (NA_ROWS - 1)
    dc = jnp.clip(cq[None, :] - cq[:, None], -(NA_COLS - 1), NA_COLS - 1) + (NA_COLS - 1)
    bias = rpb[:, dr[:, None, :, None], dc[None, :, None, :]].astype(F32)
    s_nb = jnp.where(col_mask[:, None, :], s_nb + bias, -jnp.inf)
    s_c = jnp.einsum('bhrqd,bchd->bhrqc', qg, kc).astype(F32) * scale
    n_nb = wr * GRID_W
    p = jax.nn.softmax(jnp.concatenate([s_nb.reshape(B_, H, rows, GRID_W, n_nb), s_c], axis=-1), axis=-1)
    p_nb = p[..., :n_nb].reshape(s_nb.shape).astype(v.dtype)
    p_c = p[..., n_nb:].astype(v.dtype)
    o = (jnp.einsum('bhrqwk,bhrwkd->bhrqd', p_nb, v_rows)
         + jnp.einsum('bhrqc,bchd->bhrqd', p_c, vc))
    out = jnp.transpose(o, (0, 2, 3, 1, 4)).reshape(B_, S, H * dh)
    out_c = None
    if need_ctx:
        sc = jnp.einsum('bqhd,bkhd->bhqk', qc, kc).astype(F32) * scale
        out_c = jnp.einsum('bhqk,bkhd->bqhd', jax.nn.softmax(sc, axis=-1).astype(vc.dtype), vc).reshape(B_, L, H * dh)
    return out, out_c

def hier_moe(h, w_rg, b_rg, w_re, b_re, w_up, w_down):
    n_tok, D = h.shape
    n_assign = n_tok * TOP_K
    n_blocks = -(-(n_assign + N_EXPERTS * (MOE_BLOCK - 1)) // MOE_BLOCK)
    logit_g = (h @ w_rg + b_rg).astype(F32)
    grp = jnp.argmax(logit_g, axis=-1)
    p_grp = jnp.take_along_axis(jax.nn.softmax(logit_g, axis=-1), grp[:, None], axis=1)
    logit_e = (h @ w_re + b_re).astype(F32).reshape(n_tok, N_GROUPS, EXPERTS_PER_GROUP)
    logit_e = jnp.take_along_axis(logit_e, grp[:, None, None], axis=1)[:, 0]
    top_v, top_i = lax.top_k(logit_e, TOP_K)
    gate = jax.nn.softmax(top_v, axis=-1) * p_grp
    expert = (grp[:, None] * EXPERTS_PER_GROUP + top_i).reshape(-1)
    order = jnp.argsort(expert)
    e_sorted = expert[order]
    tok_sorted = order // TOP_K
    counts = jnp.bincount(expert, length=N_EXPERTS)
    padded = (counts + MOE_BLOCK - 1) // MOE_BLOCK * MOE_BLOCK
    start = jnp.cumsum(counts) - counts
    pad_end = jnp.cumsum(padded)
    pad_start = pad_end - padded
    dest = pad_start[e_sorted] + jnp.arange(n_assign) - start[e_sorted]
    buf = jnp.zeros((n_blocks * MOE_BLOCK, D), h.dtype).at[dest].set(h[tok_sorted])
    blk_expert = jnp.minimum(jnp.searchsorted(pad_end, jnp.arange(n_blocks) * MOE_BLOCK, side='right'), N_EXPERTS - 1)

    def expert_block(args):
        xb, e = args
        g, u = jnp.split(xb @ w_up[e], 2, axis=-1)
        return (jax.nn.silu(g) * u) @ w_down[e]

    y = lax.map(expert_block, (buf.reshape(n_blocks, MOE_BLOCK, D), blk_expert)).reshape(-1, D)
    y = y[dest] * gate.reshape(-1)[order][:, None].astype(h.dtype)
    return jax.ops.segment_sum(y, tok_sorted, num_segments=n_tok)

def hybrid_layer(x, xc, c_act, cc_act, rope, layer_idx, need_ctx,
                 w_mod, b_mod, g1, g2, w_in, w_out, lam, g_sub,
                 w_dec, b_dec, g_gla, rpb, w_rg, b_rg, w_re, b_re, w_up, w_down):
    B_, S, D = x.shape
    L = xc.shape[1]
    mod = (c_act @ w_mod + b_mod).reshape(B_, 6, 1, D)
    modc = (cc_act @ w_mod + b_mod).reshape(6, D)
    h = rms_norm(x, g1) * (1 + mod[:, 1]) + mod[:, 0]
    hc = rms_norm(xc, g1) * (1 + modc[1]) + modc[0]
    qa, ka, va, qb, kb, vb, rb, gb, qn, kn, vn = split_in(h @ w_in)
    qa_c, ka_c, va_c, qb_c, kb_c, vb_c, rb_c, gb_c, qn_c, kn_c, vn_c = split_in(hc @ w_in)

    lam_init = 0.8 - 0.6 * math.exp(-0.3 * layer_idx)
    lam_f = lam.astype(F32)
    lam_val = jnp.exp(jnp.sum(lam_f[0] * lam_f[1])) - jnp.exp(jnp.sum(lam_f[2] * lam_f[3])) + lam_init

    def a_qk(t):
        return t.reshape(t.shape[0], t.shape[1], A_HEADS, 2, A_QK)

    ya, ya_c = diff_attention(apply_axial_rope(a_qk(qa), rope), apply_axial_rope(a_qk(ka), rope),
                              va.reshape(B_, S, A_HEADS, A_V), a_qk(qa_c), a_qk(ka_c),
                              va_c.reshape(B_, L, A_HEADS, A_V), lam_val, lam_init, g_sub, need_ctx)
    yb, yb_c = gla_mixer(qb, kb, vb, rb, gb, qb_c, kb_c, vb_c, rb_c, gb_c, w_dec, b_dec, g_gla, need_ctx)

    def c_heads(t):
        return t.reshape(t.shape[0], t.shape[1], C_HEADS, C_DH)

    yn, yn_c = neighborhood_attention(c_heads(qn), c_heads(kn), c_heads(vn),
                                      c_heads(qn_c), c_heads(kn_c), c_heads(vn_c), rpb, need_ctx)
    x = x + mod[:, 2] * (jnp.concatenate([ya, yb, yn], axis=-1) @ w_out)
    h2 = rms_norm(x, g2) * (1 + mod[:, 4]) + mod[:, 3]
    if need_ctx:
        xc = xc + modc[2] * (jnp.concatenate([ya_c, yb_c, yn_c], axis=-1) @ w_out)
        h2c = rms_norm(xc, g2) * (1 + modc[4]) + modc[3]
        f = hier_moe(jnp.concatenate([h2.reshape(-1, D), h2c.reshape(-1, D)], axis=0),
                     w_rg, b_rg, w_re, b_re, w_up, w_down)
        x = x + mod[:, 5] * f[:B_ * S].reshape(B_, S, D)
        xc = xc + modc[5] * f[B_ * S:].reshape(B_, L, D)
    else:
        f = hier_moe(h2.reshape(-1, D), w_rg, b_rg, w_re, b_re, w_up, w_down)
        x = x + mod[:, 5] * f.reshape(B_, S, D)
    return x, xc

def first_inputs(seed: int = 0) -> dict:
    key = jax.random.key(seed)
    ks = jax.random.split(key, 23)
    D = D_MODEL

    def nrm(k, shape, s):
        return jax.random.normal(k, shape, F32) * s

    return {
        'x': nrm(ks[0], (BATCH, SEQ, D), 1.0),
        'c': nrm(ks[1], (BATCH, D), 1.0),
        'ctx': nrm(ks[2], (BATCH, CTX_LEN, D), 1.0),
        'c_ctx': nrm(ks[3], (D,), 1.0),
        'w_mod': nrm(ks[4], (DEPTH, D, 6 * D), 0.5 * D ** -0.5),
        'b_mod': nrm(ks[5], (DEPTH, 6 * D), 0.02),
        'norm1_g': 1.0 + nrm(ks[6], (DEPTH, D), 0.02),
        'norm2_g': 1.0 + nrm(ks[7], (DEPTH, D), 0.02),
        'w_in': nrm(ks[8], (DEPTH, D, IN_WIDTH), D ** -0.5),
        'w_out': nrm(ks[9], (DEPTH, MIX_WIDTH, D), MIX_WIDTH ** -0.5),
        'diff_lambda': nrm(ks[10], (DEPTH, 4, A_QK), 0.1),
        'diff_sub_g': 1.0 + nrm(ks[11], (DEPTH, A_V), 0.02),
        'gla_w_decay': nrm(ks[12], (DEPTH, 2, B_GATE_RANK, B_HEADS * B_DK), B_GATE_RANK ** -0.5),
        'gla_b_decay': nrm(ks[13], (DEPTH, 2, B_HEADS * B_DK), 0.1),
        'gla_norm_g': 1.0 + nrm(ks[14], (DEPTH, B_DV), 0.02),
        'na_rel_bias': nrm(ks[15], (DEPTH, C_HEADS, 2 * NA_ROWS - 1, 2 * NA_COLS - 1), 0.02),
        'w_router_group': nrm(ks[16], (DEPTH, D, N_GROUPS), D ** -0.5),
        'b_router_group': nrm(ks[17], (DEPTH, N_GROUPS), 0.01),
        'w_router_expert': nrm(ks[18], (DEPTH, D, N_EXPERTS), D ** -0.5),
        'b_router_expert': nrm(ks[19], (DEPTH, N_EXPERTS), 0.01),
        'w_expert_up': nrm(ks[20], (DEPTH, N_EXPERTS, D, 2 * EXPERT_HIDDEN), D ** -0.5),
        'w_expert_down': nrm(ks[21], (DEPTH, N_EXPERTS, EXPERT_HIDDEN, D), EXPERT_HIDDEN ** -0.5),
        'final_g': 1.0 + nrm(ks[22], (D,), 0.02),
    }

def first_block(x, c, ctx, c_ctx, w_mod, b_mod, norm1_g, norm2_g, w_in, w_out,
              diff_lambda, diff_sub_g, gla_w_decay, gla_b_decay, gla_norm_g, na_rel_bias,
              w_router_group, b_router_group, w_router_expert, b_router_expert,
              w_expert_up, w_expert_down, final_g):
    rope = axial_rope_tables(x.shape[1], x.dtype)
    c_act = jax.nn.silu(c)
    cc_act = jax.nn.silu(c_ctx)
    xc = ctx
    for l in range(DEPTH):
        x, xc = hybrid_layer(x, xc, c_act, cc_act, rope, l, l < DEPTH - 1,
                             w_mod[l], b_mod[l], norm1_g[l], norm2_g[l], w_in[l], w_out[l],
                             diff_lambda[l], diff_sub_g[l], gla_w_decay[l], gla_b_decay[l],
                             gla_norm_g[l], na_rel_bias[l], w_router_group[l], b_router_group[l],
                             w_router_expert[l], b_router_expert[l], w_expert_up[l], w_expert_down[l])
    return rms_norm(x, final_g)


DEPTH_2 = 2

CHUNK = 64
Q_BLOCK = 128
EPS = 1e-6

A_HEADS_2 = 8
A_NOPE = 64
A_ROPE = 32
A_VDIM = 64
A_QLORA = 256
A_KVLORA = 128

B_DIM = 64

POOL_WINDOWS = (2, 4, 8, 16)
POOL_CH = 64

A_WIDTH_2 = A_HEADS_2 * A_VDIM
B_WIDTH_2 = B_HEADS * B_DIM
C_WIDTH_2 = len(POOL_WINDOWS) * POOL_CH
D_MIX = A_WIDTH_2 + B_WIDTH_2 + C_WIDTH_2

A_IN = A_QLORA + A_KVLORA + A_ROPE
B_IN = 3 * B_WIDTH_2
D_IN = A_IN + B_IN + C_WIDTH_2

TOP_K_INNER = 2
D_EXPERT = 256


def rms_norm_2(x, g):
    xf = x.astype(jnp.float32)
    y = xf * lax.rsqrt(jnp.mean(xf * xf, axis=-1, keepdims=True) + EPS)
    return (y * g.astype(jnp.float32)).astype(x.dtype)

def rope_tables(seq):
    pos = jnp.arange(seq, dtype=jnp.float32)
    inv = ROPE_THETA ** (-jnp.arange(0, A_ROPE, 2, dtype=jnp.float32) / A_ROPE)
    ang = pos[:, None] * inv[None, :]
    return jnp.cos(ang), jnp.sin(ang)

def apply_rope(x, cos, sin):
    half = x.shape[-1] // 2
    x1 = x[..., :half].astype(jnp.float32)
    x2 = x[..., half:].astype(jnp.float32)
    out = jnp.concatenate([x1 * cos - x2 * sin, x2 * cos + x1 * sin], axis=-1)
    return out.astype(x.dtype)

def mla_mixer(c_q, c_kv, k_r, q_norm_g, w_uq, kv_norm_g, w_ukv):
    B, S, _ = c_q.shape
    cos, sin = rope_tables(S)
    q = jnp.einsum('bsr,rf->bsf', rms_norm_2(c_q, q_norm_g), w_uq).reshape(B, S, A_HEADS_2, A_NOPE + A_ROPE)
    q = jnp.concatenate([q[..., :A_NOPE], apply_rope(q[..., A_NOPE:], cos[None, :, None], sin[None, :, None])], axis=-1)
    kv = jnp.einsum('bsr,rf->bsf', rms_norm_2(c_kv, kv_norm_g), w_ukv).reshape(B, S, A_HEADS_2, A_NOPE + A_VDIM)
    k_rope = apply_rope(k_r, cos[None], sin[None])
    k = jnp.concatenate([kv[..., :A_NOPE], jnp.broadcast_to(k_rope[:, :, None, :], (B, S, A_HEADS_2, A_ROPE))], axis=-1)
    v = kv[..., A_NOPE:]
    scale = (A_NOPE + A_ROPE) ** -0.5
    chunk_id = jnp.arange(S) // CHUNK
    outs = []
    for i in range(S // Q_BLOCK):
        q0, q1 = i * Q_BLOCK, (i + 1) * Q_BLOCK
        s = jnp.einsum('bqhd,bkhd->bhqk', q[:, q0:q1], k[:, :q1]).astype(jnp.float32) * scale
        allowed = chunk_id[:q1][None, :] <= chunk_id[q0:q1][:, None]
        s = jnp.where(allowed, s, -1e30)
        p = jax.nn.softmax(s, axis=-1).astype(v.dtype)
        outs.append(jnp.einsum('bhqk,bkhd->bqhd', p, v[:, :q1]))
    return jnp.concatenate(outs, axis=1).reshape(B, S, A_WIDTH_2)

def stick_breaking_mixer(q, k, v):
    B, S = q.shape[0], q.shape[1]
    pos = jnp.arange(S)
    scale = B_DIM ** -0.5
    outs = []
    for i in range(S // Q_BLOCK):
        q0, q1 = i * Q_BLOCK, (i + 1) * Q_BLOCK
        z = jnp.einsum('bqhd,bkhd->bhqk', q[:, q0:q1], k[:, :q1]).astype(jnp.float32) * scale
        strict = pos[:q1][None, :] < pos[q0:q1][:, None]
        log_1m_beta = jnp.where(strict, -jax.nn.softplus(z), 0.0)
        between = lax.cumsum(log_1m_beta, axis=3, reverse=True) - log_1m_beta
        a = jnp.where(strict, jnp.exp(jax.nn.log_sigmoid(z) + between), 0.0).astype(v.dtype)
        outs.append(jnp.einsum('bhqk,bkhd->bqhd', a, v[:, :q1]))
    return jnp.concatenate(outs, axis=1).reshape(B, S, B_WIDTH_2)

def pool_mixer(u, pool_w, pool_scale):
    B, S, _ = u.shape
    uf = u.astype(jnp.float32)
    cs = jnp.concatenate([jnp.zeros((B, 1, C_WIDTH_2), jnp.float32), jnp.cumsum(uf, axis=1)], axis=1)
    pos = jnp.arange(S, dtype=jnp.float32)
    groups = []
    for g, w in enumerate(POOL_WINDOWS):
        c = cs[..., g * POOL_CH:(g + 1) * POOL_CH]
        lag = jnp.pad(c[:, :S - w + 1], ((0, 0), (w - 1, 0), (0, 0)))
        count = jnp.minimum(pos + 1.0, float(w))[None, :, None]
        mean = (c[:, 1:] - lag) / count
        groups.append(mean - uf[..., g * POOL_CH:(g + 1) * POOL_CH])
    d = jnp.stack(groups, axis=2).astype(u.dtype)
    y = jnp.einsum('bsgc,gcd->bsgd', d, pool_w).reshape(B, S, C_WIDTH_2)
    return y * pool_scale

def hier_moe_2(h, w_group, b_group, w_expert, b_expert, w_gate, w_up, w_down):
    B, S, D = h.shape
    t = h.reshape(B * S, D)
    g_prob = jax.nn.softmax((t @ w_group + b_group).astype(jnp.float32), axis=-1)
    p_sel, g_idx = lax.top_k(g_prob, 1)
    p_sel, g_idx = p_sel[:, 0], g_idx[:, 0]
    e_logits = (t @ w_expert + b_expert).astype(jnp.float32).reshape(B * S, N_GROUPS, EXPERTS_PER_GROUP)
    e_in = jnp.take_along_axis(e_logits, g_idx[:, None, None], axis=1)[:, 0]
    e_prob = jax.nn.softmax(e_in, axis=-1)
    w_k, i_k = lax.top_k(e_prob, TOP_K_INNER)
    w_k = w_k / jnp.sum(w_k, axis=-1, keepdims=True)
    inner = jnp.sum(jax.nn.one_hot(i_k, EXPERTS_PER_GROUP, dtype=jnp.float32) * w_k[..., None], axis=1)
    combine = (p_sel[:, None, None] * jax.nn.one_hot(g_idx, N_GROUPS, dtype=jnp.float32)[:, :, None]
               * inner[:, None, :]).astype(t.dtype)
    y = jnp.zeros_like(t)
    for g in range(N_GROUPS):
        a = jnp.einsum('nd,edf->nef', t, w_gate[g])
        b = jnp.einsum('nd,edf->nef', t, w_up[g])
        hid = jax.nn.silu(a) * b * combine[:, g, :, None]
        y = y + jnp.einsum('nef,efd->nd', hid, w_down[g])
    return y.reshape(B, S, D)

def hybrid_layer_2(x, norm1_g, w_in, q_norm_g, w_uq, kv_norm_g, w_ukv, pool_w, pool_scale, w_out,
                 norm2_g, w_group, b_group, w_expert, b_expert, w_gate, w_up, w_down):
    B, S, _ = x.shape
    hn = rms_norm_2(x, norm1_g)
    proj = jnp.einsum('bsd,df->bsf', hn, w_in)
    o1 = A_QLORA
    o2 = o1 + A_KVLORA
    o3 = o2 + A_ROPE
    o4 = o3 + B_IN
    ya = mla_mixer(proj[..., :o1], proj[..., o1:o2], proj[..., o2:o3], q_norm_g, w_uq, kv_norm_g, w_ukv)
    qkv_b = proj[..., o3:o4].reshape(B, S, 3, B_HEADS, B_DIM)
    yb = stick_breaking_mixer(qkv_b[:, :, 0], qkv_b[:, :, 1], qkv_b[:, :, 2])
    yc = pool_mixer(proj[..., o4:], pool_w, pool_scale)
    mixed = jnp.concatenate([ya, yb, yc], axis=-1)
    x = x + jnp.einsum('bsm,md->bsd', mixed, w_out)
    x = x + hier_moe_2(rms_norm_2(x, norm2_g), w_group, b_group, w_expert, b_expert, w_gate, w_up, w_down)
    return x

def second_inputs(seed: int = 0) -> dict:
    key = jax.random.key(seed)
    ks = jax.random.split(key, 20)
    L, D = DEPTH_2, D_MODEL

    def nrm(k, shape, fan_in):
        return jax.random.normal(k, shape, jnp.float32) * (fan_in ** -0.5)

    def gain(k, shape):
        return 1.0 + 0.02 * jax.random.normal(k, shape, jnp.float32)

    return {
        'x': jax.random.normal(ks[0], (BATCH, SEQ, D), jnp.float32),
        'norm1_g': gain(ks[1], (L, D)),
        'w_in': nrm(ks[2], (L, D, D_IN), D),
        'q_norm_g': gain(ks[3], (L, A_QLORA)),
        'w_uq': nrm(ks[4], (L, A_QLORA, A_HEADS_2 * (A_NOPE + A_ROPE)), A_QLORA),
        'kv_norm_g': gain(ks[5], (L, A_KVLORA)),
        'w_ukv': nrm(ks[6], (L, A_KVLORA, A_HEADS_2 * (A_NOPE + A_VDIM)), A_KVLORA),
        'pool_w': nrm(ks[7], (L, len(POOL_WINDOWS), POOL_CH, POOL_CH), POOL_CH),
        'pool_scale': gain(ks[8], (L, C_WIDTH_2)),
        'w_out': nrm(ks[9], (L, D_MIX, D), D_MIX),
        'norm2_g': gain(ks[10], (L, D)),
        'w_group': nrm(ks[11], (L, D, N_GROUPS), D),
        'b_group': 0.01 * jax.random.normal(ks[12], (L, N_GROUPS), jnp.float32),
        'w_expert': nrm(ks[13], (L, D, N_GROUPS * EXPERTS_PER_GROUP), D),
        'b_expert': 0.01 * jax.random.normal(ks[14], (L, N_GROUPS * EXPERTS_PER_GROUP), jnp.float32),
        'w_gate': nrm(ks[15], (L, N_GROUPS, EXPERTS_PER_GROUP, D, D_EXPERT), D),
        'w_up': nrm(ks[16], (L, N_GROUPS, EXPERTS_PER_GROUP, D, D_EXPERT), D),
        'w_down': nrm(ks[17], (L, N_GROUPS, EXPERTS_PER_GROUP, D_EXPERT, D), D_EXPERT),
        'final_g': gain(ks[18], (D,)),
    }

def second_block(x, norm1_g, w_in, q_norm_g, w_uq, kv_norm_g, w_ukv, pool_w, pool_scale, w_out,
              norm2_g, w_group, b_group, w_expert, b_expert, w_gate, w_up, w_down, final_g):
    for l in range(DEPTH_2):
        x = hybrid_layer_2(x, norm1_g[l], w_in[l], q_norm_g[l], w_uq[l], kv_norm_g[l], w_ukv[l],
                         pool_w[l], pool_scale[l], w_out[l], norm2_g[l], w_group[l], b_group[l],
                         w_expert[l], b_expert[l], w_gate[l], w_up[l], w_down[l])
    return rms_norm_2(x, final_g)


def setup_inputs(seed=0):
    out = dict(first_inputs(seed))
    for name, value in second_inputs(seed + 1).items():
        if name != "x":
            out[name + "_2"] = value
    return out


def reference(
    x, c, ctx, c_ctx, w_mod, b_mod, norm1_g, norm2_g, w_in, w_out, diff_lambda, diff_sub_g,
    gla_w_decay, gla_b_decay, gla_norm_g, na_rel_bias, w_router_group, b_router_group,
    w_router_expert, b_router_expert, w_expert_up, w_expert_down, final_g, norm1_g_2, w_in_2,
    q_norm_g_2, w_uq_2, kv_norm_g_2, w_ukv_2, pool_w_2, pool_scale_2, w_out_2, norm2_g_2,
    w_group_2, b_group_2, w_expert_2, b_expert_2, w_gate_2, w_up_2, w_down_2, final_g_2,
):
    x = first_block(
        x, c, ctx, c_ctx, w_mod, b_mod, norm1_g, norm2_g, w_in, w_out, diff_lambda, diff_sub_g,
        gla_w_decay, gla_b_decay, gla_norm_g, na_rel_bias, w_router_group, b_router_group,
        w_router_expert, b_router_expert, w_expert_up, w_expert_down, final_g,
    )
    return second_block(
        x, norm1_g_2, w_in_2, q_norm_g_2, w_uq_2, kv_norm_g_2, w_ukv_2, pool_w_2, pool_scale_2,
        w_out_2, norm2_g_2, w_group_2, b_group_2, w_expert_2, b_expert_2, w_gate_2, w_up_2,
        w_down_2, final_g_2,
    )


_drawn_inputs = setup_inputs


def setup_inputs(seed=0):
    import zlib

    import numpy as np

    out = dict(_drawn_inputs(seed))
    spreads = {}
    factors = {'diff_sub_g': 3.909,
     'gla_b_decay': 3.305,
     'gla_norm_g': 5.83,
     'na_rel_bias': 50.343,
     'b_router_group': 7.248,
     'b_router_expert': 3.128,
     'q_norm_g_2': 3.09,
     'kv_norm_g_2': 3.105,
     'b_group_2': 8.0,
     'b_expert_2': 2.843,
     'final_g_2': 21.352,
     'pool_scale_2': 3.116}
    for name, (base, spread) in spreads.items():
        noise = np.random.default_rng([zlib.crc32(name.encode()), seed]).standard_normal(out[name].shape)
        drawn = base * np.exp(spread * noise) if base else spread * noise
        out[name] = jnp.asarray(drawn.astype(out[name].dtype))
    for name, factor in factors.items():
        out[name] = (out[name] * factor).astype(out[name].dtype)
    return out
```

```python
from contextlib import ExitStack

import numpy as np
import concourse.bass as bass
from concourse import mybir

F32 = mybir.dt.float32
I32 = mybir.dt.int32
ALU = mybir.AluOpType
ACT = mybir.ActivationFunctionType
AX = mybir.AxisListType.X

P = 128
D = 1024
KD = D // P
S = 256
NT = S // P
SLOT = 6144
RING = 4
WIN = 32
NE = 32
NG = 4
EG = NE // NG
GRID = 64
BIG = 1e30
EPS = 1e-6
LAM_INIT = 0.2

CONST_COLS = {"ident": P, "ones": P, "tri": P, "ones64": P, "slot_id": P, "iota8": 8, "step": 8}
CONST1_COLS = {"rope_cos": 2 * 64, "rope_sin": 2 * 64, "nb_mask": GRID, "mask_fwd": 32, "mask_bwd": 32}
CONST2_COLS = {"rope_cos": 2 * 32, "rope_sin": 2 * 32, "chunk_mask": P, "strict_mask": P, "pool": 4 * 2 * S}


def offsets(cols):
    at, out = 0, {}
    for name, n in cols.items():
        out[name] = (at, n)
        at += n
    return out, at


def rope_table(n_tokens, dim, positions):
    inv = np.float32(10000.0) ** (-np.arange(16, dtype=np.float32) / np.float32(16))
    cos, sin = [], []
    for pos in positions:
        ang = pos.astype(np.float32)[:, None] * inv.astype(np.float32)
        cos += [np.cos(ang), np.cos(ang)]
        sin += [-np.sin(ang), np.sin(ang)]
    cos, sin = (np.concatenate(x, axis=1).astype(np.float32) for x in (cos, sin))
    tile = lambda t: t.reshape(n_tokens // P, P, dim).transpose(1, 0, 2).reshape(P, -1)
    return tile(cos), tile(sin)


def shape_constants():
    r = np.arange(P)
    t = np.arange(S)
    c = {
        "ident": np.eye(P),
        "ones": np.ones((P, P)),
        "tri": r[:, None] < r[None, :],
        "ones64": (r[:, None] // 64) == (r[None, :] // 64),
        "slot_id": np.broadcast_to(r % WIN, (P, P)),
        "iota8": np.broadcast_to(np.arange(8), (P, 8)),
        "step": np.broadcast_to(WIN * (np.arange(8) + 1), (P, 8)),
    }
    cos, sin = rope_table(S, 64, [t // GRID, t % GRID])
    q = r % GRID
    start = np.clip(q - 8, 0, GRID - 16)
    k = np.arange(GRID)
    inside = (k[None, :] >= start[:, None]) & (k[None, :] < start[:, None] + 16)
    s32, t32 = r[:, None] % 32, np.arange(32)[None, :]
    c1 = {
        "rope_cos": cos, "rope_sin": sin, "nb_mask": np.where(inside, 0.0, -BIG),
        "mask_fwd": t32 >= s32, "mask_bwd": s32 >= t32,
    }
    cos, sin = rope_table(S, 32, [t])
    pool = np.zeros((4, S, S))
    for g, w in enumerate((2, 4, 8, 16)):
        for tt in range(S):
            lo = max(0, tt - w + 1)
            pool[g, lo:tt + 1, tt] = np.float32(1.0) / np.float32(min(tt + 1, w))
            pool[g, tt, tt] -= 1.0
    pool = pool.reshape(4, 2, P, S).transpose(2, 0, 1, 3).reshape(P, -1)
    c2 = {
        "rope_cos": cos, "rope_sin": sin,
        "chunk_mask": np.where(r[None, :] // 64 <= r[:, None] // 64, 0.0, -BIG),
        "strict_mask": np.where(r[None, :] < r[:, None], 0.0, -BIG),
        "pool": pool,
    }
    pack = lambda d, cols: np.concatenate([np.asarray(d[n], np.float32).reshape(P, -1) for n in cols], axis=1)
    return {"const0": pack(c, CONST_COLS), "const1": pack(c1, CONST1_COLS), "const2": pack(c2, CONST2_COLS)}


QB, KB, VB, RB, GB, QN, KN, VN = 1536, 1664, 1792, 2048, 2304, 2336, 2592, 2848

def straight_pieces():
    mods = [("mod", j) for j in range(12)]
    wins = [("win", j) for j in range(6)]
    first = mods[:4] + wins[:1]
    for j in range(4):
        first += mods[4 + 2 * j:6 + 2 * j] + [wins[1 + j]]
    first += [wins[5], ("wout", 0), ("wout", 1)]
    second = [("win2", 0), ("win2", 1), ("mla", 0), ("wout2", 0), ("wout2", 1)]
    return first, second


def projection_units():
    u = [("T", 0, "qb", 0, "s"), ("T", 0, "kb", 0, "v"), ("T", 0, "gb", 0, "s"),
         ("T", 0, "rb", 0, "s"), ("T", 0, "rb", 1, "s")]
    u += [("K", 1, "vbn", t, "v") for t in range(4)]
    u += [("T", 2, "qn", 0, "s"), ("T", 2, "qn", 1, "v"), ("T", 2, "kn", 0, "s"), ("T", 2, "kn", 1, "v")]
    u += [("K", 3, "qa", 0, "v"), ("K", 3, "qa", 1, "v"), ("X", 3, "qa", 0, "s")]
    u += [("K", 4, "ka", 0, "v"), ("X", 3, "qa", 1, "s"), ("K", 4, "ka", 1, "v"), ("X", 4, "ka", 0, "s"),
          ("K", 4, "ka", 2, "v"), ("X", 4, "ka", 1, "s"), ("K", 4, "ka", 3, "v"), ("X", 4, "ka", 2, "s")]
    u += [("K", 5, "va", 0, "s"), ("X", 4, "ka", 3, "s")]
    u += [("K", 5, "va", t, "v" if t % 2 else "s") for t in range(1, 4)]
    return u


UNITS = projection_units()


def emptied(units, n, engine):
    return sum(1 for u in units[:n] if u[4] == engine)


SEMS = """params loaded_x loaded_ctx loaded_bias bias_out piece0 piece1 piece2 piece3 piece_used
vector_step scalar_step gpsimd_step silu_c c_T c_cols b_T b_cols mod_mm mod_row mod_t mod_col
sumsq mean sqrt_done xn x_T xT_v xT_s unit_mm unit_v unit_s rot_tile zero_done
gate_z z_bias z_exp z_ln decay gla_d gla_e gla_qk gla_at gla_b gla_c at_sb c_sb at_masked gla_o o_sb o_sq gla_ss gla_mean gla_sqrt gla_y
score score_b neg_max exps probs tr tr_sb pv pv_sb a_sq a_ss a_mean a_sqrt mixed
diag gate_bc gate_sb out_mm resid
n2_T n2_v n2_s logits lg lg_exp route rank_mm 
w_sel w_gath w_ct w_gsb w_csb w_gt w_xg w_up w_silu w_hid w_ht w_hsb w_y w_ysb w_comb w_half p2_mm p2_s p2_v st_mm pool_w head_s head_v final_gain moe_mm
fin_sq fin_mean fin_sqrt fin_x
cq_sb cq_sq cq_mean cq_sqrt cq_n cq_T cq_Ts q_mm q_sb kv_mm kv_sb head_T head_Ts
st_z st_zb st_exp st_ln st_x st_a st_T st_Ts st_pv st_o pool_d pool_ds pool_y pool_o
const2 params2 written scale lam lam_sums lam_exp router_w zero_tile ranked w_cur w_xm c_used x_T2""".split()


ROWS = {"c": 8, "c_ctx": 8, "b_mod": 48, "norm1_g": 8, "norm2_g": 8, "norm1_g_2": 16, "norm2_g_2": 16,
        "q_norm_g_2": 4, "kv_norm_g_2": 2, "pool_scale_2": 4, "diff_sub_g": 1, "gla_b_decay": 2, "gla_norm_g": 1}
PARAMS = 16 * (len(ROWS) + 2)
PARAMS2 = 16 * 6


def flat_rows(src):
    names = "abcd"[:len(src.shape)]
    flat = src if len(names) == 1 else src.rearrange(f"{' '.join(names)} -> ({' '.join(names)})")
    return flat.rearrange("(r n) -> r n", n=P)


class Tally:

    def __init__(self, sems):
        self.sems, self.n = sems, {name: 0 for name in sems}

    def __call__(self, name, k=1):
        self.n[name] += k
        return self.sems[name], self.n[name]

    def plus(self, name, k):
        return self.sems[name], self.n[name] + k


class Ring:

    def __init__(self, sems):
        self.sems, self.n, self.loads = sems, 0, [0] * RING

    def place(self, dmas):
        slot = self.n % RING
        self.n += 1
        self.loads[slot] += 16 * dmas
        return slot, self.sems[f"piece{slot}"], self.loads[slot]

    def loop(self, turns, per_turn, dmas):
        assert per_turn == RING
        out = []
        for j in range(per_turn):
            slot = (self.n + j) % RING
            out.append((slot, self.sems[f"piece{slot}"], self.loads[slot], 16 * dmas))
            self.loads[slot] += 16 * dmas * turns
        self.n += turns * per_turn
        return out


DMAS = {"mod": 1, "win": 1, "wout": 1, "win2": 1, "mla": 2, "wout2": 1}
E1_DMAS, E2_DMAS = 2, 3
WIN_COLS = [[(QB, 256), (RB, 256), (GB, 32)], [(VB, 256), (VN, 256)], [(QN, 512)], [(0, 512)], [(512, 512)],
            [(1024, 512)]]
WIN_WIDTH = [sum(n for _, n in cols) for cols in WIN_COLS]
WIN2_COLS = [[(0, 416), (1184, 256)], [(416, 768)]]
WIN2_WIDTH = [sum(n for _, n in cols) for cols in WIN2_COLS]


def dmas_of(piece):
    kind, j = piece
    if kind == "win":
        return len(WIN_COLS[j])
    if kind == "win2":
        return len(WIN2_COLS[j])
    return DMAS[kind]


def hybrid_kernel(nc, ins, out):
    first_pieces, second_pieces = straight_pieces()
    row_places, n_rows = offsets(ROWS)
    c0, n_c0 = offsets(CONST_COLS)
    c1, n_c1 = offsets(CONST1_COLS)
    c2, n_c2 = offsets(CONST2_COLS)

    with ExitStack() as ctx:
        def sb(name, cols, dt=F32, rows=P):
            return ctx.enter_context(nc.sbuf_tensor(name, [rows, cols], dt))[:, :]

        sems = {name: ctx.enter_context(nc.semaphore(name)) for name in SEMS}

        ring = sb("ring", RING * SLOT).rearrange("p (r n) -> p r n", r=RING)
        X = sb("X", NT * D).rearrange("p (t d) -> p t d", t=NT)
        xn = sb("xn", NT * D).rearrange("p (t d) -> p t d", t=NT)
        hTf = sb("hT", KD * 2 * S)
        hT = hTf.rearrange("p (k n) -> p k n", k=KD)
        h2T = hTf[:, 0:KD * S].rearrange("p (k n) -> p k n", k=KD)
        const0 = sb("const0_sb", n_c0)
        C0 = {n: const0[:, a:a + w] for n, (a, w) in c0.items()}
        ident, ones, tri = C0["ident"], C0["ones"], C0["tri"]
        small = sb("small", 400)
        modT = small[:, 0:96].rearrange("p (j i) -> p j i", i=2)
        scaleT = small[:, 96:120].rearrange("p (n k) -> p n k", k=KD)
        ss = small[:, 120:124]
        rstd = small[:, 124:128]
        rowsT = small[:, 128:256]
        PT = {n: rowsT[:, a:a + w] for n, (a, w) in row_places.items()}
        router_b = small[:, 256:292]
        cols = small[:, 292:400]
        psum = ctx.enter_context(nc.psum_tensor("psum", [P, 8, 512], F32))
        ps = [psum[:, b, :] for b in range(8)]
        bias_dram = ins["bias_scratch"]

        arena = sb("arena", 18944)
        at_col = [0]

        def area(n):
            at_col[0] += n
            return arena[:, at_col[0] - n:at_col[0]]

        cxf = area(2048)
        rotf = area(1536)
        cx = cxf.rearrange("p (t d) -> p t d", t=NT)
        rot_b, rot_o = rotf[:, 0:512], rotf[:, 512:1536].rearrange("p (b n) -> p b n", b=2)
        qk = arena[:, 0:3584].rearrange("p (d n) -> p d n", d=2)
        probs1 = cxf.rearrange("p (b m n) -> p b m n", b=2, m=2)
        qaT = area(1024).rearrange("p (h n) -> p h n", h=4)
        kaT = area(2048).rearrange("p (h n) -> p h n", h=4)
        va = area(2048).rearrange("p (t n) -> p t n", t=4)
        vbn = area(2048).rearrange("p (t n) -> p t n", t=4)
        qnT = area(512).rearrange("p (h n) -> p h n", h=2)
        knT = area(1024).rearrange("p (h n) -> p h n", h=2)
        qbT = area(256)
        kbT = area(512)
        rT = area(512).rearrange("p (h n) -> p h n", h=2)
        glow = area(512)
        nb_biasf = area(2048)
        nb_bias = nb_biasf.rearrange("p (t h n) -> p t h n", t=2, h=4)
        const1 = area(n_c1)
        C1 = {n: const1[:, a:a + w] for n, (a, w) in c1.items()}
        mixf = area(2048)
        mixT = mixf.rearrange("p (k n) -> p k n", k=KD)
        wdec = area(256)[0:32, :].rearrange("p (d n) -> p d n", d=2)
        rows = cxf[:, 0:P]
        cT = nb_biasf[:, 0:256].rearrange("p (k i) -> p k i", i=32)
        mod_row = nb_biasf[:, 256:512].rearrange("p (b n) -> p b n", b=2)
        lam_row = nb_biasf[:, 512:768].rearrange("p (n d) -> p n d", d=64)
        zg = xn[:, 0, :].rearrange("p (d n) -> p d n", d=2)
        ze = xn[:, 1, :].rearrange("p (d n) -> p d n", d=2)
        pre = mixf[:, 0:1024].rearrange("p (d s n) -> p d s n", d=2, s=2)
        dif = hTf[:, 0:1024].rearrange("p (l n) -> p l n", l=4)
        atT = hTf[:, 1024:3072].rearrange("p (h s n) -> p h s n", h=4, s=2)
        ctT = hTf[:, 3072:4096].rearrange("p (b s n) -> p b s n", b=2, s=2)
        gl_o = hTf[:, 0:512].rearrange("p (h n) -> p h n", h=2)
        gl_s = hTf[:, 512:1024].rearrange("p (h n) -> p h n", h=2)
        at_b = rotf[:, 0:256]
        prT = hTf.rearrange("p (b m k n) -> p b m k n", b=2, m=2, k=4)
        oA = xn[:, 0, :].rearrange("p (h n) -> p h n", h=4)
        oS = xn[:, 1, :].rearrange("p (h n) -> p h n", h=4)
        band_flat = arena[0:GRID, 3584:7168]
        band = band_flat.rearrange("p (r u) -> p r u", u=P)
        work = arena[:, 0:3584]
        sel_gate = work[:, 0:256].rearrange("p (t n) -> p t n", t=NT)
        sel = work[:, 256:320].rearrange("p (t n) -> p t n", t=NT)
        comb = work[:, 320:576]
        got = work[:, 576:832]
        gotT = work[:, 832:1088].rearrange("p (c n) -> p c n", c=2)
        silu_sb, hid, hidT = work[:, 1088:1216], work[:, 1216:1344], work[:, 1344:1472]
        y_sb = work[:, 1472:1728]
        cur = work[:, 1728:1732]
        junk = arena[:, 3584:4608]
        router_w = kaT.rearrange("p h n -> p (h n)")[:, 0:288].rearrange("p (k n) -> p k n", k=KD)
        rt = kaT.rearrange("p h n -> p (h n)")[:, 288:2048]
        ranks = rt[:, 0:128].rearrange("p (r e) -> p r e", e=NE)
        chosen = rt[:, 128:192].rearrange("p (t e) -> p t e", t=NT)
        lg = rt[:, 192:272].rearrange("p (t n) -> p t n", t=NT)
        r8 = rt[:, 272:272 + 16 * 12].rearrange("p (n t e) -> p n t e", t=NT, e=EG)
        r4 = rt[:, 480:480 + 8 * 6].rearrange("p (n t g) -> p n t g", t=NT, g=NG)
        r1 = rt[:, 544:544 + 2 * 16].rearrange("p (n t) -> p n t", t=NT)
        r32 = rt[:, 600:664].rearrange("p (t e) -> p t e", t=NT)
        extra_f = rt[0:1, 664:696]
        extra_cmp = rt[0:1, 704:960].rearrange("p (e j) -> p e j", j=8)
        extra = ctx.enter_context(nc.sbuf_tensor("extra", [1, NE], I32))
        zeros = rt[:, 960:1088]
        final_g = va.rearrange("p t n -> p (t n)")[:, 0:D]
        vbf = vbn.rearrange("p t n -> p (t n)")
        gate_diag = vbf[:, 0:D].rearrange("p (k n) -> p k n", k=KD)
        gate_sb = vbf[:, D:2 * D]
        res_tmp = vbf[:, 0:D]
        junk2 = arena[:, 2560:3584]
        def lie(start, n):
            return arena[:, start:start + n]

        const2 = lie(7680, n_c2)
        C2 = {n: const2[:, a:a + w] for n, (a, w) in c2.items()}
        low = 7680 + n_c2
        cq = lie(low, 832).rearrange("p (t n) -> p t n", t=NT)
        pool_u = lie(low + 832, 512).rearrange("p (t n) -> p t n", t=NT)
        bqT = lie(low + 1344, 512).rearrange("p (h n) -> p h n", h=2)
        bkT = lie(low + 1856, 512).rearrange("p (h n) -> p h n", h=2)
        bv = lie(low + 2368, 512).rearrange("p (t n) -> p t n", t=NT)
        pool_dT = lie(low + 2880, 512).rearrange("p (c n) -> p c n", c=2)
        pool_w = lie(low + 3392, 128).rearrange("p (c n) -> p c n", c=2)
        st_z = lie(low + 3520, 1536).rearrange("p (m n) -> p m n", m=2)
        rot2a = lie(low + 5056, 256).rearrange("p (h n) -> p h n", h=8)
        rot2b = lie(low + 5312, 256).rearrange("p (h n) -> p h n", h=8)
        key_rot = lie(low + 5568, 64).rearrange("p (t n) -> p t n", t=NT)
        st_e = work[:, 0:1536].rearrange("p (m n) -> p m n", m=2)
        st_s = work[:, 1536:3072].rearrange("p (m n) -> p m n", m=2)
        q_tok = work[:, 0:1536].rearrange("p (t h n) -> p t h n", t=NT, h=8)
        k_tok = work[:, 1536:3072].rearrange("p (t h n) -> p t h n", t=NT, h=8)
        v2 = lie(4608, 1024).rearrange("p (t h n) -> p t h n", t=NT, h=8)
        cqT = lie(5632, 768).rearrange("p (c n) -> p c n", c=3)
        q2T = hTf[:, 0:2048].rearrange("p (h n) -> p h n", h=8)
        k2T = hTf[:, 2048:4096].rearrange("p (h n) -> p h n", h=8)
        probs2 = lie(3584, 1024).rearrange("p (b m n) -> p b m n", b=2, m=2)
        xnf = xn.rearrange("p t d -> p (t d)")
        st_pT = xnf.rearrange("p (h c n) -> p h c n", h=4, c=2)
        prT2 = xnf.rearrange("p (b m c n) -> p b m c n", b=2, m=2, c=2)
        pool_mat = C2["pool"].rearrange("p (g s n) -> p g s n", g=4, s=NT)

        def pr_of(kind):
            return probs1 if kind != "mla" else probs2

        def prT_of(kind):
            return prT if kind != "mla" else prT2

        def mix_of(kind):
            return mixT

        def junk_of(t):
            return junk if t == 0 else junk2
        windows = {}

        def counter(eng, name):
            reg = ctx.enter_context(eng.register(name))
            eng.reg_mov(reg, 0)
            return reg

        block = ctx.enter_context(nc.Block())

        def w_cols(slot, width):
            return ring[:, slot, 0:KD * width].rearrange("p (k n) -> p k n", k=KD)

        def start_piece(sp, slot, sem, piece, layer):
            kind, j = piece
            if kind == "mod":
                src = ins["w_mod"][0].rearrange("(k p) n -> p k n", p=P)[:, :, 512 * j:512 * j + 512]
                sp.dma_start(w_cols(slot, 512), src).then_inc(sem, 16)
            elif kind in ("win", "win2"):
                cols_, width = (WIN_COLS, WIN_WIDTH) if kind == "win" else (WIN2_COLS, WIN2_WIDTH)
                w = ins["w_in"][0] if kind == "win" else ins["w_in_2"][layer]
                at = 0
                for col, n in cols_[j]:
                    sp.dma_start(w_cols(slot, width[j])[:, :, at:at + n],
                                 w.rearrange("(k p) n -> p k n", p=P)[:, :, col:col + n]).then_inc(sem, 16)
                    at += n
            elif kind in ("wout", "wout2"):
                w = ins["w_out"][0] if kind == "wout" else ins["w_out_2"][layer]
                sp.dma_start(ring[:, slot, 0:4 * D].rearrange("p (k n) -> p k n", k=4),
                             w[512 * j:512 * j + 512, :].rearrange("(k p) n -> p k n", p=P)).then_inc(sem, 16)
            elif kind == "mla":
                sp.dma_start(ring[:, slot, 0:1536].rearrange("p (k n) -> p k n", k=2),
                             ins["w_uq_2"][layer].rearrange("(k p) n -> p k n", p=P)).then_inc(sem, 16)
                sp.dma_start(ring[:, slot, 1536:2560], ins["w_ukv_2"][layer]).then_inc(sem, 16)

        def e1_up(slot):
            return ring[:, slot, 0:4 * D].rearrange("p (k n) -> p k n", k=4)

        def e1_down(slot):
            return ring[:, slot, 4 * D:6 * D].rearrange("p (k n) -> p k n", k=2)

        def e2_gate(slot):
            return ring[:, slot, 0:2048].rearrange("p (k n) -> p k n", k=KD)

        def e2_up(slot):
            return ring[:, slot, 2048:4096].rearrange("p (k n) -> p k n", k=KD)

        def e2_down(slot):
            return ring[:, slot, 4096:6144].rearrange("p (k n) -> p k n", k=2)

        up1 = ins["w_expert_up"][0].rearrange("e (h k p) n -> (e h) p k n", h=2, p=P)
        down1 = ins["w_expert_down"][0].rearrange("e (h k p) n -> (e h) p k n", h=2, p=P)


        def items_of(kind):
            return [(g, t) for g in range(2 if kind == "na" else 4) for t in range(NT)]

        def keys_of(kind, t):
            return P * (t + 1) if kind == "mla" else 4 * P

        def attention_pe(pe, at, kind):
            items = items_of(kind)

            def scores(i):
                g, t = items[i]
                if i >= 2:
                    pe.wait_ge(*at.plus("exps", i - 1))
                for m in range(2):
                    if kind == "mla":
                        q, k = q2T[0:96, 2 * g + m, P * t:P * t + P], k2T[0:96, 2 * g + m, 0:P * (t + 1)]
                    else:
                        q_all, k_all = (qnT, knT) if kind == "na" else (qaT, kaT)
                        q, k = q_all[64 * m:64 * m + 64, g, P * t:P * t + P], k_all[64 * m:64 * m + 64, g, :]
                    mm = pe.matmul(ps[2 * (i % 2) + m][:, 0:keys_of(kind, t)], q, k, start=True, stop=True)
                mm.then_inc(sems["score"], 1)

            def turns(i):
                g, t = items[i]
                pe.wait_ge(*at.plus("probs", i + 1))
                lag = 2 if kind == "diff" else 1
                if i >= lag:
                    pe.wait_ge(*at.plus("tr_sb", i + 1 - lag))
                for m in range(1 if kind == "diff" else 2):
                    bank = ps[4 + (i % 2 if kind == "diff" else m)]
                    for c in range(keys_of(kind, t) // P):
                        mm = pe.transpose(bank[:, P * c:P * c + P], pr_of(kind)[:, i % 2, m, P * c:P * c + P], ident)
                mm.then_inc(sems["tr"], 1)

            def values(i):
                g, _ = items[i]
                pe.wait_ge(*at.plus("tr_sb", i + 1))
                if g >= 2:
                    pe.wait_ge(*at.plus("pv_sb", g - 1))
                bank = ps[6 + g % 2]
                for m in range(1 if kind == "diff" else 2):
                    for c in range(2 if kind == "mla" else 4):
                        if kind == "diff":
                            dst, v = bank[:, 0:S], va[:, c, P * g:P * g + P]
                        elif kind == "na":
                            dst, v = bank[64 * m:64 * m + 64, 0:S], vbn[:, c, S + 64 * (2 * g + m):S + 64 * (2 * g + m) + 64]
                        else:
                            dst, v = bank[64 * m:64 * m + 64, P * c:S], v2[:, c, 2 * g + m, :]
                        rhs = prT_of(kind)[:, g % 2, m, c, :]
                        if kind == "mla":
                            rhs = rhs[:, P * c:S]
                        mm = pe.matmul(dst, v, rhs, start=(c == 0), stop=(c == (1 if kind == "mla" else 3)))
                mm.then_inc(sems["pv"], 1)

            scores(0)
            for i in range(len(items)):
                if i + 1 < len(items):
                    scores(i + 1)
                turns(i)
                if items[i][1] == NT - 1:
                    values(i)
            for name, n in (("exps", len(items)), ("probs", len(items)), ("tr_sb", len(items)), ("pv_sb", len(items) // 2)):
                pe.wait_ge(*at(name, n))

        def attention_act(act, at, kind):
            items = items_of(kind)
            scale = {"na": 1.0, "diff": 0.125, "mla": 96.0 ** -0.5}[kind]

            def exps(i):
                g, t = items[i]
                act.wait_ge(*at.plus("neg_max", i + 1))
                if i >= 2:
                    act.wait_ge(*at.plus("tr", i - 1))
                n = keys_of(kind, t)
                for m in range(2):
                    a = 16 + 2 * (i % 2) + m
                    ins_ = act.activation(pr_of(kind)[:, i % 2, m, 0:n], ps[2 * (i % 2) + m][:, 0:n], ACT.Exp,
                                          bias=cols[:, a:a + 1], scale=scale, accum_out=cols[:, a + 4:a + 5])
                ins_.then_inc(sems["exps"], 1)

            def copies(i):
                g, t = items[i]
                act.wait_ge(*at.plus("tr", i + 1))
                if g >= 2 and t == 0:
                    act.wait_ge(*at.plus("pv", g - 1))
                c = keys_of(kind, t) // P
                for m in range(1 if kind == "diff" else 2):
                    bank = ps[4 + (i % 2 if kind == "diff" else m)]
                    ins_ = act.activation(prT_of(kind)[:, g % 2, m, 0:c, P * t:P * t + P],
                                          bank[:, 0:P * c].rearrange("p (c n) -> p c n", c=c), ACT.Copy)
                ins_.then_inc(sems["tr_sb"], 1)

            exps(0)
            for i in range(len(items)):
                if i + 1 < len(items):
                    exps(i + 1)
                copies(i)
            at("neg_max", len(items)), at("tr", len(items)), at("pv", len(items) // 2)

        def attention_dve(dve, at, link, kind):
            items = items_of(kind)
            scale = {"na": 1.0, "diff": 0.125, "mla": 96.0 ** -0.5}[kind]

            def maxima(i):
                g, t = items[i]
                dve.wait_ge(*at.plus("score", i + 1))
                b, n = 2 * (i % 2), keys_of(kind, t)
                if kind == "na":
                    link(dve.tensor_tensor(psum[:, b:b + 2, 0:S], psum[:, b:b + 2, 0:S],
                                           nb_bias[:, t, 2 * g:2 * g + 2, :], ALU.add))
                if kind == "mla":
                    link(dve.tensor_tensor(psum[:, b:b + 2, n - P:n], psum[:, b:b + 2, n - P:n],
                                           C2["chunk_mask"].unsqueeze(1).broadcast_to([P, 2, P]), ALU.add))
                a = 16 + b
                link(dve.tensor_reduce(cols[:, a:a + 2], psum[:, b:b + 2, 0:n], AX, ALU.max))
                dve.tensor_scalar(cols[:, a:a + 2], cols[:, a:a + 2], -scale, None, ALU.mult).then_inc(sems["neg_max"], 1)

            def normalise(i):
                dve.wait_ge(*at.plus("exps", i + 1))
                a = 20 + 2 * (i % 2)
                n = keys_of(kind, items[i][1])
                pr = pr_of(kind)[:, i % 2, :, :]
                link(dve.reciprocal(cols[:, a:a + 2], cols[:, a:a + 2]))
                if kind == "diff":
                    link(dve.tensor_scalar(cols[:, a + 1:a + 2], cols[:, a + 1:a + 2], cols[:, 10:11], None, ALU.mult))
                    link(dve.tensor_scalar(pr[:, 0, :], pr[:, 0, :], cols[:, a:a + 1], None, ALU.mult))
                    ins_ = dve.scalar_tensor_tensor(pr[:, 0, :], pr[:, 1, :], cols[:, a + 1:a + 2], pr[:, 0, :],
                                                    ALU.mult, ALU.add)
                else:
                    for m in range(2):
                        ins_ = dve.tensor_scalar(pr[:, m, 0:n], pr[:, m, 0:n], cols[:, a + m:a + m + 1], None, ALU.mult)
                ins_.then_inc(sems["probs"], 1)

            def outputs(g):
                dve.wait_ge(*at.plus("pv", g + 1))
                dst = oA[:, g, :] if kind == "diff" else mix_of(kind)[:, (6 if kind == "na" else 0) + g, :]
                dve.tensor_copy(dst, ps[6 + g % 2][:, 0:S]).then_inc(sems["pv_sb"], 1)

            maxima(0)
            for i in range(len(items)):
                if i + 1 < len(items):
                    maxima(i + 1)
                normalise(i)
                if items[i][1] == NT - 1 and items[i][0] >= 1:
                    outputs(items[i][0] - 1)
            outputs(items[-1][0])
            at("score", len(items)), at("exps", len(items)), at("pv", len(items) // 2)

        def out_projection_pe(pe, at, piece_ready, kind, mix):
            for j in range(2):
                slot = piece_ready((kind, j))
                w = ring[:, slot, 0:4 * D].rearrange("p (k n) -> p k n", k=4)
                for t in range(NT):
                    for n in range(2):
                        for k in range(4):
                            mm = pe.matmul(ps[2 * t + n], mix[:, 4 * j + k, P * t:P * t + P],
                                           w[:, k, 512 * n:512 * n + 512], start=(j == 0 and k == 0),
                                           stop=(j == 1 and k == 3))
                mm.then_inc(sems["out_mm"], 1)
                pe.wait_ge(*at("out_mm"))
                pe.sem_inc(sems["piece_used"], 1)

        def gate_diagonals_dve(dve, at, part):
            for k in range(KD):
                ins_ = dve.tensor_scalar(gate_diag[:, k, :], ident, modT[:, KD * part + k, 0:1], None, ALU.mult)
            ins_.then_inc(sems["diag"], 1)

        def gate_broadcast_pe(pe, at, bank):
            pe.wait_ge(*at("diag"))
            for n in range(2):
                mm = pe.matmul(ps[bank + n], ones, gate_diag[:, 4 * n:4 * n + 4, :].rearrange("p k n -> p (k n)"),
                               start=True, stop=True)
            mm.then_inc(sems["gate_bc"], 1)

        def residual_dve(dve, at, link, bank, gate_bank=None):
            if gate_bank is not None:
                dve.wait_ge(*at("gate_bc"))
                link(dve.tensor_copy(gate_sb, psum[:, gate_bank:gate_bank + 2, :].rearrange("p b n -> p (b n)")))
            for t in range(NT):
                src = psum[:, bank + 2 * t:bank + 2 * t + 2, :].rearrange("p b n -> p (b n)")
                if gate_bank is not None:
                    link(dve.tensor_tensor(res_tmp, src, gate_sb, ALU.mult))
                    src = res_tmp
                ins_ = dve.tensor_tensor(X[:, t, :], X[:, t, :], src, ALU.add)
                link(ins_)
            dve.sem_inc(sems["resid"], 1)

        def squares_act(act, at):
            act.wait_ge(*at("resid"))
            for t in range(NT):
                ins_ = act.activation(junk_of(t), X[:, t, :], ACT.Square, accum_out=ss[:, t:t + 1])
            ins_.then_inc(sems["sumsq"], 1)
            act.wait_ge(*at("sumsq"))
            act.wait_ge(*at("mean"))
            act.activation(rstd[:, 0:NT], ss[:, 0:NT], ACT.Sqrt).then_inc(sems["sqrt_done"], 1)

        def rstd_dve(dve, at, link):
            dve.wait_ge(*at("sumsq"))
            link(dve.tensor_scalar(ss[:, 0:NT], ss[:, 0:NT], 1.0 / D, EPS, ALU.mult, ALU.add))
            dve.reciprocal(ss[:, 0:NT], ss[:, 0:NT]).then_inc(sems["mean"], 1)
            dve.wait_ge(*at("sqrt_done"))

        def norm_dve(dve, at, link, scale, shift):
            rstd_dve(dve, at, link)
            for t in range(NT):
                dve.tensor_scalar(xn[:, t, :], X[:, t, :], rstd[:, t:t + 1], None, ALU.mult).then_inc(sems["xn"], 1)
            for b in range(2):
                dve.wait_ge(*at.plus("x_T", b + 1))
                for k in (2 * b, 2 * b + 1):
                    src = ps[4 + b][:, S * (k % 2):S * (k % 2) + S]
                    if shift is None:
                        ins_ = dve.tensor_scalar(h2T[:, k, :], src, scale[:, k:k + 1], None, ALU.mult)
                    else:
                        ins_ = dve.tensor_scalar(h2T[:, k, :], src, scale[:, k:k + 1], shift[:, k, 0:1], ALU.mult, ALU.add)
                ins_.then_inc(sems["xT_v"], 1)
            at("x_T", 4)

        def norm_act(act, at, scale, shift):
            squares_act(act, at)
            for b in range(2, 4):
                act.wait_ge(*at.plus("x_T", b + 1))
                for k in (2 * b, 2 * b + 1):
                    src = ps[4 + b][:, S * (k % 2):S * (k % 2) + S]
                    ins_ = act.activation(h2T[:, k, :], src, ACT.Identity, scale=scale[:, k:k + 1],
                                          bias=0.0 if shift is None else shift[:, k, 0:1])
                ins_.then_inc(sems["xT_s"], 1)
            at("x_T", 4)

        def norm_pe(pe, at):
            pe.wait_ge(*at("xn", 2))
            for b in range(4):
                for k in (2 * b, 2 * b + 1):
                    for t in range(NT):
                        o = S * (k % 2) + P * t
                        mm = pe.transpose(ps[4 + b][:, o:o + P], xn[:, t, P * k:P * k + P], ident)
                mm.then_inc(sems["x_T"], 1)
            pe.wait_ge(*at("xT_v", 2))
            pe.wait_ge(*at("xT_s", 2))

        def final_dve(dve, at, link):
            rstd_dve(dve, at, link)
            for t in range(NT):
                ins_ = dve.scalar_tensor_tensor(X[:, t, :], X[:, t, :], rstd[:, t:t + 1], final_g, ALU.mult, ALU.mult)
            link(ins_)
            dve.sem_inc(sems["resid"], 1)
            dve.sem_inc(sems["fin_x"], 1)

        def route_pe(pe, at, which):
            pe.wait_ge(*at("router_w", 48 if which == 1 else 64))
            for t in range(NT):
                for k in range(KD):
                    mm = pe.matmul(ps[0][:, 64 * t:64 * t + NG + NE], h2T[:, k, P * t:P * t + P], router_w[:, k, :],
                                   start=(k == 0), stop=(k == KD - 1))
            mm.then_inc(sems["logits"], 1)
            pe.wait_ge(*at("zero_tile"))
            for b in range(4, 8):
                pe.matmul(ps[b], zeros, xn[:, 0, 0:512], start=True, stop=True)
            pe.wait_ge(*at("route"))
            r = ps[1][:, 0:3 * NE].rearrange("p (n e) -> p n e", e=NE)
            pe.matmul(r[:, 0, :], tri, chosen[:, 0, :], start=True, stop=True)
            pe.matmul(r[:, 1, :], tri, chosen[:, 1, :], start=True, stop=False)
            pe.matmul(r[:, 1, :], ones, chosen[:, 0, :], start=False, stop=True)
            for t in range(NT):
                mm = pe.matmul(r[:, 2, :], ones, chosen[:, t, :], start=(t == 0), stop=(t == 1))
            mm.then_inc(sems["rank_mm"], 1)

        def route_act(act, at):
            act.wait_ge(*at("lg"))
            act.activation(r4[:, 1, :, :], r4[:, 1, :, :], ACT.Exp).then_inc(sems["lg_exp"], 1)
            act.wait_ge(*at("lg"))
            act.activation(r1[:, 6, :], r1[:, 6, :], ACT.Exp).then_inc(sems["lg_exp"], 1)

        def route_dve(dve, at, link):
            spread = lambda x, n: x.unsqueeze(2).broadcast_to([P, NT, n])

            def first_of(x, n, top, mark, where):
                link(dve.tensor_reduce(top, x, AX, ALU.max))
                link(dve.tensor_tensor(where, x, spread(top, n), ALU.is_equal))
                link(dve.scalar_tensor_tensor(where, where, -16.0, iota_of(n), ALU.mult, ALU.add))
                link(dve.tensor_reduce(mark, where, AX, ALU.min))
                link(dve.tensor_tensor(where, where, spread(mark, n), ALU.is_equal))

            def iota_of(n):
                return C0["iota8"][:, 0:n].unsqueeze(1).broadcast_to([P, NT, n])

            dve.wait_ge(*at("logits"))
            src = ps[0][:, 0:128].rearrange("p (t n) -> p t n", t=NT)[:, :, 0:NG + NE]
            link(dve.tensor_tensor(lg[:, :, 0:NG + NE], src, router_b.unsqueeze(1).broadcast_to([P, NT, NG + NE]), ALU.add))
            groups = lg[:, :, 0:NG]
            first_of(groups, NG, r1[:, 0, :], r1[:, 1, :], r4[:, 0, :, :])
            dve.tensor_tensor(r4[:, 1, :, :], groups, spread(r1[:, 0, :], NG), ALU.subtract).then_inc(sems["lg"], 1)
            for t in range(NT):
                e3 = lg[:, t, NG:NG + NE].rearrange("p (g e) -> p g e", g=NG)
                dve.tensor_tensor(r32[:, t, :].rearrange("p (g e) -> p g e", g=NG), e3,
                                  r4[:, 0, t, :].unsqueeze(2).broadcast_to([P, NG, EG]), ALU.mult)
            dve.wait_ge(*at("lg"))
            dve.wait_ge(*at("lg_exp"))
            link(dve.tensor_reduce(r1[:, 2, :], r4[:, 1, :, :], AX, ALU.add))
            link(dve.reciprocal(r1[:, 2, :], r1[:, 2, :]))
            for t in range(NT):
                ins_ = dve.tensor_reduce(r8[:, 0, t, :], r32[:, t, :].rearrange("p (g e) -> p e g", g=NG), AX, ALU.add)
            link(ins_)
            first_of(r8[:, 0, :, :], EG, r1[:, 3, :], r1[:, 4, :], r8[:, 1, :, :])
            link(dve.scalar_tensor_tensor(r8[:, 2, :, :], r8[:, 1, :, :], -BIG, r8[:, 0, :, :], ALU.mult, ALU.add))
            first_of(r8[:, 2, :, :], EG, r1[:, 5, :], r1[:, 4, :], r8[:, 3, :, :])
            dve.tensor_tensor(r1[:, 6, :], r1[:, 5, :], r1[:, 3, :], ALU.subtract).then_inc(sems["lg"], 1)
            dve.wait_ge(*at("lg"))
            dve.wait_ge(*at("lg_exp"))
            link(dve.tensor_scalar(r1[:, 7, :], r1[:, 6, :], 1.0, None, ALU.add))
            link(dve.reciprocal(r1[:, 7, :], r1[:, 7, :]))
            link(dve.tensor_tensor(r1[:, 7, :], r1[:, 7, :], r1[:, 2, :], ALU.mult))
            link(dve.tensor_tensor(r1[:, 8, :], r1[:, 7, :], r1[:, 6, :], ALU.mult))
            link(dve.tensor_tensor(r8[:, 4, :, :], r8[:, 1, :, :], r8[:, 3, :, :], ALU.add))
            link(dve.tensor_tensor(r8[:, 5, :, :], r8[:, 1, :, :], spread(r1[:, 7, :], EG), ALU.mult))
            link(dve.tensor_tensor(r8[:, 6, :, :], r8[:, 3, :, :], spread(r1[:, 8, :], EG), ALU.mult))
            link(dve.tensor_tensor(r8[:, 5, :, :], r8[:, 5, :, :], r8[:, 6, :, :], ALU.add))
            for t in range(NT):
                g3 = r4[:, 0, t, :].unsqueeze(2).broadcast_to([P, NG, EG])
                for dst, src in ((chosen[:, t, :], r8[:, 4, t, :]), (ranks[:, NT + t, :], r8[:, 5, t, :])):
                    ins_ = dve.tensor_tensor(dst.rearrange("p (g e) -> p g e", g=NG), g3,
                                             src.unsqueeze(1).broadcast_to([P, NG, EG]), ALU.mult)
            ins_.then_inc(sems["route"], 1)
            dve.wait_ge(*at("route"))
            dve.wait_ge(*at("rank_mm"))
            r = ps[1][:, 0:3 * NE].rearrange("p (n e) -> p n e", e=NE)
            link(dve.scalar_tensor_tensor(ranks[:, 0:NT, :], r[:, 0:NT, :], 1.0, chosen, ALU.add, ALU.mult))
            link(dve.tensor_scalar(ranks[:, 0:NT, :], ranks[:, 0:NT, :], -1.0, None, ALU.add))
            link(dve.tensor_copy(extra_f, r[0:1, 2, :]))
            link(dve.tensor_tensor(extra_cmp, extra_f.unsqueeze(2).broadcast_to([1, NE, 8]),
                                   C0["step"][0:1, :].unsqueeze(1).broadcast_to([1, NE, 8]), ALU.is_gt))
            link(dve.tensor_reduce(extra_f, extra_cmp, AX, ALU.add))
            link(dve.tensor_copy(extra[:, :], extra_f))
            dve.sem_inc(sems["ranked"], 1)

        def each_expert(eng, at, which, window, before=None):
            pieces = 2 if which == 1 else 1
            per_turn = RING // pieces
            eng.wait_ge(*at("ranked"))
            with eng.Fori(0, NE // per_turn) as turn:
                for j in range(per_turn):
                    e = turn * per_turn + j
                    if before:
                        before(turn, j, e)
                    n = eng.value_load(extra[0:1, bass.ds(e, 1)], min_val=0, max_val=7)
                    with eng.If(n > 0):
                        with eng.Fori(0, n):
                            window(j, e, False)
                    window(j, e, True)

        def experts_pe(pe, at, plan, which):
            route_pe(pe, at, which)
            win = windows["pe"]
            pieces = 2 if which == 1 else 1
            slots = plan.loop(2 * NE // RING if which == 1 else NE // RING, RING, E1_DMAS if which == 1 else E2_DMAS)

            def weights_ready(turn, j, e):
                for _, sem, base, step in slots[pieces * j:pieces * j + pieces]:
                    pe.wait_ge(sem, turn * step + (base + step))

            def window(j, e, last):
                mine = [s[0] for s in slots[pieces * j:pieces * j + pieces]]
                pe.reg_add(win, win, 1)
                v = pe.snap(win)
                pe.wait_ge(sems["w_sel"], v)
                for t in range(NT):
                    for g in range(4):
                        mm = pe.matmul(ps[0][32 * g:32 * g + 32, 0:S], sel[:, t, :], xn[:, t, S * g:S * g + S],
                                       start=(t == 0), stop=(t == NT - 1))
                mm.then_inc(sems["w_gath"], 1)
                for t in range(NT):
                    mm = pe.transpose(ps[1][:, P * t:P * t + P], sel_gate[:, t, :], ident)
                mm.then_inc(sems["w_ct"], 1)
                pe.wait_ge(sems["w_gsb"], v)
                for c in range(2):
                    mm = pe.transpose(ps[2][:, P * c:P * c + P], got[:, P * c:P * c + P], ident)
                mm.then_inc(sems["w_gt"], 1)
                pe.wait_ge(sems["w_xg"], v)
                w = P if which == 1 else 64
                for k in range(KD):
                    for g in range(4):
                        if which == 1:
                            rhs = e1_up(mine[k // 4])[:, k % 4, :].rearrange("p (u n) -> p u n", u=2)[:, :, P * g:P * g + P]
                        else:
                            rhs = ring[:, mine[0], 0:4096].rearrange("p (u k n) -> p u k n", u=2, k=KD)[:, :, k, 64 * g:64 * g + 64]
                        mm = pe.matmul(ps[3][32 * g:32 * g + 32, 0:2 * w].rearrange("p (u n) -> p u n", u=2),
                                       gotT[:, k % 2, 32 * (k // 2):32 * (k // 2) + 32], rhs,
                                       start=(k == 0), stop=(k == KD - 1))
                mm.then_inc(sems["w_up"], 1)
                pe.wait_ge(sems["w_hid"], v)
                pe.transpose(ps[0][:, 0:P], hid, ident).then_inc(sems["w_ht"], 1)
                pe.wait_ge(sems["w_hsb"], v)
                chunks = 4 if which == 1 else 2
                for k in range(chunks):
                    for g in range(4):
                        wd = e1_down(mine[k // 2])[:, k % 2, :] if which == 1 else e2_down(mine[0])[:, k, :]
                        mm = pe.matmul(ps[1][32 * g:32 * g + 32, 0:S], hidT[:, 32 * k:32 * k + 32],
                                       wd[:, S * g:S * g + S], start=(k == 0), stop=(k == chunks - 1))
                mm.then_inc(sems["w_y"], 1)
                if last:
                    pe.wait_ge(sems["w_y"], v)
                    pe.sem_inc(sems["piece_used"], pieces)
                pe.wait_ge(sems["w_ysb"], v)
                for half in range(2):
                    if half:
                        pe.wait_ge(sems["w_half"], v)
                    for g in range(4):
                        t = (g + half) % 2
                        mm = pe.matmul(ps[4 + 2 * t + g // 2][:, S * (g % 2):S * (g % 2) + S],
                                       comb[32 * g:32 * g + 32, P * t:P * t + P], y_sb[32 * g:32 * g + 32, :],
                                       start=False, stop=True, skip_group_check=True)
                    mm.then_inc(sems["w_comb" if half else "w_half"], 1)

            each_expert(pe, at, which, window, weights_ready)
            pe.wait_ge(sems["w_comb"], pe.snap(win))
            pe.sem_inc(sems["moe_mm"], 1)

        def experts_act(act, at, which):
            route_act(act, at)
            win = windows["act"]

            def window(j, e, last):
                act.reg_add(win, win, 1)
                v = act.snap(win)
                act.wait_ge(sems["w_gath"], v)
                act.activation(got, ps[0][:, 0:S], ACT.Copy).then_inc(sems["w_gsb"], 1)
                act.wait_ge(sems["w_up"], v)
                w = P if which == 1 else 64
                act.activation(silu_sb[:, 0:w], ps[3][:, 0:w], ACT.Silu).then_inc(sems["w_silu"], 1)
                act.wait_ge(sems["w_ht"], v)
                if which == 1:
                    act.activation(hidT, ps[0][:, 0:P], ACT.Copy).then_inc(sems["w_hsb"], 1)
                else:
                    for half in range(2):
                        r = slice(64 * half, 64 * half + 64)
                        ins_ = act.activation(hidT[r, 0:64].rearrange("p (c s) -> p c s", c=2),
                                              ps[0][r, 0:P].rearrange("p (c u s) -> p c u s", c=2, u=2)[:, :, half, :],
                                              ACT.Copy)
                    ins_.then_inc(sems["w_hsb"], 1)

            each_expert(act, at, which, window)

        def experts_dve(dve, at, link, which, scale, shift):
            win = windows["dve"]
            scale4 = scale.rearrange("p (j c) -> p c j", c=2).unsqueeze(3).broadcast_to([P, 2, 4, 32])
            if shift is not None:
                shift4 = shift[:, :, 0].rearrange("p (j c) -> p c j", c=2).unsqueeze(3).broadcast_to([P, 2, 4, 32])

            def window(j, e, last):
                dve.reg_add(win, win, 1)
                v = dve.snap(win)
                if last:
                    dve.tensor_copy(cur.unsqueeze(2), ranks[:, :, bass.ds(e, 1)]).then_inc(sems["w_cur"], 1)
                else:
                    dve.tensor_scalar(cur[:, 0:NT], cur[:, 0:NT], -float(WIN), None, ALU.add).then_inc(sems["w_cur"], 1)
                dve.reg_add(currents, currents, 1)
                dve.wait_ge(sems["w_cur"], dve.snap(currents))
                for t in range(NT):
                    dve.tensor_scalar(sel_gate[:, t, :], C0["slot_id"], cur[:, t:t + 1], cur[:, NT + t:NT + t + 1],
                                      ALU.is_equal, ALU.mult)
                    ins_ = dve.tensor_scalar(sel[:, t, :], C0["slot_id"][:, 0:WIN], cur[:, t:t + 1], None, ALU.is_equal)
                ins_.then_inc(sems["w_sel"], 1)
                dve.wait_ge(sems["w_ct"], v)
                dve.tensor_copy(comb, ps[1][:, 0:S]).then_inc(sems["w_csb"], 1)
                dve.wait_ge(sems["w_gt"], v)
                src = ps[2][:, 0:S].rearrange("p (c j s) -> p c j s", c=2, j=4)
                dst = gotT.rearrange("p c (j s) -> p c j s", j=4)
                if shift is None:
                    dve.tensor_tensor(dst, src, scale4, ALU.mult).then_inc(sems["w_xg"], 1)
                else:
                    dve.tensor_tensor(dst, src, scale4, ALU.mult).then_inc(sems["w_xm"], 1)
                    dve.wait_ge(sems["w_xm"], v)
                    dve.tensor_tensor(dst, dst, shift4, ALU.add).then_inc(sems["w_xg"], 1)
                dve.wait_ge(sems["w_silu"], v)
                w = P if which == 1 else 64
                twice = lambda x: x.unsqueeze(1).broadcast_to([P, P // w, w])
                dve.tensor_tensor(hid.rearrange("p (r n) -> p r n", n=w), twice(silu_sb[:, 0:w]),
                                  twice(ps[3][:, w:2 * w]), ALU.mult).then_inc(sems["w_hid"], 1)
                dve.wait_ge(sems["w_y"], v)
                dve.tensor_copy(y_sb, ps[1][:, 0:S]).then_inc(sems["w_ysb"], 1)

            def begin(turn, j, e):
                dve.tensor_copy(cur.unsqueeze(2), ranks[:, :, bass.ds(e, 1)]).then_inc(sems["w_cur"], 1)
                dve.reg_add(currents, currents, 1)
                dve.wait_ge(sems["w_cur"], dve.snap(currents))

            currents = windows["cur"]
            each_expert(dve, at, which, window, begin)
            dve.wait_ge(*at("moe_mm"))


        def emptied_before(at_engine, unit):
            if unit >= 4:
                who = UNITS[unit - 4][4]
                at_engine.wait_ge(sems["unit_" + who], emptied(UNITS, unit - 3, who))

        score_items = [(h, t) for h in range(4) for t in range(NT)]
        pair_items = [(h, t) for h in range(2) for t in range(NT)]

        def context_values(pe, at, h):
            pe.wait_ge(*at("c_sb"))
            o = ps[7][64 * (h % 2):64 * (h % 2) + 64, S * (h // 2):S * (h // 2) + S]
            for s in range(2):
                mm = pe.matmul(o, vbn[:, NT + s, 64 * h:64 * h + 64], ctT[:, h % 2, s, :],
                               start=(s == 0 and h < 2), stop=False, skip_group_check=True)
            mm.then_inc(sems["c_used"], 1)

        def diagonal(rows_, h, off):
            base = atT[rows_, h, :, :]
            return bass.AP(tensor=base.tensor, offset=base.offset + off, ap=[base.ap[0], (S + P, 2), (1, 32)])

        def second_block_loads(sp, plan, straight):
            for layer in range(2):
                straight(second_pieces, layer)
                base, turns = plan.n, NE // RING
                slots = plan.loop(turns, RING, E2_DMAS)
                gate, up, down = (ins[n][layer].rearrange("g e (k p) n -> (g e) p k n", p=P)
                                  for n in ("w_gate_2", "w_up_2", "w_down_2"))
                with sp.Fori(0, turns) as turn:
                    for j, (slot, sem, _, _) in enumerate(slots):
                        sp.wait_ge(sems["piece_used"], turn * RING + (base + j - RING + 1))
                        e = turn * RING + j
                        sp.dma_start(e2_gate(slot), gate[bass.ds(e, 1)][0]).then_inc(sem, 16)
                        sp.dma_start(e2_up(slot), up[bass.ds(e, 1)][0]).then_inc(sem, 16)
                        sp.dma_start(e2_down(slot), down[bass.ds(e, 1)][0]).then_inc(sem, 16)

        def second_block_pool(pool, at):
            pool.wait_ge(*at("fin_x"))
            pool.dma_start(const2, ins["const2"]).then_inc(sems["const2"], 16)
            for layer in range(2):
                for m in range(2):
                    pool.dma_start(pool_w[64 * m:64 * m + 64, :, :], ins["pool_w_2"][layer]
                                   .rearrange("(c m) k n -> m k c n", m=2)[m]).then_inc(sems["pool_w"], 16)
                pool.wait_ge(*at("mixed"))
                for name, dst in (("w_group_2", router_w[:, :, 0:NG]), ("w_expert_2", router_w[:, :, NG:])):
                    pool.dma_start(dst, ins[name][layer].rearrange("(k p) n -> p k n", p=P)).then_inc(sems["router_w"], 16)
                for name, dst in (("b_group_2", router_b[:, 0:NG]), ("b_expert_2", router_b[:, NG:])):
                    pool.dma_start(dst, ins[name][layer:layer + 1, :].to_broadcast([P, dst.shape[1]]))\
                        .then_inc(sems["router_w"], 16)
                pool.memset(zeros, 0.0).then_inc(sems["zero_tile"], 1)
            pool.dma_start(final_g, ins["final_g_2"].rearrange("(o n) -> o n", o=1).to_broadcast([P, D]))\
                .then_inc(sems["final_gain"], 16)
            pool.wait_ge(*at("fin_x"))
            pool.dma_start(out[0].rearrange("(t p) d -> p t d", p=P), X).then_inc(sems["written"], 16)
            pool.wait_ge(sems["written"], 16)

        def second_block_pe(pe, at, plan, piece_ready):
            for layer in range(2):
                norm_pe(pe, at)
                slot = piece_ready(("win2", 0))
                w = w_cols(slot, WIN2_WIDTH[0])
                for t in range(NT):
                    for k in range(KD):
                        mm = pe.matmul(ps[t][:, 0:416], h2T[:, k, P * t:P * t + P], w[:, k, 0:416],
                                       start=(k == 0), stop=(k == KD - 1))
                    mm.then_inc(sems["p2_mm"], 1)
                for t in range(NT):
                    for k in range(KD):
                        mm = pe.matmul(ps[2][:, S * t:S * t + S], h2T[:, k, P * t:P * t + P], w[:, k, 416:672],
                                       start=(k == 0), stop=(k == KD - 1))
                mm.then_inc(sems["p2_mm"], 1)
                pe.wait_ge(*at("p2_mm", 3))
                pe.sem_inc(sems["piece_used"], 1)
                slot = piece_ready(("win2", 1))
                w = w_cols(slot, WIN2_WIDTH[1])
                for part in range(2):
                    for c in range(2):
                        for k in range(KD):
                            col = 256 * part + P * c
                            mm = pe.matmul(ps[3 + part][:, S * c:S * c + S], w[:, k, col:col + P], h2T[:, k, :],
                                           start=(k == 0), stop=(k == KD - 1))
                    mm.then_inc(sems["p2_mm"], 1)
                for t in range(NT):
                    for k in range(KD):
                        mm = pe.matmul(ps[5][:, S * t:S * t + S], h2T[:, k, P * t:P * t + P], w[:, k, 512:768],
                                       start=(k == 0), stop=(k == KD - 1))
                mm.then_inc(sems["p2_mm"], 1)
                pe.wait_ge(*at("p2_mm", 3))
                pe.sem_inc(sems["piece_used"], 1)
                pe.wait_ge(*at("p2_v", 3))
                pe.wait_ge(*at("p2_s", 3))
                if layer == 0:
                    pe.wait_ge(sems["const2"], 16)
                for g in range(4):
                    for s in range(NT):
                        mm = pe.matmul(ps[6][64 * (g % 2):64 * (g % 2) + 64, S * (g // 2):S * (g // 2) + S],
                                       pool_u[:, s, 64 * g:64 * g + 64], pool_mat[:, g, s, :],
                                       start=(s == 0), stop=(s == 1))
                mm.then_inc(sems["pool_d"], 1)
                for t in range(NT):
                    for m in range(2):
                        for hp in range(2):
                            n = P * (t + 1)
                            r = slice(64 * m, 64 * m + 64)
                            mm = pe.matmul(ps[2 * t + m][:, n * hp:n * hp + n], bqT[r, hp, P * t:P * t + P],
                                           bkT[r, hp, 0:n], start=True, stop=True)
                mm.then_inc(sems["st_mm"], 1)
                pe.wait_ge(*at("cq_n"))
                for t in range(NT):
                    for c in range(3):
                        mm = pe.transpose(ps[4 + t][:, P * c:P * c + P], cq[:, t, P * c:P * c + P], ident)
                mm.then_inc(sems["cq_T"], 1)
                pe.wait_ge(*at("pool_ds"))
                pe.wait_ge(*at("pool_w", 32))
                for g in range(4):
                    r = slice(64 * (g % 2), 64 * (g % 2) + 64)
                    mm = pe.matmul(ps[7][r, S * (g // 2):S * (g // 2) + S], pool_w[r, g // 2, :], pool_dT[r, g // 2, :],
                                   start=True, stop=True)
                mm.then_inc(sems["pool_y"], 1)
                pe.wait_ge(*at("st_a"))
                for b, (t, c) in enumerate(((0, 0), (1, 0), (1, 1))):
                    for h in range(4):
                        mm = pe.transpose(ps[b][:, P * h:P * h + P], st_block(st_e, h, t)[:, P * c:P * c + P], ident)
                mm.then_inc(sems["st_T"], 1)
                pe.wait_ge(*at("st_Ts"))
                for h in range(4):
                    m, hp = h % 2, h // 2
                    o = ps[6][64 * m:64 * m + 64, S * hp:S * hp + S]
                    pe.matmul(o, bv[:, 0, 64 * h:64 * h + 64], st_pT[:, h, 0, :], start=True, stop=False,
                              skip_group_check=True)
                    mm = pe.matmul(o[:, P:S], bv[:, 1, 64 * h:64 * h + 64], st_pT[:, h, 1, P:S], start=False, stop=True,
                                   skip_group_check=True)
                mm.then_inc(sems["st_pv"], 1)
                pe.wait_ge(*at("st_o"))
                pe.wait_ge(*at("pool_o"))
                pe.wait_ge(*at("cq_Ts"))
                slot = piece_ready(("mla", 0))
                uq = ring[:, slot, 0:1536].rearrange("p (k n) -> p k n", k=2)
                ukv = ring[:, slot, 1536:2560]
                for t in range(NT):
                    for b, (a, n) in enumerate(((0, 512), (512, 256))):
                        for k in range(2):
                            mm = pe.matmul(ps[4 * t + b][:, 0:n], cqT[:, k, P * t:P * t + P], uq[:, k, a:a + n],
                                           start=(k == 0), stop=(k == 1))
                    mm.then_inc(sems["q_mm"], 1)
                    for b in range(2):
                        mm = pe.matmul(ps[4 * t + 2 + b], cqT[:, 2, P * t:P * t + P], ukv[:, 512 * b:512 * b + 512],
                                       start=True, stop=True)
                    mm.then_inc(sems["kv_mm"], 1)
                pe.wait_ge(*at("kv_mm", 2))
                pe.sem_inc(sems["piece_used"], 1)
                for t in range(NT):
                    pe.wait_ge(*at("q_sb"))
                    pe.wait_ge(*at("kv_sb"))
                    for b in range(4):
                        src = q_tok if b < 2 else k_tok
                        for h in range(4):
                            mm = pe.transpose(ps[4 * t + b][0:96, P * h:P * h + P], src[:, t, 4 * (b % 2) + h, :], ident)
                        mm.then_inc(sems["head_T"], 1)
                pe.wait_ge(*at("head_v", 4))
                pe.wait_ge(*at("head_s", 4))
                attention_pe(pe, at, "mla")
                out_projection_pe(pe, at, piece_ready, "wout2", mixT)
                norm_pe(pe, at)
                experts_pe(pe, at, plan, 2)

        def st_block(x, h, t):
            o = (P * (h // 2)) if t == 0 else (2 * P + S * (h // 2))
            return x[:, h % 2, o:o + P * (t + 1)]

        def second_block_act(act, at, link):
            for layer in range(2):
                norm_act(act, at, PT["norm1_g_2"][:, KD * layer:KD * layer + KD], None)
                for t in range(NT):
                    act.wait_ge(*at("p2_mm"))
                    act.activation(cq[:, t, :], ps[t][:, 0:416], ACT.Copy).then_inc(sems["p2_s"], 1)
                act.wait_ge(*at("p2_s", 2))
                for t in range(NT):
                    link(act.activation(junk[:, 0:256], cq[:, t, 0:256], ACT.Square, accum_out=cols[:, 32 + t:33 + t]))
                    link(act.activation(junk[:, 0:128], cq[:, t, 256:384], ACT.Square, accum_out=cols[:, 34 + t:35 + t]))
                act.sem_inc(sems["cq_sq"], 1)
                act.wait_ge(*at("p2_mm", 2))
                act.activation(bqT.rearrange("p h n -> p (h n)"), ps[3], ACT.Copy, scale=0.125).then_inc(sems["p2_s"], 1)
                act.wait_ge(*at("p2_s"))
                act.wait_ge(*at("cq_mean"))
                act.activation(cols[:, 32:36], cols[:, 32:36], ACT.Sqrt).then_inc(sems["cq_sqrt"], 1)
                act.wait_ge(*at("pool_d"))
                act.activation(pool_dT.rearrange("p c n -> p (c n)"), ps[6], ACT.Copy).then_inc(sems["pool_ds"], 1)
                act.wait_ge(*at("st_zb"))
                link(act.activation(st_e, st_e, ACT.Exp))
                act.activation(st_e, st_e, ACT.Ln, bias=1.0).then_inc(sems["st_ln"], 1)
                act.wait_ge(*at("st_x"))
                act.activation(st_e, st_z, ACT.Exp).then_inc(sems["st_a"], 1)
                act.wait_ge(*at("st_T"))
                for b, (t, c) in enumerate(((0, 0), (1, 0), (1, 1))):
                    ins_ = act.activation(st_pT[:, :, c, P * t:P * t + P], ps[b].rearrange("p (h n) -> p h n", h=4), ACT.Copy)
                ins_.then_inc(sems["st_Ts"], 1)
                for t in range(NT):
                    act.wait_ge(*at("kv_mm"))
                    kv = psum[:, 4 * t + 2:4 * t + 4, :].rearrange("p b n -> p (b n)").rearrange("p (h u n) -> p h u n", h=8, u=2)
                    act.activation(k_tok[:, t, :, 0:64], kv[:, :, 0, :], ACT.Copy)
                    act.activation(v2[:, t, :, :], kv[:, :, 1, :], ACT.Copy).then_inc(sems["kv_sb"], 1)
                for t in range(NT):
                    for b in range(2):
                        act.wait_ge(*at.plus("head_T", 4 * t + b + 1))
                        act.activation(q2T[0:96, 4 * b:4 * b + 4, P * t:P * t + P],
                                       ps[4 * t + b][0:96, :].rearrange("p (h n) -> p h n", h=4), ACT.Copy)\
                            .then_inc(sems["head_s"], 1)
                at("head_T", 8), at("p2_mm", 2)
                attention_act(act, at, "mla")
                norm_act(act, at, PT["norm2_g_2"][:, KD * layer:KD * layer + KD], None)
                experts_act(act, at, 2)
            squares_act(act, at)

        def second_block_dve(dve, at, link):
            for layer in range(2):
                norm_dve(dve, at, link, PT["norm1_g_2"][:, KD * layer:KD * layer + KD], None)
                dve.wait_ge(*at("p2_mm", 3))
                dve.tensor_copy(pool_u.rearrange("p t n -> p (t n)"), ps[2]).then_inc(sems["p2_v"], 1)
                dve.wait_ge(*at("cq_sq"))
                link(dve.tensor_scalar(cols[:, 32:34], cols[:, 32:34], 1.0 / 256, EPS, ALU.mult, ALU.add))
                link(dve.tensor_scalar(cols[:, 34:36], cols[:, 34:36], 1.0 / 128, EPS, ALU.mult, ALU.add))
                dve.reciprocal(cols[:, 32:36], cols[:, 32:36]).then_inc(sems["cq_mean"], 1)
                dve.wait_ge(*at("p2_mm", 2))
                dve.tensor_copy(bkT.rearrange("p h n -> p (h n)"), ps[4]).then_inc(sems["p2_v"], 1)
                dve.wait_ge(*at("p2_mm"))
                dve.tensor_copy(bv.rearrange("p t n -> p (t n)"), ps[5]).then_inc(sems["p2_v"], 1)
                dve.wait_ge(*at("cq_sqrt"))
                if layer == 0:
                    dve.wait_ge(sems["const2"], 16)
                for t in range(NT):
                    dve.tensor_scalar(cq[:, t, 0:256], cq[:, t, 0:256], cols[:, 32 + t:33 + t], None, ALU.mult)
                    ins_ = dve.tensor_scalar(cq[:, t, 256:384], cq[:, t, 256:384], cols[:, 34 + t:35 + t], None, ALU.mult)
                ins_.then_inc(sems["cq_n"], 1)
                dve.wait_ge(*at("p2_v", 3))
                for t in range(NT):
                    cos = C2["rope_cos"][:, 32 * t:32 * t + 32]
                    sin = C2["rope_sin"][:, 32 * t:32 * t + 32]
                    kr = cq[:, t, 384:416]
                    for b in range(2):
                        dve.tensor_tensor(rot2b[:, t, 16 * b:16 * b + 16], kr[:, 16 - 16 * b:32 - 16 * b],
                                          sin[:, 16 * b:16 * b + 16], ALU.mult)
                    link(dve.tensor_tensor(rot2a[:, t, :], kr, cos, ALU.mult))
                    link(dve.tensor_tensor(key_rot[:, t, :], rot2a[:, t, :], rot2b[:, t, :], ALU.add))
                dve.wait_ge(*at("st_mm"))
                mask = C2["strict_mask"].unsqueeze(1).broadcast_to([P, 2, P])
                for m in range(2):
                    z0 = st_z[:, m, 0:2 * P].rearrange("p (h n) -> p h n", h=2)
                    z1 = st_z[:, m, 2 * P:].rearrange("p (h n) -> p h n", h=2)
                    p1 = ps[2 + m].rearrange("p (h n) -> p h n", h=2)
                    dve.tensor_tensor(z0, ps[m][:, 0:2 * P].rearrange("p (h n) -> p h n", h=2), mask, ALU.add)
                    dve.tensor_copy(z1[:, :, 0:P], p1[:, :, 0:P])
                    ins_ = dve.tensor_tensor(z1[:, :, P:2 * P], p1[:, :, P:2 * P], mask, ALU.add)
                link(ins_)
                dve.scalar_tensor_tensor(st_e, st_z, -1.0, st_z, ALU.mult, ALU.min).then_inc(sems["st_zb"], 1)
                dve.wait_ge(*at("cq_T"))
                for t in range(NT):
                    for c in range(3):
                        g = PT["q_norm_g_2"][:, 2 * layer + c:2 * layer + c + 1] if c < 2 else PT["kv_norm_g_2"][:, layer:layer + 1]
                        ins_ = dve.tensor_scalar(cqT[:, c, P * t:P * t + P], ps[4 + t][:, P * c:P * c + P], g, None, ALU.mult)
                ins_.then_inc(sems["cq_Ts"], 1)
                dve.wait_ge(*at("st_ln"))
                link(dve.scalar_tensor_tensor(st_e, st_z, 0.0, st_e, ALU.max, ALU.add))
                for t in range(NT):
                    for h in range(4):
                        n = P * (t + 1)
                        ins_ = dve.tensor_tensor_scan(st_block(st_s, h, t)[:, ::-1], ones[:, 0:1].broadcast_to([P, n]),
                                                      st_block(st_e, h, t)[:, ::-1], 0.0, ALU.mult, ALU.add)
                link(ins_)
                dve.tensor_tensor(st_z, st_z, st_s, ALU.subtract).then_inc(sems["st_x"], 1)
                dve.wait_ge(*at("pool_y"))
                for c in range(2):
                    ins_ = dve.tensor_scalar(mixT[:, 6 + c, :], ps[7][:, S * c:S * c + S],
                                             PT["pool_scale_2"][:, 2 * layer + c:2 * layer + c + 1], None, ALU.mult)
                ins_.then_inc(sems["pool_o"], 1)
                dve.wait_ge(*at("st_pv"))
                dve.tensor_copy(mixT[:, 4:6, :].rearrange("p c n -> p (c n)"), ps[6]).then_inc(sems["st_o"], 1)
                for t in range(NT):
                    dve.wait_ge(*at("q_mm"))
                    q = psum[:, 4 * t:4 * t + 2, :].rearrange("p b n -> p (b n)")[:, 0:768].rearrange("p (h n) -> p h n", h=8)
                    cos = C2["rope_cos"][:, 32 * t:32 * t + 32].unsqueeze(1).broadcast_to([P, 8, 32])
                    sin = C2["rope_sin"][:, 32 * t:32 * t + 32]
                    dve.tensor_copy(q_tok[:, t, :, 0:64], q[:, :, 0:64])
                    for b in range(2):
                        dve.tensor_tensor(rot2b[:, :, 16 * b:16 * b + 16], q[:, :, 80 - 16 * b:96 - 16 * b],
                                          sin[:, 16 * b:16 * b + 16].unsqueeze(1).broadcast_to([P, 8, 16]), ALU.mult)
                    dve.tensor_copy(k_tok[:, t, :, 64:96], key_rot[:, t, :].unsqueeze(1).broadcast_to([P, 8, 32]))
                    link(dve.tensor_tensor(rot2a, q[:, :, 64:96], cos, ALU.mult))
                    dve.tensor_tensor(q_tok[:, t, :, 64:96], rot2a, rot2b, ALU.add).then_inc(sems["q_sb"], 1)
                    dve.wait_ge(*at("q_sb"))
                for t in range(NT):
                    for b in range(2):
                        dve.wait_ge(*at.plus("head_T", 4 * t + 2 + b + 1))
                        dve.tensor_copy(k2T[0:96, 4 * b:4 * b + 4, P * t:P * t + P],
                                        ps[4 * t + 2 + b][0:96, :].rearrange("p (h n) -> p h n", h=4))\
                            .then_inc(sems["head_v"], 1)
                at("head_T", 8)
                attention_dve(dve, at, link, "mla")
                dve.sem_inc(sems["mixed"], 1)
                dve.wait_ge(*at("out_mm", 2))
                residual_dve(dve, at, link, 0)
                norm_dve(dve, at, link, PT["norm2_g_2"][:, KD * layer:KD * layer + KD], None)
                dve.wait_ge(*at("router_w", 64))
                route_dve(dve, at, link)
                experts_dve(dve, at, link, 2, PT["norm2_g_2"][:, KD * layer:KD * layer + KD], None)
                residual_dve(dve, at, link, 4)
            dve.wait_ge(sems["final_gain"], 16)
            final_dve(dve, at, link)

        @block.sync
        def _(sp):
            plan = Ring(sems)

            def straight(pieces, layer):
                for piece in pieces:
                    if plan.n >= RING:
                        sp.wait_ge(sems["piece_used"], plan.n - RING + 1)
                    slot, sem, _ = plan.place(dmas_of(piece))
                    start_piece(sp, slot, sem, piece, layer)

            sp.dma_start(X, ins["x"][0].rearrange("(t p) d -> p t d", p=P)).then_inc(sems["loaded_x"], 16)
            straight(first_pieces, 0)
            base, turns = plan.n, 2 * NE // RING
            slots = plan.loop(turns, RING, E1_DMAS)
            with sp.Fori(0, turns) as turn:
                for j, (slot, sem, _, _) in enumerate(slots):
                    sp.wait_ge(sems["piece_used"], turn * RING + (base + j - RING + 1))
                    half = turn * RING + j
                    sp.dma_start(e1_up(slot), up1[bass.ds(half, 1)][0]).then_inc(sem, 16)
                    sp.dma_start(e1_down(slot), down1[bass.ds(half, 1)][0]).then_inc(sem, 16)
            second_block_loads(sp, plan, straight)

        @block.gpsimd
        def _(pool):
            at = Tally(sems)
            pool.memset(cT, 0.0).then_inc(sems["zero_done"], 1)
            pool.memset(band, 0.0).then_inc(sems["zero_done"], 1)
            pool.memset(wdec, 0.0).then_inc(sems["zero_done"], 1)
            for name, (row, n) in row_places.items():
                src = ins[name]
                if name == "gla_norm_g":
                    for half in range(2):
                        pool.dma_start(rows[row:row + 1, 64 * half:64 * half + 64], src).then_inc(sems["params"], 16)
                    continue
                flat = flat_rows(src)
                pool.dma_start(rows[row:row + n, :], flat).then_inc(sems["params"], 16)
            pool.dma_start(const0, ins["const0"]).then_inc(sems["params"], 16)
            pool.wait_ge(*at("c_cols"))
            pool.dma_start(cx, ins["ctx"][0].rearrange("(t p) d -> p t d", p=P)).then_inc(sems["loaded_ctx"], 16)
            pool.dma_start(const1, ins["const1"]).then_inc(sems["params2"], 16)
            pool.dma_start(lam_row, ins["diff_lambda"][0:1].rearrange("o n d -> o (n d)").to_broadcast([P, 256])
                           .rearrange("p (n d) -> p n d", d=64)).then_inc(sems["params2"], 16)
            pool.wait_ge(sems["zero_done"], 3)
            for d in range(2):
                pool.dma_start(wdec[16 * d:16 * d + 16, d, :], ins["gla_w_decay"][0, d]).then_inc(sems["params2"], 16)
            pool.dma_start(router_b[:, 0:NG], ins["b_router_group"].to_broadcast([P, NG])).then_inc(sems["params2"], 16)
            pool.dma_start(router_b[:, NG:NG + NE], ins["b_router_expert"].to_broadcast([P, NE])).then_inc(sems["params2"], 16)
            for h in range(4):
                pool.dma_start(band[:, 7 * h:7 * h + 7, 48:79],
                               ins["na_rel_bias"][0, h:h + 1, 4:11, :].rearrange("o r c -> o (r c)")
                               .to_broadcast([GRID, 7 * 31]).rearrange("p (r c) -> p r c", c=31))\
                    .then_inc(sems["loaded_bias"], 16)
            pool.wait_ge(sems["loaded_bias"], 64)
            pool.dma_start(bias_dram[0:GRID * 28 * P].rearrange("(p n) -> p n", p=GRID), band_flat)\
                .then_inc(sems["bias_out"], 16)
            pool.wait_ge(sems["bias_out"], 16)
            pool.wait_ge(*at("mod_t", 12))
            pool.wait_ge(*at("mod_col", 12))
            pool.wait_ge(*at("lam"))
            for r in range(4):
                for h in range(4):
                    off = (7 * h + 3 - r) * P + 63
                    pitch = 28 * P - 1
                    src = bias_dram[off:off + GRID * pitch].rearrange("(q n) -> q n", n=pitch)[:, 0:4 * P]\
                        .rearrange("q (k c) -> q k c", k=4)[:, :, 0:GRID]
                    pool.dma_start(nb_bias[64 * (r % 2):64 * (r % 2) + 64, r // 2, h, :]
                                   .rearrange("q (k c) -> q k c", k=4), src).then_inc(sems["loaded_bias"], 16)
            pool.wait_ge(*at("mixed"))
            pool.dma_start(router_w[:, :, 0:NG], ins["w_router_group"][0].rearrange("(k p) n -> p k n", p=P))\
                .then_inc(sems["router_w"], 16)
            pool.dma_start(router_w[:, :, NG:], ins["w_router_expert"][0].rearrange("(k p) n -> p k n", p=P))\
                .then_inc(sems["router_w"], 16)
            pool.dma_start(final_g, ins["final_g"].rearrange("(o n) -> o n", o=1).to_broadcast([P, D]))\
                .then_inc(sems["router_w"], 16)
            pool.memset(zeros, 0.0).then_inc(sems["zero_tile"], 1)
            second_block_pool(pool, at)
        @block.tensor
        def _(pe):
            at = Tally(sems)
            plan = Ring(sems)
            windows["pe"] = counter(pe, "window_pe")

            def piece_ready(piece):
                slot, sem, value = plan.place(dmas_of(piece))
                pe.wait_ge(sem, value)
                return slot

            def turn(dst, src):
                return pe.transpose(dst, src, ident[0:src.shape[0], 0:src.shape[0]])

            pe.wait_ge(sems["params"], PARAMS)
            turn(ps[4][:, 0:n_rows], rows[0:n_rows, :]).then_inc(sems["c_T"], 1)
            pe.wait_ge(*at("c_cols", 2))

            def modulate(j):
                slot = piece_ready(("mod", j))
                w = w_cols(slot, 512)
                for k in range(KD):
                    for g in range(4):
                        mm = pe.matmul(ps[j % 2][32 * g:32 * g + 32, 0:P], cT[:, k, :], w[:, k, P * g:P * g + P],
                                       start=(k == 0), stop=(k == KD - 1))
                mm.then_inc(sems["mod_mm"], 1)
                pe.wait_ge(*at("mod_row"))
                if j >= 2:
                    pe.wait_ge(sems["mod_col"], j - 1)
                turn(ps[2 + j % 2][:, 0:P], mod_row[:, j % 2, :]).then_inc(sems["mod_t"], 1)
                pe.wait_ge(sems["mod_t"], j + 1)
                pe.sem_inc(sems["piece_used"], 1)

            for j in range(4):
                modulate(j)

            pe.wait_ge(*at("xn", 4))
            for k in range(KD):
                if k >= 4:
                    pe.wait_ge(sems["xT_v" if k % 2 == 0 else "xT_s"], (k - 4) // 2 + 1)
                for t in range(2 * NT):
                    src = (xn[:, t, :] if t < NT else cx[:, t - NT, :])[:, P * k:P * k + P]
                    mm = turn(ps[4 + k % 4][:, P * t:P * t + P], src)
                mm.then_inc(sems["x_T"], 1)
            pe.wait_ge(*at("xT_v", 4))
            pe.wait_ge(*at("xT_s", 4))

            where = {"qb": (0, 128, S), "kb": (128, 128, 2 * S), "rb": (256, 128, S), "gb": (512, 32, 2 * S),
                     "qn": (0, 128, S), "kn": (256, 128, 2 * S)}
            mods = iter(range(4, 12))
            piece = -1
            for n, (kind, of, what, i, who) in enumerate(UNITS):
                if kind != "X" and of != piece:
                    if 1 <= of <= 4:
                        modulate(next(mods))
                        modulate(next(mods))
                    piece = of
                    slot = piece_ready(("win", piece))
                    w = w_cols(slot, WIN_WIDTH[piece])
                emptied_before(pe, n)
                bank = ps[4 + n % 4]
                last = n + 1 == len(UNITS) or all(u[1] != of or u[0] == "X" for u in UNITS[n + 1:])
                if kind == "T":
                    col, m, tokens = where[what]
                    for k in range(KD):
                        mm = pe.matmul(bank[0:m, 0:tokens], w[:, k, col + P * i:col + P * i + m], hT[:, k, 0:tokens],
                                       start=(k == 0), stop=(k == KD - 1))
                elif kind == "K":
                    for k in range(KD):
                        mm = pe.matmul(bank, hT[:, k, P * i:P * i + P], w[:, k, :], start=(k == 0), stop=(k == KD - 1))
                else:
                    tile = i if what == "qa" else NT + i
                    pe.wait_ge(sems["rot_tile"], tile + 1)
                    for c in range(4):
                        mm = turn(bank[:, P * c:P * c + P], rot_o[:, tile % 2, P * c:P * c + P])
                mm.then_inc(sems["unit_mm"], 1)
                if kind != "X" and last:
                    pe.wait_ge(sems["unit_mm"], n + 1)
                    pe.sem_inc(sems["piece_used"], 1)

            pe.wait_ge(sems["params2"], PARAMS2)
            pe.wait_ge(sems["unit_s"], emptied(UNITS, len(UNITS), "s"))
            pe.wait_ge(sems["unit_v"], emptied(UNITS, len(UNITS), "v"))
            pe.wait_ge(sems["mod_row"], 12)
            for d in range(2):
                pe.matmul(ps[d], wdec[:, d, :], glow[0:32, :], start=True, stop=True).then_inc(sems["gate_z"], 1)
            pe.wait_ge(*at("gla_qk", 2))
            for h in range(4):
                if h:
                    pe.wait_ge(sems["gla_at"], h)
                r = slice(32 * h, 32 * h + 32)

                def part(d, name, a, n, _r=r):
                    o = {"base_q": 768, "base_k": 1024, "ctx_q": 1280, "ctx_k": 1536}.get(name, 256 * int(name[-1])
                                                                                     if name[0] == "l" else 0)
                    return qk[_r, d, o + a:o + a + n]

                A = ps[h].rearrange("p (s t) -> p s t", s=2)

                def block_mm(dst, d, key, query, s0, t0, n, m):
                    return pe.matmul(dst, part(d, key, s0, m), part(d, query, t0, n), start=True, stop=True)

                block_mm(A[:, 0, P:2 * P], 0, "l0", "l0", 0, P, P, P)
                block_mm(A[:, 1, 0:P], 1, "l0", "l0", P, 0, P, P)
                for u in range(2):
                    o = P * u
                    block_mm(A[0:64, u, o + 64:o + 128], 0, "l1", "l1", o, o + 64, 64, 64)
                    block_mm(A[64:128, u, o:o + 64], 1, "l1", "l1", o + 64, o, 64, 64)
                    for v in range(2):
                        a, b = 64 * v, 64 * v + 32
                        block_mm(A[a:a + 32, u, o + b:o + b + 32], 0, "l2", "l2", o + a, o + b, 32, 32)
                        block_mm(A[b:b + 32, u, o + a:o + a + 32], 1, "l2", "l2", o + b, o + a, 32, 32)
                    for j in range(4):
                        a = 32 * j
                        block_mm(A[a:a + 32, u, o + a:o + a + 32], 0, "base_k", "base_q", o + a, o + a, 32, 32)
                        mm = block_mm(ps[4][a:a + 32, 64 * h + 32 * u:64 * h + 32 * u + 32], 1, "base_k", "base_q",
                                      o + a, o + a, 32, 32)
                mm.then_inc(sems["gla_at"], 1)
                if h >= 2:
                    pe.wait_ge(sems["c_sb"], h - 1)
                for s in range(2):
                    for d in range(2):
                        mm = pe.matmul(ps[5 + h % 2][:, S * s:S * s + S], part(d, "ctx_k", P * s, P),
                                       part(d, "ctx_q", 0, S), start=(d == 0), stop=(d == 1))
                mm.then_inc(sems["gla_c"], 1)
                if h >= 1:
                    context_values(pe, at, h - 1)
            context_values(pe, at, 3)
            pe.wait_ge(*at("at_masked"))
            for h in range(4):
                o = ps[7][64 * (h % 2):64 * (h % 2) + 64, S * (h // 2):S * (h // 2) + S]
                for s in range(2):
                    mm = pe.matmul(o, vbn[:, s, 64 * h:64 * h + 64], atT[:, h, s, :], start=False,
                                   stop=(s == 1), skip_group_check=True)
            mm.then_inc(sems["gla_o"], 1)
            pe.wait_ge(*at("o_sq"))
            pe.matmul(ps[4], C0["ones64"], gl_s.rearrange("p h n -> p (h n)"), start=True, stop=True)\
                .then_inc(sems["gla_ss"], 1)

            pe.wait_ge(*at("gla_y"))
            attention_pe(pe, at, "na")
            attention_pe(pe, at, "diff")
            pe.wait_ge(*at("a_sq"))
            for b in range(2):
                mm = pe.matmul(ps[b], ones, oS[:, 2 * b:2 * b + 2, :].rearrange("p h n -> p (h n)"), start=True, stop=True)
            mm.then_inc(sems["a_ss"], 1)

            pe.wait_ge(*at("mixed"))
            out_projection_pe(pe, at, piece_ready, "wout", mixT)
            gate_broadcast_pe(pe, at, 4)
            norm_pe(pe, at)
            experts_pe(pe, at, plan, 1)
            gate_broadcast_pe(pe, at, 0)
            second_block_pe(pe, at, plan, piece_ready)


        @block.scalar
        def _(act):
            at = Tally(sems)
            windows["act"] = counter(act, "window_act")

            def link(ins):
                ins.then_inc(sems["scalar_step"], 1)
                act.wait_ge(*at("scalar_step"))

            act.wait_ge(*at("c_cols"))
            act.wait_ge(*at("zero_done", 3))
            act.activation(cT[:, :, 0:2], rowsT[:, 0:16].rearrange("p (i k) -> p k i", i=2), ACT.Silu)\
                .then_inc(sems["c_cols"], 1)
            act.wait_ge(sems["loaded_x"], 16)
            act.wait_ge(sems["loaded_ctx"], 16)
            for t in range(2 * NT):
                src = X[:, t, :] if t < NT else cx[:, t - NT, :]
                link(act.activation(hTf[:, D * t:D * t + D], src, ACT.Square, accum_out=ss[:, t:t + 1]))
            act.sem_inc(sems["sumsq"], 1)
            act.wait_ge(*at("mean"))
            act.activation(rstd, ss, ACT.Sqrt).then_inc(sems["sqrt_done"], 1)

            def mod_copy(j):
                act.wait_ge(*at("mod_mm"))
                if j >= 2:
                    act.wait_ge(sems["mod_t"], j - 1)
                act.activation(mod_row[:, j % 2, :], ps[j % 2][:, 0:P], ACT.Copy).then_inc(sems["mod_row"], 1)

            for j in range(4):
                mod_copy(j)
            act.wait_ge(*at("scale"))
            for k in range(1, KD, 2):
                act.wait_ge(sems["x_T"], k + 1)
                link(act.activation(hT[:, k, 0:S], ps[4 + k % 4][:, 0:S], ACT.Identity,
                                    bias=modT[:, k, 0:1], scale=scaleT[:, 0, k:k + 1]))
                act.activation(hT[:, k, S:2 * S], ps[4 + k % 4][:, S:2 * S], ACT.Identity,
                               bias=modT[:, k, 1:2], scale=scaleT[:, 1, k:k + 1]).then_inc(sems["xT_s"], 1)
            at("x_T", KD)
            mods = iter(range(4, 12))
            piece = -1
            act.wait_ge(sems["bias_out"], 16)
            for n, (kind, of, what, i, who) in enumerate(UNITS):
                if kind != "X" and of != piece:
                    if 1 <= of <= 4:
                        mod_copy(next(mods))
                        mod_copy(next(mods))
                    piece = of
                if who != "s":
                    continue
                act.wait_ge(sems["unit_mm"], n + 1)
                bank = ps[4 + n % 4]
                if kind == "X":
                    dst = qaT if what == "qa" else kaT
                    ins_ = act.activation(dst[:, :, P * i:P * i + P], bank.rearrange("p (c n) -> p c n", c=4), ACT.Copy)
                elif what == "qb":
                    ins_ = act.activation(qbT, bank[:, 0:S], ACT.Copy, scale=32.0 ** -0.5)
                elif what == "gb":
                    ins_ = act.activation(glow[0:32, :], bank[0:32, :], ACT.Copy)
                elif what == "rb":
                    ins_ = act.activation(rT[:, i, :], bank[:, 0:S], ACT.Silu)
                elif what == "qn":
                    ins_ = act.activation(qnT[:, i, :], bank[:, 0:S], ACT.Copy, scale=0.125)
                elif what == "kn":
                    ins_ = act.activation(knT[:, i, :], bank, ACT.Copy)
                else:
                    ins_ = act.activation(va[:, i, :], bank, ACT.Copy)
                ins_.then_inc(sems["unit_s"], 1)

            act.wait_ge(*at("z_bias"))
            link(act.activation(ze, ze, ACT.Exp))
            act.activation(ze, ze, ACT.Ln, bias=1.0).then_inc(sems["z_ln"], 1)
            for d in range(2):
                act.wait_ge(*at("gla_d"))
                link(act.activation(qk[:, d, 0:768], qk[:, d, 0:768], ACT.Exp))
                link(act.activation(qk[:, d, 768:1024], dif[:, 3, :], ACT.Exp, scale=1.0 if d == 0 else -1.0))
                link(act.activation(qk[:, d, 1024:1280], dif[:, 3, :], ACT.Exp, scale=-1.0 if d == 0 else 1.0))
                if d == 0:
                    link(act.activation(qk[:, d, 1280:1536], pre[:, d, 0, :], ACT.Exp))
                    link(act.activation(qk[:, d, 1536:1792], pre[:, d, 1, :], ACT.Exp, bias=pre[:, d, 1, S - 1:S], scale=-1.0))
                else:
                    link(act.activation(qk[:, d, 1280:1536], pre[:, d, 0, :], ACT.Exp, bias=cols[:, 0:1], scale=-1.0))
                    link(act.activation(qk[:, d, 1536:1792], pre[:, d, 1, :], ACT.Exp))
                act.sem_inc(sems["gla_e"], 1)
            for h in range(4):
                act.wait_ge(*at("gla_c"))
                if h >= 2:
                    act.wait_ge(sems["c_used"], h - 1)
                act.activation(ctT[:, h % 2, :, :].rearrange("p s n -> p (s n)"), ps[5 + h % 2], ACT.Copy)\
                    .then_inc(sems["c_sb"], 1)
            act.wait_ge(*at("o_sb"))
            act.activation(gl_s, gl_o, ACT.Square).then_inc(sems["o_sq"], 1)
            act.wait_ge(*at("gla_mean"))
            act.activation(gl_s, gl_s, ACT.Sqrt).then_inc(sems["gla_sqrt"], 1)
            act.wait_ge(*at("lam_sums"))
            act.activation(cols[:, 8:10], cols[:, 8:10], ACT.Exp).then_inc(sems["lam_exp"], 1)
            attention_act(act, at, "na")
            attention_act(act, at, "diff")
            act.wait_ge(*at("pv_sb", 2 + 4))
            act.activation(oS, oA, ACT.Square).then_inc(sems["a_sq"], 1)
            act.wait_ge(*at("a_mean"))
            act.activation(oS, oS, ACT.Sqrt).then_inc(sems["a_sqrt"], 1)
            norm_act(act, at, scaleT[:, 2, :], modT[:, 3 * KD:4 * KD, :])
            experts_act(act, at, 1)
            squares_act(act, at)
            second_block_act(act, at, link)

        @block.vector
        def _(dve):
            at = Tally(sems)
            windows["dve"] = counter(dve, "window_dve")
            windows["cur"] = counter(dve, "experts_dve")

            def link(ins):
                ins.then_inc(sems["vector_step"], 1)
                dve.wait_ge(*at("vector_step"))

            dve.wait_ge(*at("c_T"))
            dve.tensor_copy(rowsT[:, 0:n_rows], ps[4][:, 0:n_rows]).then_inc(sems["c_cols"], 1)
            dve.wait_ge(*at("c_cols", 2))
            dve.wait_ge(*at("sumsq"))
            link(dve.tensor_scalar(ss, ss, 1.0 / D, EPS, ALU.mult, ALU.add))
            dve.reciprocal(ss, ss).then_inc(sems["mean"], 1)
            dve.wait_ge(*at("sqrt_done"))
            for t in range(2 * NT):
                src = X[:, t, :] if t < NT else cx[:, t - NT, :]
                dst = xn[:, t, :] if t < NT else cx[:, t - NT, :]
                dve.tensor_scalar(dst, src, rstd[:, t:t + 1], None, ALU.mult).then_inc(sems["xn"], 1)

            def mod_columns(j):
                dve.wait_ge(*at("mod_t"))
                dve.tensor_tensor(modT[:, 4 * j:4 * j + 4, :],
                                  ps[2 + j % 2][:, 0:P].rearrange("p (g i) -> p g i", i=32)[:, :, 0:2],
                                  PT["b_mod"][:, 4 * j:4 * j + 4].unsqueeze(2).broadcast_to([P, 4, 2]), ALU.add)\
                    .then_inc(sems["mod_col"], 1)

            for j in range(4):
                mod_columns(j)
            dve.wait_ge(*at("mod_col", 4))
            for i in range(2):
                link(dve.tensor_scalar(scaleT[:, i, :], modT[:, KD:2 * KD, i], 1.0, None, ALU.add))
                link(dve.tensor_tensor(scaleT[:, i, :], scaleT[:, i, :], PT["norm1_g"], ALU.mult))
            dve.sem_inc(sems["scale"], 1)
            for k in range(0, KD, 2):
                dve.wait_ge(sems["x_T"], k + 1)
                link(dve.tensor_scalar(hT[:, k, 0:S], ps[4 + k % 4][:, 0:S], scaleT[:, 0, k:k + 1], modT[:, k, 0:1],
                                       ALU.mult, ALU.add))
                dve.tensor_scalar(hT[:, k, S:2 * S], ps[4 + k % 4][:, S:2 * S], scaleT[:, 1, k:k + 1],
                                  modT[:, k, 1:2], ALU.mult, ALU.add).then_inc(sems["xT_v"], 1)
            at("x_T", KD)
            dve.wait_ge(sems["params2"], PARAMS2)
            link(dve.tensor_tensor(lam_row[:, 0:3:2, :], lam_row[:, 0:3:2, :], lam_row[:, 1:4:2, :], ALU.mult))
            dve.tensor_reduce(cols[:, 8:10], lam_row[:, 0:3:2, :], AX, ALU.add).then_inc(sems["lam"], 1)
            dve.wait_ge(*at("lam"))
            dve.sem_inc(sems["lam_sums"], 1)

            def rotate(bank, tile):
                cos = C1["rope_cos"][:, 64 * tile:64 * tile + 64].unsqueeze(1).broadcast_to([P, 8, 64])
                x4 = bank.rearrange("p (h a b f) -> p h a b f", h=8, a=2, b=2)
                s4 = C1["rope_sin"][:, 64 * tile:64 * tile + 64].rearrange("p (a b f) -> p a b f", a=2, b=2)
                b4 = rot_b.rearrange("p (h a b f) -> p h a b f", h=8, a=2, b=2)
                for b in range(2):
                    dve.tensor_tensor(b4[:, :, :, b, :], x4[:, :, :, 1 - b, :],
                                      s4[:, :, b, :].unsqueeze(1).broadcast_to([P, 8, 2, 16]), ALU.mult)
                return cos

            tiles = 0
            mods = iter(range(4, 12))
            piece = -1
            dve.wait_ge(sems["bias_out"], 16)
            for n, (kind, of, what, i, who) in enumerate(UNITS):
                if kind != "X" and of != piece:
                    if 1 <= of <= 4:
                        mod_columns(next(mods))
                        mod_columns(next(mods))
                    piece = of
                if who != "v":
                    continue
                dve.wait_ge(sems["unit_mm"], n + 1)
                bank = ps[4 + n % 4]
                if what == "kb":
                    dve.tensor_copy(kbT, bank).then_inc(sems["unit_v"], 1)
                elif what == "vbn":
                    dve.tensor_copy(vbn[:, i, :], bank).then_inc(sems["unit_v"], 1)
                elif what == "qn":
                    dve.tensor_scalar(qnT[:, i, :], bank[:, 0:S], 0.125, None, ALU.mult).then_inc(sems["unit_v"], 1)
                elif what == "kn":
                    dve.tensor_copy(knT[:, i, :], bank).then_inc(sems["unit_v"], 1)
                elif what == "va":
                    dve.tensor_copy(va[:, i, :], bank).then_inc(sems["unit_v"], 1)
                else:
                    if tiles >= 2:
                        turned = [m for m, u in enumerate(UNITS) if u[0] == "X"][tiles - 2]
                        dve.wait_ge(sems["unit_mm"], turned + 1)
                    o = rot_o[:, tiles % 2, :]
                    if i < NT:
                        if tiles:
                            dve.wait_ge(sems["rot_tile"], tiles)
                        cos = rotate(bank, i)
                        x3 = bank.rearrange("p (h n) -> p h n", h=8)
                        dve.tensor_tensor(o.rearrange("p (h n) -> p h n", h=8), x3, cos, ALU.mult)\
                            .then_inc(sems["unit_v"], 1)
                        dve.wait_ge(sems["unit_v"], emptied(UNITS, n + 1, "v"))
                        dve.tensor_tensor(o, o, rot_b, ALU.add).then_inc(sems["rot_tile"], 1)
                    else:
                        dve.tensor_copy(o, bank).then_inc(sems["unit_v"], 1)
                        dve.wait_ge(sems["unit_v"], emptied(UNITS, n + 1, "v"))
                        dve.sem_inc(sems["rot_tile"], 1)
                    tiles += 1

            dve.wait_ge(*at("gate_z", 2))
            for d in range(2):
                link(dve.tensor_scalar(zg[:, d, :], ps[d], PT["gla_b_decay"][:, d:d + 1], None, ALU.add))
            dve.scalar_tensor_tensor(ze, zg, -1.0, zg, ALU.mult, ALU.min).then_inc(sems["z_bias"], 1)
            dve.wait_ge(*at("z_ln"))
            link(dve.scalar_tensor_tensor(zg, zg, 0.0, ze, ALU.min, ALU.subtract))
            link(dve.tensor_scalar(zg, zg, 1.0 / 16.0, None, ALU.mult))
            for d in range(2):
                for s in range(2):
                    ins_ = dve.tensor_tensor_scan(pre[:, d, s, :], ones[:, 0:1].broadcast_to([P, S]),
                                                  zg[:, d, S * s:S * s + S], 0.0, ALU.mult, ALU.add)
            link(ins_)
            link(dve.tensor_copy(cols[:, 0:1], pre[:, 1, 0, S - 1:S]))
            link(dve.tensor_tensor(pre[:, 1, :, :].rearrange("p s n -> p (s n)"),
                                   pre[:, 1, :, :].rearrange("p s n -> p (s n)"), zg[:, 1, :], ALU.subtract))

            def decayed(d):
                p = pre[:, d, 0, :]
                if d == 1:
                    dve.wait_ge(*at("gla_e"))
                for lv in range(4):
                    blk = S >> lv
                    v = p.rearrange("p (b n) -> p b n", n=blk)
                    mid = blk // 2 if (d == 1 or lv == 3) else blk // 2 - 1
                    link(dve.tensor_tensor(dif[:, lv, :].rearrange("p (b n) -> p b n", n=blk), v,
                                           v[:, :, mid:mid + 1].broadcast_to([P, S // blk, blk]), ALU.subtract))
                flat = dif[:, 0:3, :].rearrange("p l n -> p (l n)")
                dve.scalar_tensor_tensor(qk[:, d, 0:768], flat, -1.0, flat, ALU.mult, ALU.min)\
                    .then_inc(sems["gla_d"], 1)

            def products(d):
                for lv in range(3):
                    blk = S >> lv
                    view = lambda x: x.rearrange("p (b u n) -> p b u n", u=2, n=blk // 2)
                    e = view(qk[:, d, S * lv:S * lv + S])
                    for u in range(2):
                        who = view(qbT if (u == 1) == (d == 0) else kbT[:, 0:S])
                        dve.tensor_tensor(e[:, :, u, :], e[:, :, u, :], who[:, :, u, :], ALU.mult)
                for o, who in ((768, qbT), (1024, kbT[:, 0:S]), (1280, qbT), (1536, kbT[:, S:2 * S])):
                    e = qk[:, d, o:o + S]
                    ins_ = dve.tensor_tensor(e, e, who, ALU.mult)
                ins_.then_inc(sems["gla_qk"], 1)

            decayed(0)
            decayed(1)
            products(0)
            dve.wait_ge(*at("gla_e"))
            products(1)
            lim = 3.0e38
            dve.wait_ge(*at("gla_at", 4))
            for h in range(4):
                link(dve.tensor_scalar(atT[:, h, :, :].rearrange("p s n -> p (s n)"), ps[h], lim, -lim, ALU.min, ALU.max))
            link(dve.tensor_scalar(at_b, ps[4][:, 0:S], lim, -lim, ALU.min, ALU.max))
            b3 = at_b.rearrange("p (g n) -> p g n", n=32)
            link(dve.tensor_tensor(b3, b3, C1["mask_bwd"].unsqueeze(1).broadcast_to([P, 8, 32]), ALU.mult))
            for j in range(4):
                rows_ = slice(32 * j, 32 * j + 32)
                for h in range(4):
                    dg = diagonal(rows_, h, 32 * j)
                    dve.tensor_tensor(dg, dg, C1["mask_fwd"][rows_, :].unsqueeze(1).broadcast_to([32, 2, 32]), ALU.mult)
            link(dve.tensor_copy(cols[:, 1:2], cols[:, 0:1]))
            for j in range(4):
                rows_ = slice(32 * j, 32 * j + 32)
                for h in range(4):
                    dg = diagonal(rows_, h, 32 * j)
                    ins_ = dve.tensor_tensor(dg, dg, b3[rows_, 2 * h:2 * h + 2, :], ALU.add)
            ins_.then_inc(sems["at_masked"], 1)
            dve.wait_ge(*at("gla_o"))
            dve.tensor_copy(gl_o.rearrange("p h n -> p (h n)"), ps[7]).then_inc(sems["o_sb"], 1)
            dve.wait_ge(*at("gla_ss"))
            g2 = gl_s.rearrange("p h n -> p (h n)")
            link(dve.tensor_scalar(g2, ps[4], 1.0 / 64, EPS, ALU.mult, ALU.add))
            dve.reciprocal(g2, g2).then_inc(sems["gla_mean"], 1)
            dve.wait_ge(*at("gla_sqrt"))
            link(dve.scalar_tensor_tensor(gl_o, gl_o, PT["gla_norm_g"], gl_s, ALU.mult, ALU.mult))
            dve.tensor_tensor(mixT[:, 4:6, :], gl_o, rT, ALU.mult).then_inc(sems["gla_y"], 1)
            dve.wait_ge(*at("gla_y"))

            dve.wait_ge(sems["loaded_bias"], 64 + 16 * 16)
            for t in range(NT):
                b4 = nb_bias[:, t, :, :].rearrange("p h (k c) -> p (h k) c", c=GRID)
                ins_ = dve.tensor_tensor(b4, b4, C1["nb_mask"].unsqueeze(1).broadcast_to([P, 16, GRID]), ALU.add)
            link(ins_)
            dve.wait_ge(*at("lam_exp"))
            link(dve.tensor_tensor(cols[:, 10:11], cols[:, 9:10], cols[:, 8:9], ALU.subtract))
            link(dve.tensor_scalar(cols[:, 10:11], cols[:, 10:11], -LAM_INIT, None, ALU.add))
            link(dve.tensor_scalar(cols[:, 11:12], PT["diff_sub_g"], 1.0 - LAM_INIT, None, ALU.mult))
            attention_dve(dve, at, link, "na")
            attention_dve(dve, at, link, "diff")
            dve.wait_ge(*at("a_ss"))
            for b in range(2):
                half = oS[:, 2 * b:2 * b + 2, :].rearrange("p h n -> p (h n)")
                link(dve.tensor_scalar(half, ps[b], 1.0 / P, EPS, ALU.mult, ALU.add))
            dve.reciprocal(oS, oS).then_inc(sems["a_mean"], 1)
            dve.wait_ge(*at("a_sqrt"))
            dve.scalar_tensor_tensor(mixT[:, 0:4, :], oA, cols[:, 11:12], oS, ALU.mult, ALU.mult)\
                .then_inc(sems["mixed"], 1)
            dve.wait_ge(*at("mixed"))
            gate_diagonals_dve(dve, at, 2)
            link(dve.tensor_scalar(scaleT[:, 2, :], modT[:, 4 * KD:5 * KD, 0], 1.0, None, ALU.add))
            link(dve.tensor_tensor(scaleT[:, 2, :], scaleT[:, 2, :], PT["norm2_g"], ALU.mult))
            dve.wait_ge(*at("out_mm", 2))
            residual_dve(dve, at, link, 0, 4)
            norm_dve(dve, at, link, scaleT[:, 2, :], modT[:, 3 * KD:4 * KD, :])
            route_dve(dve, at, link)
            experts_dve(dve, at, link, 1, scaleT[:, 2, :], modT[:, 3 * KD:4 * KD, :])
            gate_diagonals_dve(dve, at, 5)
            residual_dve(dve, at, link, 4, 0)
            dve.wait_ge(*at("router_w", 48))
            final_dve(dve, at, link)
            second_block_dve(dve, at, link)



INS = ["x", "ctx", "c", "c_ctx", "w_mod", "b_mod", "norm1_g", "norm2_g", "w_in", "w_out", "diff_lambda", "diff_sub_g",
       "gla_w_decay", "gla_b_decay", "gla_norm_g", "na_rel_bias", "w_router_group", "b_router_group",
       "w_router_expert", "b_router_expert", "w_expert_up", "w_expert_down", "final_g", "norm1_g_2", "w_in_2",
       "q_norm_g_2", "w_uq_2", "kv_norm_g_2", "w_ukv_2", "pool_w_2", "pool_scale_2", "w_out_2", "norm2_g_2",
       "w_group_2", "b_group_2", "w_expert_2", "b_expert_2", "w_gate_2", "w_up_2", "w_down_2", "final_g_2"]
SCRATCH = GRID * 28 * P + 32 * P


def kernel(**inputs):
    import concourse.bacc as bacc
    from concourse.bass_utils import run_bass_kernel_spmd

    arrays = {n: np.ascontiguousarray(inputs[n]) for n in INS}
    arrays.update(shape_constants())
    nc = bacc.Bacc("TRN2", target_bir_lowering=False, num_devices=1)
    ins = {n: nc.dram_tensor(f"in_{n}", a.shape, F32, kind="ExternalInput").ap() for n, a in arrays.items()}
    ins["bias_scratch"] = nc.dram_tensor("bias_scratch", [SCRATCH], F32, kind="Internal").ap()
    out = nc.dram_tensor("out", [1, S, D], F32, kind="ExternalOutput").ap()
    hybrid_kernel(nc, ins, out)
    result = run_bass_kernel_spmd(nc, [{f"in_{n}": a for n, a in arrays.items()}], core_ids=[0])
    return result.results[0]["out"]
```

```python
from contextlib import ExitStack

import numpy as np
import concourse.bass as bass
from concourse import mybir

F32 = mybir.dt.float32
I32 = mybir.dt.int32
ALU = mybir.AluOpType
ACT = mybir.ActivationFunctionType
AX = mybir.AxisListType.X

P = 128
D = 1024
KD = D // P
S = 256
NT = S // P
SLOT = 4096
RING = 6
NE = 32
NG = 4
EG = NE // NG
GRID = 64
BIG = 1e30
EPS = 1e-6
LAM_INIT = 0.2

CONST_COLS = {"ident": P, "ones": P, "tri": P, "ones64": P, "slot64": P, "slot32": P, "iota8": 8, "step": 8}
CONST1_COLS = {"rope_cos": 2 * 64, "rope_sin": 2 * 64, "nb_mask": GRID, "mask_fwd": 32, "mask_bwd": 32}
CONST2_COLS = {"rope_cos": 2 * 32, "rope_sin": 2 * 32, "chunk_mask": P, "strict_mask": P, "pool": 4 * 2 * S}


def offsets(cols):
    at, out = 0, {}
    for name, n in cols.items():
        out[name] = (at, n)
        at += n
    return out, at


def rope_table(n_tokens, dim, positions):
    inv = np.float32(10000.0) ** (-np.arange(16, dtype=np.float32) / np.float32(16))
    cos, sin = [], []
    for pos in positions:
        ang = pos.astype(np.float32)[:, None] * inv.astype(np.float32)
        cos += [np.cos(ang), np.cos(ang)]
        sin += [-np.sin(ang), np.sin(ang)]
    cos, sin = (np.concatenate(x, axis=1).astype(np.float32) for x in (cos, sin))
    tile = lambda t: t.reshape(n_tokens // P, P, dim).transpose(1, 0, 2).reshape(P, -1)
    return tile(cos), tile(sin)


def shape_constants():
    r = np.arange(P)
    t = np.arange(S)
    c = {
        "ident": np.eye(P),
        "ones": np.ones((P, P)),
        "tri": r[:, None] < r[None, :],
        "ones64": (r[:, None] // 64) == (r[None, :] // 64),
        "slot64": np.broadcast_to(r % 64, (P, P)),
        "slot32": np.broadcast_to(r % 32, (P, P)),
        "iota8": np.broadcast_to(np.arange(8), (P, 8)),
        "step": np.broadcast_to(np.arange(8) + 1, (P, 8)),
    }
    cos, sin = rope_table(S, 64, [t // GRID, t % GRID])
    q = r % GRID
    start = np.clip(q - 8, 0, GRID - 16)
    k = np.arange(GRID)
    inside = (k[None, :] >= start[:, None]) & (k[None, :] < start[:, None] + 16)
    s32, t32 = r[:, None] % 32, np.arange(32)[None, :]
    c1 = {
        "rope_cos": cos, "rope_sin": sin, "nb_mask": np.where(inside, 0.0, -BIG),
        "mask_fwd": t32 >= s32, "mask_bwd": s32 >= t32,
    }
    cos, sin = rope_table(S, 32, [t])
    pool = np.zeros((4, S, S))
    for g, w in enumerate((2, 4, 8, 16)):
        for tt in range(S):
            lo = max(0, tt - w + 1)
            pool[g, lo:tt + 1, tt] = np.float32(1.0) / np.float32(min(tt + 1, w))
            pool[g, tt, tt] -= 1.0
    pool = pool.reshape(4, 2, P, S).transpose(2, 0, 1, 3).reshape(P, -1)
    c2 = {
        "rope_cos": cos, "rope_sin": sin,
        "chunk_mask": np.where(r[None, :] // 64 <= r[:, None] // 64, 0.0, -BIG),
        "strict_mask": np.where(r[None, :] < r[:, None], 0.0, -BIG),
        "pool": pool,
    }
    pack = lambda d, cols: np.concatenate([np.asarray(d[n], np.float32).reshape(P, -1) for n in cols], axis=1)
    return {"const0": pack(c, CONST_COLS), "const1": pack(c1, CONST1_COLS), "const2": pack(c2, CONST2_COLS)}


QB, KB, VB, RB, GB, QN, KN, VN = 1536, 1664, 1792, 2048, 2304, 2336, 2592, 2848

def straight_pieces():
    mods = [("mod", j) for j in range(12)]
    wins = [("win", j) for j in range(7)]
    first = mods[:4] + wins[:2]
    for j in range(4):
        first += mods[4 + 2 * j:6 + 2 * j] + [wins[2 + j]]
    first += [wins[6], ("wout", 0), ("wout", 1)]
    second = [("win2", 0), ("win2", 1), ("win2", 2), ("mla", 0), ("wout2", 0), ("wout2", 1)]
    return first, second


def projection_units():
    u = [("T", 0, "qb", 0, "s"), ("T", 0, "kb", 0, "v"), ("T", 0, "rb", 0, "s"), ("T", 0, "rb", 1, "s"),
         ("T", 1, "gb", 0, "s")]
    u += [("K", 2, "vbn", t, "v") for t in range(4)]
    u += [("T", 3, "qn", 0, "s"), ("T", 3, "qn", 1, "v"), ("T", 3, "kn", 0, "s"), ("T", 3, "kn", 1, "v")]
    u += [("K", 4, "qa", 0, "v"), ("K", 4, "qa", 1, "v"), ("X", 4, "qa", 0, "s")]
    u += [("K", 5, "ka", 0, "v"), ("X", 4, "qa", 1, "s"), ("K", 5, "ka", 1, "v"), ("X", 5, "ka", 0, "s"),
          ("K", 5, "ka", 2, "v"), ("X", 5, "ka", 1, "s"), ("K", 5, "ka", 3, "v"), ("X", 5, "ka", 2, "s")]
    u += [("K", 6, "va", 0, "s"), ("X", 5, "ka", 3, "s")]
    u += [("K", 6, "va", t, "v" if t % 2 else "s") for t in range(1, 4)]
    return u


UNITS = projection_units()


def emptied(units, n, engine):
    return sum(1 for u in units[:n] if u[4] == engine)


SEMS = """params loaded_x loaded_ctx loaded_bias bias_out piece0 piece1 piece2 piece3 piece4 piece5 piece_used
vector_step scalar_step c_T c_cols mod_mm mod_row mod_t mod_col
sumsq mean sqrt_done xn x_T xT_v xT_s unit_mm unit_v unit_s rot_tile zero_done
gate_z z_bias z_ln gla_d gla_e gla_qk gla_at gla_c c_sb at_masked gla_o o_sb o_sq gla_ss gla_mean gla_sqrt gla_y
score neg_max exps probs tr tr_sb pv pv_sb a_sq a_ss a_mean a_sqrt mixed
diag gate_bc out_mm resid
logits lg lg_exp route rank_mm 
w_sel w_gath w_ct w_csb w_up w_silu w_hid w_ht w_hsb w_y w_comb w_got_s w_got_v w_gt0 w_gt1 w_xg_v w_xg_s w_ysb_s w_ysb_v w_selg p2_mm p2_s p2_v st_mm pool_w head_s head_v final_gain moe_mm
fin_x
cq_sq cq_mean cq_sqrt cq_n cq_T cq_Ts q_mm q_sb kv_mm kv_sb head_T 
st_zb st_ln st_x st_a st_T st_Ts st_pv st_o pool_d pool_ds pool_y pool_o
const2 params2 written scale lam lam_sums lam_exp router_w zero_tile ranked w_cur w_xm c_used """.split()


ROWS = {"c": 8, "c_ctx": 8, "b_mod": 48, "norm1_g": 8, "norm2_g": 8, "norm1_g_2": 16, "norm2_g_2": 16,
        "q_norm_g_2": 4, "kv_norm_g_2": 2, "pool_scale_2": 4, "diff_sub_g": 1, "gla_b_decay": 2, "gla_norm_g": 1}
PARAMS = 16 * (len(ROWS) + 2)
PARAMS2 = 16 * 6


def flat_rows(src):
    names = "abcd"[:len(src.shape)]
    flat = src if len(names) == 1 else src.rearrange(f"{' '.join(names)} -> ({' '.join(names)})")
    return flat.rearrange("(r n) -> r n", n=P)


class Tally:

    def __init__(self, sems):
        self.sems, self.n = sems, {name: 0 for name in sems}

    def __call__(self, name, k=1):
        self.n[name] += k
        return self.sems[name], self.n[name]

    def plus(self, name, k):
        return self.sems[name], self.n[name] + k


class Ring:

    def __init__(self, sems):
        self.sems, self.n, self.loads = sems, 0, [0] * RING

    def place(self, dmas):
        slot = self.n % RING
        self.n += 1
        self.loads[slot] += 16 * dmas
        return slot, self.sems[f"piece{slot}"], self.loads[slot]

    def loop(self, turns, per_turn, dmas, dmas_down):
        assert per_turn == RING
        out = []
        for j in range(per_turn):
            slot, step = (self.n + j) % RING, 16 * (dmas if j < 4 else dmas_down)
            out.append((slot, self.sems[f"piece{slot}"], self.loads[slot], step))
            self.loads[slot] += step * turns
        self.n += turns * per_turn
        return out


DMAS = {"mod": 1, "win": 1, "wout": 1, "win2": 1, "mla": 2, "wout2": 1}
WIN_COLS = [[(QB, 256), (RB, 256)], [(GB, 32)], [(VB, 256), (VN, 256)], [(QN, 512)], [(0, 512)], [(512, 512)],
            [(1024, 512)]]
WIN_WIDTH = [sum(n for _, n in cols) for cols in WIN_COLS]
WIN2_COLS = [[(0, 416)], [(1184, 256), (928, 256)], [(416, 512)]]
WIN2_WIDTH = [sum(n for _, n in cols) for cols in WIN2_COLS]


def dmas_of(piece):
    kind, j = piece
    if kind == "win":
        return len(WIN_COLS[j])
    if kind == "win2":
        return len(WIN2_COLS[j])
    return DMAS[kind]


def hybrid_kernel(nc, ins, out):
    first_pieces, second_pieces = straight_pieces()
    row_places, n_rows = offsets(ROWS)
    c0, n_c0 = offsets(CONST_COLS)
    c1, n_c1 = offsets(CONST1_COLS)
    c2, n_c2 = offsets(CONST2_COLS)

    with ExitStack() as ctx:
        def sb(name, cols, dt=F32, rows=P):
            return ctx.enter_context(nc.sbuf_tensor(name, [rows, cols], dt))[:, :]

        sems = {name: ctx.enter_context(nc.semaphore(name)) for name in SEMS}

        ring = sb("ring", RING * SLOT).rearrange("p (r n) -> p r n", r=RING)
        X = sb("X", NT * D).rearrange("p (t d) -> p t d", t=NT)
        xn = sb("xn", NT * D).rearrange("p (t d) -> p t d", t=NT)
        hTf = sb("hT", KD * 2 * S)
        hT = hTf.rearrange("p (k n) -> p k n", k=KD)
        h2T = hTf[:, 0:KD * S].rearrange("p (k n) -> p k n", k=KD)
        const0 = sb("const0_sb", n_c0)
        C0 = {n: const0[:, a:a + w] for n, (a, w) in c0.items()}
        ident, ones, tri = C0["ident"], C0["ones"], C0["tri"]
        small = sb("small", 400)
        modT = small[:, 0:96].rearrange("p (j i) -> p j i", i=2)
        scaleT = small[:, 96:120].rearrange("p (n k) -> p n k", k=KD)
        ss = small[:, 120:124]
        rstd = small[:, 124:128]
        rowsT = small[:, 128:256]
        PT = {n: rowsT[:, a:a + w] for n, (a, w) in row_places.items()}
        router_b = small[:, 256:292]
        cols = small[:, 292:400]
        psum = ctx.enter_context(nc.psum_tensor("psum", [P, 8, 512], F32))
        ps = [psum[:, b, :] for b in range(8)]
        bias_dram = ins["bias_scratch"]

        arena = sb("arena", 18944)
        at_col = [0]

        def area(n):
            at_col[0] += n
            return arena[:, at_col[0] - n:at_col[0]]

        cxf = area(2048)
        rotf = area(1536)
        cx = cxf.rearrange("p (t d) -> p t d", t=NT)
        rot_b, rot_o = rotf[:, 0:512], rotf[:, 512:1536].rearrange("p (b n) -> p b n", b=2)
        qk = arena[:, 0:3584].rearrange("p (d n) -> p d n", d=2)
        probs1 = cxf.rearrange("p (b m n) -> p b m n", b=2, m=2)
        qaT = area(1024).rearrange("p (h n) -> p h n", h=4)
        kaT = area(2048).rearrange("p (h n) -> p h n", h=4)
        va = area(2048).rearrange("p (t n) -> p t n", t=4)
        vbn = area(2048).rearrange("p (t n) -> p t n", t=4)
        qnT = area(512).rearrange("p (h n) -> p h n", h=2)
        knT = area(1024).rearrange("p (h n) -> p h n", h=2)
        qbT = area(256)
        kbT = area(512)
        rT = area(512).rearrange("p (h n) -> p h n", h=2)
        glow = area(512)
        nb_biasf = area(2048)
        nb_bias = nb_biasf.rearrange("p (t h n) -> p t h n", t=2, h=4)
        const1 = area(n_c1)
        C1 = {n: const1[:, a:a + w] for n, (a, w) in c1.items()}
        mixf = area(2048)
        mixT = mixf.rearrange("p (k n) -> p k n", k=KD)
        wdec = area(256)[0:32, :].rearrange("p (d n) -> p d n", d=2)
        rows = cxf[:, 0:P]
        cT = nb_biasf[:, 0:256].rearrange("p (k i) -> p k i", i=32)
        mod_row = nb_biasf[:, 256:512].rearrange("p (b n) -> p b n", b=2)
        lam_row = nb_biasf[:, 512:768].rearrange("p (n d) -> p n d", d=64)
        zg = xn[:, 0, :].rearrange("p (d n) -> p d n", d=2)
        ze = xn[:, 1, :].rearrange("p (d n) -> p d n", d=2)
        pre = mixf[:, 0:1024].rearrange("p (d s n) -> p d s n", d=2, s=2)
        dif = hTf[:, 0:1024].rearrange("p (l n) -> p l n", l=4)
        atT = hTf[:, 1024:3072].rearrange("p (h s n) -> p h s n", h=4, s=2)
        ctT = hTf[:, 3072:4096].rearrange("p (b s n) -> p b s n", b=2, s=2)
        gl_o = hTf[:, 0:512].rearrange("p (h n) -> p h n", h=2)
        gl_s = hTf[:, 512:1024].rearrange("p (h n) -> p h n", h=2)
        at_b = rotf[:, 0:256]
        prT = hTf.rearrange("p (b m k n) -> p b m k n", b=2, m=2, k=4)
        oA = xn[:, 0, :].rearrange("p (h n) -> p h n", h=4)
        oS = xn[:, 1, :].rearrange("p (h n) -> p h n", h=4)
        band_flat = arena[0:GRID, 3584:7168]
        band = band_flat.rearrange("p (r u) -> p r u", u=P)
        work = arena[:, 0:3584]
        sel_gate = work[:, 0:256].rearrange("p (t n) -> p t n", t=NT)
        sel = work[:, 256:512].rearrange("p (t n) -> p t n", t=NT)
        comb = work[:, 512:768]
        cur = work[:, 768:784]
        silu_sb, hid = work[:, 784:1296], work[:, 1296:1808]
        hidT = work[:, 1808:2320].rearrange("p (c n) -> p c n", c=4)
        gotT = work[:, 2320:3344].rearrange("p (k n) -> p k n", k=KD)
        got = arena[:, 11008:12032]
        y_sb = arena[:, 12032:13056]
        junk = arena[:, 3584:4608]
        router_w = kaT.rearrange("p h n -> p (h n)")[:, 0:288].rearrange("p (k n) -> p k n", k=KD)
        rt = kaT.rearrange("p h n -> p (h n)")[:, 288:2048]
        ranks = rt[:, 0:128].rearrange("p (r e) -> p r e", e=NE)
        chosen = rt[:, 128:192].rearrange("p (t e) -> p t e", t=NT)
        lg = rt[:, 192:272].rearrange("p (t n) -> p t n", t=NT)
        r8 = rt[:, 272:272 + 16 * 12].rearrange("p (n t e) -> p n t e", t=NT, e=EG)
        r4 = rt[:, 480:480 + 8 * 6].rearrange("p (n t g) -> p n t g", t=NT, g=NG)
        r1 = rt[:, 544:544 + 2 * 16].rearrange("p (n t) -> p n t", t=NT)
        r32 = rt[:, 600:664].rearrange("p (t e) -> p t e", t=NT)
        extra_f = rt[0:1, 664:696]
        extra_cmp = rt[0:1, 704:960].rearrange("p (e j) -> p e j", j=8)
        extra = ctx.enter_context(nc.sbuf_tensor("extra", [1, NE], I32))
        zeros = rt[:, 960:1088]
        extra_m = rt[0:1, 1088:1104]
        final_g = va.rearrange("p t n -> p (t n)")[:, 0:D]
        vbf = vbn.rearrange("p t n -> p (t n)")
        gate_diag = vbf[:, 0:D].rearrange("p (k n) -> p k n", k=KD)
        gate_sb = vbf[:, D:2 * D]
        res_tmp = vbf[:, 0:D]
        junk2 = arena[:, 2560:3584]
        def lie(start, n):
            return arena[:, start:start + n]

        const2 = lie(7680, n_c2)
        C2 = {n: const2[:, a:a + w] for n, (a, w) in c2.items()}
        low = 7680 + n_c2
        cq = lie(low, 832).rearrange("p (t n) -> p t n", t=NT)
        pool_u = lie(low + 832, 512).rearrange("p (t n) -> p t n", t=NT)
        bqT = lie(low + 1344, 512).rearrange("p (h n) -> p h n", h=2)
        bkT = lie(low + 1856, 512).rearrange("p (h n) -> p h n", h=2)
        bv = lie(low + 2368, 512).rearrange("p (t n) -> p t n", t=NT)
        pool_dT = lie(low + 2880, 512).rearrange("p (c n) -> p c n", c=2)
        pool_w = lie(low + 3392, 128).rearrange("p (c n) -> p c n", c=2)
        st_z = lie(low + 3520, 1536).rearrange("p (m n) -> p m n", m=2)
        rot2a = lie(low + 5056, 256).rearrange("p (h n) -> p h n", h=8)
        rot2b = lie(low + 5312, 256).rearrange("p (h n) -> p h n", h=8)
        key_rot = lie(low + 5568, 64).rearrange("p (t n) -> p t n", t=NT)
        st_e = work[:, 0:1536].rearrange("p (m n) -> p m n", m=2)
        st_s = work[:, 1536:3072].rearrange("p (m n) -> p m n", m=2)
        q_tok = work[:, 0:1536].rearrange("p (t h n) -> p t h n", t=NT, h=8)
        k_tok = work[:, 1536:3072].rearrange("p (t h n) -> p t h n", t=NT, h=8)
        v2 = lie(4608, 1024).rearrange("p (t h n) -> p t h n", t=NT, h=8)
        cqT = lie(5632, 768).rearrange("p (c n) -> p c n", c=3)
        q2T = hTf[:, 0:2048].rearrange("p (h n) -> p h n", h=8)
        k2T = hTf[:, 2048:4096].rearrange("p (h n) -> p h n", h=8)
        probs2 = lie(3584, 1024).rearrange("p (b m n) -> p b m n", b=2, m=2)
        xnf = xn.rearrange("p t d -> p (t d)")
        st_pT = xnf.rearrange("p (h c n) -> p h c n", h=4, c=2)
        prT2 = xnf.rearrange("p (b m c n) -> p b m c n", b=2, m=2, c=2)
        pool_mat = C2["pool"].rearrange("p (g s n) -> p g s n", g=4, s=NT)

        def pr_of(kind):
            return probs1 if kind != "mla" else probs2

        def prT_of(kind):
            return prT if kind != "mla" else prT2

        def mix_of(kind):
            return mixT

        def junk_of(t):
            return junk if t == 0 else junk2
        windows = {}

        def counter(eng, name):
            reg = ctx.enter_context(eng.register(name))
            eng.reg_mov(reg, 0)
            return reg

        block = ctx.enter_context(nc.Block())

        def w_cols(slot, width):
            return ring[:, slot, 0:KD * width].rearrange("p (k n) -> p k n", k=KD)

        def start_piece(sp, slot, sem, piece, layer):
            kind, j = piece
            if kind == "mod":
                src = ins["w_mod"][0].rearrange("(k p) n -> p k n", p=P)[:, :, 512 * j:512 * j + 512]
                sp.dma_start(w_cols(slot, 512), src).then_inc(sem, 16)
            elif kind in ("win", "win2"):
                cols_, width = (WIN_COLS, WIN_WIDTH) if kind == "win" else (WIN2_COLS, WIN2_WIDTH)
                w = ins["w_in"][0] if kind == "win" else ins["w_in_2"][layer]
                at = 0
                for col, n in cols_[j]:
                    sp.dma_start(w_cols(slot, width[j])[:, :, at:at + n],
                                 w.rearrange("(k p) n -> p k n", p=P)[:, :, col:col + n]).then_inc(sem, 16)
                    at += n
            elif kind in ("wout", "wout2"):
                w = ins["w_out"][0] if kind == "wout" else ins["w_out_2"][layer]
                sp.dma_start(ring[:, slot, 0:4 * D].rearrange("p (k n) -> p k n", k=4),
                             w[512 * j:512 * j + 512, :].rearrange("(k p) n -> p k n", p=P)).then_inc(sem, 16)
            elif kind == "mla":
                sp.dma_start(ring[:, slot, 0:1536].rearrange("p (k n) -> p k n", k=2),
                             ins["w_uq_2"][layer].rearrange("(k p) n -> p k n", p=P)).then_inc(sem, 16)
                sp.dma_start(ring[:, slot, 1536:2560], ins["w_ukv_2"][layer]).then_inc(sem, 16)

        up1 = ins["w_expert_up"][0].rearrange("(b e) (k p) n -> b p e k n", e=2, p=P)
        down1 = ins["w_expert_down"][0].rearrange("(b e) (k p) n -> b p e k n", e=2, p=P)

        def expert_loads(sp, plan, which, ups, down):
            nb, _, hidden = batch_of(which)
            base, turns = plan.n, NE // nb
            slots = plan.loop(turns, RING, 2 * len(ups), hidden // P // 2)
            with sp.Fori(0, turns) as turn:
                for j, (slot, sem, _, _) in enumerate(slots):
                    sp.wait_ge(sems["piece_used"], turn * RING + (base + j - RING + 1))
                    if j < 4:
                        v = piece_view(slot, which, False)
                        for u, src in enumerate(ups):
                            for kk in range(2):
                                sp.dma_start(v[:, :, kk, :] if which == 1 else v[:, u, :, kk, :],
                                             src[bass.ds(turn, 1)][0][:, :, 2 * j + kk, :]).then_inc(sem, 16)
                    else:
                        per = hidden // P // 2
                        for kk in range(per):
                            sp.dma_start(piece_view(slot, which, True)[:, :, kk, :],
                                         down[bass.ds(turn, 1)][0][:, :, per * (j - 4) + kk, :]).then_inc(sem, 16)


        def items_of(kind):
            return [(g, t) for g in range(2 if kind == "na" else 4) for t in range(NT)]

        def keys_of(kind, t):
            return P * (t + 1) if kind == "mla" else 4 * P

        def attention_pe(pe, at, kind):
            items = items_of(kind)

            def scores(i):
                g, t = items[i]
                if i >= 2:
                    pe.wait_ge(*at.plus("exps", i - 1))
                for m in range(2):
                    if kind == "mla":
                        q, k = q2T[0:96, 2 * g + m, P * t:P * t + P], k2T[0:96, 2 * g + m, 0:P * (t + 1)]
                    else:
                        q_all, k_all = (qnT, knT) if kind == "na" else (qaT, kaT)
                        q, k = q_all[64 * m:64 * m + 64, g, P * t:P * t + P], k_all[64 * m:64 * m + 64, g, :]
                    mm = pe.matmul(ps[2 * (i % 2) + m][:, 0:keys_of(kind, t)], q, k, start=True, stop=True)
                mm.then_inc(sems["score"], 1)

            def turns(i):
                g, t = items[i]
                pe.wait_ge(*at.plus("probs", i + 1))
                lag = 2 if kind == "diff" else 1
                if i >= lag:
                    pe.wait_ge(*at.plus("tr_sb", i + 1 - lag))
                for m in range(1 if kind == "diff" else 2):
                    bank = ps[4 + (i % 2 if kind == "diff" else m)]
                    for c in range(keys_of(kind, t) // P):
                        mm = pe.transpose(bank[:, P * c:P * c + P], pr_of(kind)[:, i % 2, m, P * c:P * c + P], ident)
                mm.then_inc(sems["tr"], 1)

            def values(i):
                g, _ = items[i]
                pe.wait_ge(*at.plus("tr_sb", i + 1))
                if g >= 2:
                    pe.wait_ge(*at.plus("pv_sb", g - 1))
                bank = ps[6 + g % 2]
                for m in range(1 if kind == "diff" else 2):
                    for c in range(2 if kind == "mla" else 4):
                        if kind == "diff":
                            dst, v = bank[:, 0:S], va[:, c, P * g:P * g + P]
                        elif kind == "na":
                            dst, v = bank[64 * m:64 * m + 64, 0:S], vbn[:, c, S + 64 * (2 * g + m):S + 64 * (2 * g + m) + 64]
                        else:
                            dst, v = bank[64 * m:64 * m + 64, P * c:S], v2[:, c, 2 * g + m, :]
                        rhs = prT_of(kind)[:, g % 2, m, c, :]
                        if kind == "mla":
                            rhs = rhs[:, P * c:S]
                        mm = pe.matmul(dst, v, rhs, start=(c == 0), stop=(c == (1 if kind == "mla" else 3)))
                mm.then_inc(sems["pv"], 1)

            scores(0)
            for i in range(len(items)):
                if i + 1 < len(items):
                    scores(i + 1)
                turns(i)
                if items[i][1] == NT - 1:
                    values(i)
            for name, n in (("exps", len(items)), ("probs", len(items)), ("tr_sb", len(items)), ("pv_sb", len(items) // 2)):
                pe.wait_ge(*at(name, n))

        def attention_act(act, at, kind):
            items = items_of(kind)
            scale = {"na": 1.0, "diff": 0.125, "mla": 96.0 ** -0.5}[kind]

            def exps(i):
                g, t = items[i]
                act.wait_ge(*at.plus("neg_max", i + 1))
                if i >= 2:
                    act.wait_ge(*at.plus("tr", i - 1))
                n = keys_of(kind, t)
                for m in range(2):
                    a = 16 + 2 * (i % 2) + m
                    ins_ = act.activation(pr_of(kind)[:, i % 2, m, 0:n], ps[2 * (i % 2) + m][:, 0:n], ACT.Exp,
                                          bias=cols[:, a:a + 1], scale=scale, accum_out=cols[:, a + 4:a + 5])
                ins_.then_inc(sems["exps"], 1)

            def copies(i):
                g, t = items[i]
                act.wait_ge(*at.plus("tr", i + 1))
                if g >= 2 and t == 0:
                    act.wait_ge(*at.plus("pv", g - 1))
                c = keys_of(kind, t) // P
                for m in range(1 if kind == "diff" else 2):
                    bank = ps[4 + (i % 2 if kind == "diff" else m)]
                    ins_ = act.activation(prT_of(kind)[:, g % 2, m, 0:c, P * t:P * t + P],
                                          bank[:, 0:P * c].rearrange("p (c n) -> p c n", c=c), ACT.Copy)
                ins_.then_inc(sems["tr_sb"], 1)

            exps(0)
            for i in range(len(items)):
                if i + 1 < len(items):
                    exps(i + 1)
                copies(i)
            at("neg_max", len(items)), at("tr", len(items)), at("pv", len(items) // 2)

        def attention_dve(dve, at, link, kind):
            items = items_of(kind)
            scale = {"na": 1.0, "diff": 0.125, "mla": 96.0 ** -0.5}[kind]

            def maxima(i):
                g, t = items[i]
                dve.wait_ge(*at.plus("score", i + 1))
                b, n = 2 * (i % 2), keys_of(kind, t)
                if kind == "na":
                    link(dve.tensor_tensor(psum[:, b:b + 2, 0:S], psum[:, b:b + 2, 0:S],
                                           nb_bias[:, t, 2 * g:2 * g + 2, :], ALU.add))
                if kind == "mla":
                    link(dve.tensor_tensor(psum[:, b:b + 2, n - P:n], psum[:, b:b + 2, n - P:n],
                                           C2["chunk_mask"].unsqueeze(1).broadcast_to([P, 2, P]), ALU.add))
                a = 16 + b
                link(dve.tensor_reduce(cols[:, a:a + 2], psum[:, b:b + 2, 0:n], AX, ALU.max))
                dve.tensor_scalar(cols[:, a:a + 2], cols[:, a:a + 2], -scale, None, ALU.mult).then_inc(sems["neg_max"], 1)

            def normalise(i):
                dve.wait_ge(*at.plus("exps", i + 1))
                a = 20 + 2 * (i % 2)
                n = keys_of(kind, items[i][1])
                pr = pr_of(kind)[:, i % 2, :, :]
                link(dve.reciprocal(cols[:, a:a + 2], cols[:, a:a + 2]))
                if kind == "diff":
                    link(dve.tensor_scalar(cols[:, a + 1:a + 2], cols[:, a + 1:a + 2], cols[:, 10:11], None, ALU.mult))
                    link(dve.tensor_scalar(pr[:, 0, :], pr[:, 0, :], cols[:, a:a + 1], None, ALU.mult))
                    ins_ = dve.scalar_tensor_tensor(pr[:, 0, :], pr[:, 1, :], cols[:, a + 1:a + 2], pr[:, 0, :],
                                                    ALU.mult, ALU.add)
                else:
                    for m in range(2):
                        ins_ = dve.tensor_scalar(pr[:, m, 0:n], pr[:, m, 0:n], cols[:, a + m:a + m + 1], None, ALU.mult)
                ins_.then_inc(sems["probs"], 1)

            def outputs(g):
                dve.wait_ge(*at.plus("pv", g + 1))
                dst = oA[:, g, :] if kind == "diff" else mix_of(kind)[:, (6 if kind == "na" else 0) + g, :]
                dve.tensor_copy(dst, ps[6 + g % 2][:, 0:S]).then_inc(sems["pv_sb"], 1)

            maxima(0)
            for i in range(len(items)):
                if i + 1 < len(items):
                    maxima(i + 1)
                normalise(i)
                if items[i][1] == NT - 1 and items[i][0] >= 1:
                    outputs(items[i][0] - 1)
            outputs(items[-1][0])
            at("score", len(items)), at("exps", len(items)), at("pv", len(items) // 2)

        def out_projection_pe(pe, at, piece_ready, kind, mix):
            for j in range(2):
                slot = piece_ready((kind, j))
                w = ring[:, slot, 0:4 * D].rearrange("p (k n) -> p k n", k=4)
                for t in range(NT):
                    for n in range(2):
                        for k in range(4):
                            mm = pe.matmul(ps[2 * t + n], mix[:, 4 * j + k, P * t:P * t + P],
                                           w[:, k, 512 * n:512 * n + 512], start=(j == 0 and k == 0),
                                           stop=(j == 1 and k == 3))
                mm.then_inc(sems["out_mm"], 1)
                pe.wait_ge(*at("out_mm"))
                pe.sem_inc(sems["piece_used"], 1)

        def gate_diagonals_dve(dve, at, part):
            for k in range(KD):
                ins_ = dve.tensor_scalar(gate_diag[:, k, :], ident, modT[:, KD * part + k, 0:1], None, ALU.mult)
            ins_.then_inc(sems["diag"], 1)

        def gate_broadcast_pe(pe, at, bank):
            pe.wait_ge(*at("diag"))
            for n in range(2):
                mm = pe.matmul(ps[bank + n], ones, gate_diag[:, 4 * n:4 * n + 4, :].rearrange("p k n -> p (k n)"),
                               start=True, stop=True)
            mm.then_inc(sems["gate_bc"], 1)

        def residual_dve(dve, at, link, bank, gate_bank=None):
            if gate_bank is not None:
                dve.wait_ge(*at("gate_bc"))
                link(dve.tensor_copy(gate_sb, psum[:, gate_bank:gate_bank + 2, :].rearrange("p b n -> p (b n)")))
            for t in range(NT):
                src = psum[:, bank + 2 * t:bank + 2 * t + 2, :].rearrange("p b n -> p (b n)")
                if gate_bank is not None:
                    link(dve.tensor_tensor(res_tmp, src, gate_sb, ALU.mult))
                    src = res_tmp
                ins_ = dve.tensor_tensor(X[:, t, :], X[:, t, :], src, ALU.add)
                link(ins_)
            dve.sem_inc(sems["resid"], 1)

        def squares_act(act, at):
            act.wait_ge(*at("resid"))
            for t in range(NT):
                ins_ = act.activation(junk_of(t), X[:, t, :], ACT.Square, accum_out=ss[:, t:t + 1])
            ins_.then_inc(sems["sumsq"], 1)
            act.wait_ge(*at("sumsq"))
            act.wait_ge(*at("mean"))
            act.activation(rstd[:, 0:NT], ss[:, 0:NT], ACT.Sqrt).then_inc(sems["sqrt_done"], 1)

        def rstd_dve(dve, at, link):
            dve.wait_ge(*at("sumsq"))
            link(dve.tensor_scalar(ss[:, 0:NT], ss[:, 0:NT], 1.0 / D, EPS, ALU.mult, ALU.add))
            dve.reciprocal(ss[:, 0:NT], ss[:, 0:NT]).then_inc(sems["mean"], 1)
            dve.wait_ge(*at("sqrt_done"))

        def norm_dve(dve, at, link, scale, shift):
            rstd_dve(dve, at, link)
            for t in range(NT):
                dve.tensor_scalar(xn[:, t, :], X[:, t, :], rstd[:, t:t + 1], None, ALU.mult).then_inc(sems["xn"], 1)
            for b in range(2):
                dve.wait_ge(*at.plus("x_T", b + 1))
                for k in (2 * b, 2 * b + 1):
                    src = ps[4 + b][:, S * (k % 2):S * (k % 2) + S]
                    if shift is None:
                        ins_ = dve.tensor_scalar(h2T[:, k, :], src, scale[:, k:k + 1], None, ALU.mult)
                    else:
                        ins_ = dve.tensor_scalar(h2T[:, k, :], src, scale[:, k:k + 1], shift[:, k, 0:1], ALU.mult, ALU.add)
                ins_.then_inc(sems["xT_v"], 1)
            at("x_T", 4)

        def norm_act(act, at, scale, shift):
            squares_act(act, at)
            for b in range(2, 4):
                act.wait_ge(*at.plus("x_T", b + 1))
                for k in (2 * b, 2 * b + 1):
                    src = ps[4 + b][:, S * (k % 2):S * (k % 2) + S]
                    ins_ = act.activation(h2T[:, k, :], src, ACT.Identity, scale=scale[:, k:k + 1],
                                          bias=0.0 if shift is None else shift[:, k, 0:1])
                ins_.then_inc(sems["xT_s"], 1)
            at("x_T", 4)

        def norm_pe(pe, at):
            pe.wait_ge(*at("xn", 2))
            for b in range(4):
                for k in (2 * b, 2 * b + 1):
                    for t in range(NT):
                        o = S * (k % 2) + P * t
                        mm = pe.transpose(ps[4 + b][:, o:o + P], xn[:, t, P * k:P * k + P], ident)
                mm.then_inc(sems["x_T"], 1)
            pe.wait_ge(*at("xT_v", 2))
            pe.wait_ge(*at("xT_s", 2))

        def final_dve(dve, at, link):
            rstd_dve(dve, at, link)
            for t in range(NT):
                ins_ = dve.scalar_tensor_tensor(X[:, t, :], X[:, t, :], rstd[:, t:t + 1], final_g, ALU.mult, ALU.mult)
            link(ins_)
            dve.sem_inc(sems["resid"], 1)
            dve.sem_inc(sems["fin_x"], 1)

        def route_pe(pe, at, which):
            pe.wait_ge(*at("router_w", 48 if which == 1 else 64))
            for t in range(NT):
                for k in range(KD):
                    mm = pe.matmul(ps[0][:, 64 * t:64 * t + NG + NE], h2T[:, k, P * t:P * t + P], router_w[:, k, :],
                                   start=(k == 0), stop=(k == KD - 1))
            mm.then_inc(sems["logits"], 1)
            pe.wait_ge(*at("zero_tile"))
            for b in range(4, 8):
                pe.matmul(ps[b], zeros, xn[:, 0, 0:512], start=True, stop=True)
            pe.wait_ge(*at("route"))
            r = ps[1][:, 0:3 * NE].rearrange("p (n e) -> p n e", e=NE)
            pe.matmul(r[:, 0, :], tri, chosen[:, 0, :], start=True, stop=True)
            pe.matmul(r[:, 1, :], tri, chosen[:, 1, :], start=True, stop=False)
            pe.matmul(r[:, 1, :], ones, chosen[:, 0, :], start=False, stop=True)
            for t in range(NT):
                mm = pe.matmul(r[:, 2, :], ones, chosen[:, t, :], start=(t == 0), stop=(t == 1))
            mm.then_inc(sems["rank_mm"], 1)

        def route_act(act, at):
            act.wait_ge(*at("lg"))
            act.activation(r4[:, 1, :, :], r4[:, 1, :, :], ACT.Exp).then_inc(sems["lg_exp"], 1)
            act.wait_ge(*at("lg"))
            act.activation(r1[:, 6, :], r1[:, 6, :], ACT.Exp).then_inc(sems["lg_exp"], 1)

        def route_dve(dve, at, link, which):
            spread = lambda x, n: x.unsqueeze(2).broadcast_to([P, NT, n])

            def first_of(x, n, top, mark, where):
                link(dve.tensor_reduce(top, x, AX, ALU.max))
                link(dve.tensor_tensor(where, x, spread(top, n), ALU.is_equal))
                link(dve.scalar_tensor_tensor(where, where, -16.0, iota_of(n), ALU.mult, ALU.add))
                link(dve.tensor_reduce(mark, where, AX, ALU.min))
                link(dve.tensor_tensor(where, where, spread(mark, n), ALU.is_equal))

            def iota_of(n):
                return C0["iota8"][:, 0:n].unsqueeze(1).broadcast_to([P, NT, n])

            dve.wait_ge(*at("logits"))
            src = ps[0][:, 0:128].rearrange("p (t n) -> p t n", t=NT)[:, :, 0:NG + NE]
            link(dve.tensor_tensor(lg[:, :, 0:NG + NE], src, router_b.unsqueeze(1).broadcast_to([P, NT, NG + NE]), ALU.add))
            groups = lg[:, :, 0:NG]
            first_of(groups, NG, r1[:, 0, :], r1[:, 1, :], r4[:, 0, :, :])
            dve.tensor_tensor(r4[:, 1, :, :], groups, spread(r1[:, 0, :], NG), ALU.subtract).then_inc(sems["lg"], 1)
            for t in range(NT):
                e3 = lg[:, t, NG:NG + NE].rearrange("p (g e) -> p g e", g=NG)
                dve.tensor_tensor(r32[:, t, :].rearrange("p (g e) -> p g e", g=NG), e3,
                                  r4[:, 0, t, :].unsqueeze(2).broadcast_to([P, NG, EG]), ALU.mult)
            dve.wait_ge(*at("lg"))
            dve.wait_ge(*at("lg_exp"))
            link(dve.tensor_reduce(r1[:, 2, :], r4[:, 1, :, :], AX, ALU.add))
            link(dve.reciprocal(r1[:, 2, :], r1[:, 2, :]))
            for t in range(NT):
                ins_ = dve.tensor_reduce(r8[:, 0, t, :], r32[:, t, :].rearrange("p (g e) -> p e g", g=NG), AX, ALU.add)
            link(ins_)
            first_of(r8[:, 0, :, :], EG, r1[:, 3, :], r1[:, 4, :], r8[:, 1, :, :])
            link(dve.scalar_tensor_tensor(r8[:, 2, :, :], r8[:, 1, :, :], -BIG, r8[:, 0, :, :], ALU.mult, ALU.add))
            first_of(r8[:, 2, :, :], EG, r1[:, 5, :], r1[:, 4, :], r8[:, 3, :, :])
            dve.tensor_tensor(r1[:, 6, :], r1[:, 5, :], r1[:, 3, :], ALU.subtract).then_inc(sems["lg"], 1)
            dve.wait_ge(*at("lg"))
            dve.wait_ge(*at("lg_exp"))
            link(dve.tensor_scalar(r1[:, 7, :], r1[:, 6, :], 1.0, None, ALU.add))
            link(dve.reciprocal(r1[:, 7, :], r1[:, 7, :]))
            link(dve.tensor_tensor(r1[:, 7, :], r1[:, 7, :], r1[:, 2, :], ALU.mult))
            link(dve.tensor_tensor(r1[:, 8, :], r1[:, 7, :], r1[:, 6, :], ALU.mult))
            link(dve.tensor_tensor(r8[:, 4, :, :], r8[:, 1, :, :], r8[:, 3, :, :], ALU.add))
            link(dve.tensor_tensor(r8[:, 5, :, :], r8[:, 1, :, :], spread(r1[:, 7, :], EG), ALU.mult))
            link(dve.tensor_tensor(r8[:, 6, :, :], r8[:, 3, :, :], spread(r1[:, 8, :], EG), ALU.mult))
            link(dve.tensor_tensor(r8[:, 5, :, :], r8[:, 5, :, :], r8[:, 6, :, :], ALU.add))
            for t in range(NT):
                g3 = r4[:, 0, t, :].unsqueeze(2).broadcast_to([P, NG, EG])
                for dst, src in ((chosen[:, t, :], r8[:, 4, t, :]), (ranks[:, NT + t, :], r8[:, 5, t, :])):
                    ins_ = dve.tensor_tensor(dst.rearrange("p (g e) -> p g e", g=NG), g3,
                                             src.unsqueeze(1).broadcast_to([P, NG, EG]), ALU.mult)
            ins_.then_inc(sems["route"], 1)
            dve.wait_ge(*at("route"))
            dve.wait_ge(*at("rank_mm"))
            r = ps[1][:, 0:3 * NE].rearrange("p (n e) -> p n e", e=NE)
            link(dve.scalar_tensor_tensor(ranks[:, 0:NT, :], r[:, 0:NT, :], 1.0, chosen, ALU.add, ALU.mult))
            link(dve.tensor_scalar(ranks[:, 0:NT, :], ranks[:, 0:NT, :], -1.0, None, ALU.add))
            nb, w, _ = batch_of(which)
            link(dve.tensor_scalar(extra_f, r[0:1, 2, :], 1.0 / w, None, ALU.mult))
            link(dve.tensor_tensor(extra_cmp, extra_f.unsqueeze(2).broadcast_to([1, NE, 8]),
                                   C0["step"][0:1, :].unsqueeze(1).broadcast_to([1, NE, 8]), ALU.is_gt))
            link(dve.tensor_reduce(extra_f, extra_cmp, AX, ALU.add))
            link(dve.tensor_reduce(extra_m[:, 0:NE // nb], extra_f.rearrange("p (b e) -> p b e", e=nb), AX, ALU.max))
            link(dve.tensor_copy(extra[:, 0:NE // nb], extra_m[:, 0:NE // nb]))
            dve.sem_inc(sems["ranked"], 1)

        def batch_of(which):
            return (2, P // 2, 512) if which == 1 else (4, P // 4, 256)

        def each_batch(eng, at, which, round_, before=None):
            nb = batch_of(which)[0]
            eng.wait_ge(*at("ranked"))
            with eng.Fori(0, NE // nb) as turn:
                if before:
                    before(turn)
                n = eng.value_load(extra[0:1, bass.ds(turn, 1)], min_val=0, max_val=7)
                with eng.If(n > 0):
                    with eng.Fori(0, n):
                        round_(turn, False)
                round_(turn, True)

        def piece_view(slot, which, down):
            nb = batch_of(which)[0]
            v = ring[:, slot, :]
            if down:
                return v.rearrange("p (e k n) -> p e k n", e=nb, n=D)
            if which == 1:
                return v.rearrange("p (e k n) -> p e k n", e=nb, k=2)
            return v.rearrange("p (u e k n) -> p u e k n", u=2, e=nb, k=2)

        def experts_pe(pe, at, plan, which):
            route_pe(pe, at, which)
            win = windows["pe"]
            nb, w, hidden = batch_of(which)
            slots = plan.loop(NE // nb, RING, 2 if which == 1 else 4, hidden // P // 2)

            def round_(turn, last):
                pe.reg_add(win, win, 1)
                v = pe.snap(win)
                pe.wait_ge(sems["w_sel"], v)
                for n in range(2):
                    for t in range(NT):
                        mm = pe.matmul(ps[n], sel[:, t, :], xn[:, t, 512 * n:512 * n + 512],
                                       start=(t == 0), stop=(t == NT - 1))
                    mm.then_inc(sems["w_gath"], 1)
                pe.wait_ge(sems["w_selg"], v)
                for t in range(NT):
                    mm = pe.transpose(ps[2][:, P * t:P * t + P], sel_gate[:, t, :], ident)
                mm.then_inc(sems["w_ct"], 1)
                for half in range(2):
                    pe.wait_ge(sems["w_got_s" if half == 0 else "w_got_v"], v)
                    for k in range(4):
                        mm = pe.transpose(ps[3 if half == 0 else 0][:, P * k:P * k + P],
                                          got[:, 512 * half + P * k:512 * half + P * k + P], ident)
                    mm.then_inc(sems["w_gt0" if half == 0 else "w_gt1"], 1)
                pe.wait_ge(sems["w_csb"], v)
                for i, (slot, sem, base, step) in enumerate(slots[0:4]):
                    if i % 2 == 0:
                        pe.wait_ge(sems["w_xg_v" if i == 0 else "w_xg_s"], v)
                    pe.wait_ge(sem, turn * step + (base + step))
                    view = piece_view(slot, which, False)
                    for kk in range(2):
                        k = 2 * i + kk
                        for n in range(2 if which == 1 else 1):
                            for e in range(nb):
                                out_ = ps[1 + n][w * e:w * e + w, :]
                                if which == 1:
                                    rhs = view[:, e, kk, 512 * n:512 * n + 512]
                                else:
                                    rhs = view[:, :, e, kk, :]
                                    out_ = out_.rearrange("p (u n) -> p u n", u=2)
                                mm = pe.matmul(out_, gotT[:, k, w * e:w * e + w], rhs, start=(k == 0), stop=(k == KD - 1))
                    if i < 3:
                        if last:
                            mm.then_inc(sems["piece_used"], 1)
                    else:
                        mm.then_inc(sems["w_up"], 1)
                pe.wait_ge(sems["w_hid"], v)
                for c in range(hidden // P):
                    mm = pe.transpose(ps[3][:, P * c:P * c + P], hid[:, P * c:P * c + P], ident)
                mm.then_inc(sems["w_ht"], 1)
                if last:
                    pe.sem_inc(sems["piece_used"], 1)
                pe.wait_ge(sems["w_hsb"], v)
                chunks = hidden // P
                for i, (slot, sem, base, step) in enumerate(slots[4:6]):
                    pe.wait_ge(sem, turn * step + (base + step))
                    view = piece_view(slot, which, True)
                    per = chunks // 2
                    for kk in range(per):
                        k = per * i + kk
                        for n in range(2):
                            for e in range(nb):
                                mm = pe.matmul(ps[n][w * e:w * e + w, :], hidT[:, k, w * e:w * e + w],
                                               view[:, e, kk, 512 * n:512 * n + 512], start=(k == 0), stop=(k == chunks - 1))
                    if i == 0:
                        if last:
                            mm.then_inc(sems["piece_used"], 1)
                    else:
                        mm.then_inc(sems["w_y"], 1)
                for n in range(2):
                    pe.wait_ge(sems["w_ysb_s" if n == 0 else "w_ysb_v"], v)
                    if n == 0 and last:
                        pe.sem_inc(sems["piece_used"], 1)
                    for t in range(NT):
                        mm = pe.matmul(ps[4 + 2 * t + n], comb[:, P * t:P * t + P], y_sb[:, 512 * n:512 * n + 512],
                                       start=False, stop=True, skip_group_check=True)
                mm.then_inc(sems["w_comb"], 1)

            each_batch(pe, at, which, round_)
            pe.wait_ge(sems["w_comb"], pe.snap(win))
            pe.sem_inc(sems["moe_mm"], 1)

        def experts_act(act, at, which, scale, shift):
            route_act(act, at)
            win = windows["act"]
            hidden = batch_of(which)[2]

            def round_(turn, last):
                act.reg_add(win, win, 1)
                v = act.snap(win)
                act.wait_ge(sems["w_ct"], v)
                act.activation(got[:, 0:512], ps[0], ACT.Copy).then_inc(sems["w_got_s"], 1)
                act.wait_ge(sems["w_gt1"], v)
                for k in range(4, KD):
                    ins_ = act.activation(gotT[:, k, :], ps[0][:, P * (k - 4):P * (k - 4) + P], ACT.Identity,
                                          scale=scale[:, k:k + 1], bias=0.0 if shift is None else shift[:, k, 0:1])
                ins_.then_inc(sems["w_xg_s"], 1)
                act.wait_ge(sems["w_up"], v)
                act.activation(silu_sb[:, 0:hidden], ps[1][:, 0:hidden], ACT.Silu).then_inc(sems["w_silu"], 1)
                act.wait_ge(sems["w_ht"], v)
                act.activation(hidT.rearrange("p c n -> p (c n)")[:, 0:hidden], ps[3][:, 0:hidden], ACT.Copy)\
                    .then_inc(sems["w_hsb"], 1)
                act.wait_ge(sems["w_y"], v)
                act.activation(y_sb[:, 0:512], ps[0], ACT.Copy).then_inc(sems["w_ysb_s"], 1)

            each_batch(act, at, which, round_)

        def experts_dve(dve, at, link, which, scale, shift):
            win, currents = windows["dve"], windows["cur"]
            nb, w, hidden = batch_of(which)
            scale4 = scale[:, 0:4].unsqueeze(2).broadcast_to([P, 4, P])
            if shift is not None:
                shift4 = shift[:, 0:4, 0].unsqueeze(2).broadcast_to([P, 4, P])
            now = cur[:, 0:4 * nb].rearrange("p (r e) -> p r e", e=nb)
            slot_ids = C0["slot64" if which == 1 else "slot32"].rearrange("p (e s) -> p e s", e=nb)

            def current(ins_):
                ins_.then_inc(sems["w_cur"], 1)
                dve.reg_add(currents, currents, 1)
                dve.wait_ge(sems["w_cur"], dve.snap(currents))

            def round_(turn, last):
                dve.reg_add(win, win, 1)
                v = dve.snap(win)
                if last:
                    current(dve.tensor_copy(now, ranks[:, :, bass.ds(turn * nb, nb)]))
                else:
                    current(dve.tensor_scalar(now[:, 0:NT, :], now[:, 0:NT, :], -float(w), None, ALU.add))
                for t in range(NT):
                    s3 = sel[:, t, :].rearrange("p (e s) -> p e s", e=nb)
                    ins_ = dve.tensor_tensor(s3, slot_ids, now[:, t, :].unsqueeze(2).broadcast_to([P, nb, w]), ALU.is_equal)
                ins_.then_inc(sems["w_sel"], 1)
                dve.wait_ge(sems["w_sel"], v)
                for t in range(NT):
                    s3 = sel[:, t, :].rearrange("p (e s) -> p e s", e=nb)
                    g3 = sel_gate[:, t, :].rearrange("p (e s) -> p e s", e=nb)
                    ins_ = dve.tensor_tensor(g3, s3, now[:, NT + t, :].unsqueeze(2).broadcast_to([P, nb, w]), ALU.mult)
                ins_.then_inc(sems["w_selg"], 1)
                dve.wait_ge(sems["w_ct"], v)
                dve.tensor_copy(got[:, 512:1024], ps[1]).then_inc(sems["w_got_v"], 1)
                dve.tensor_copy(comb, ps[2][:, 0:S]).then_inc(sems["w_csb"], 1)
                dve.wait_ge(sems["w_gt0"], v)
                dst, src = gotT[:, 0:4, :], ps[3].rearrange("p (k n) -> p k n", k=4)
                if shift is None:
                    dve.tensor_tensor(dst, src, scale4, ALU.mult).then_inc(sems["w_xg_v"], 1)
                else:
                    dve.tensor_tensor(dst, src, scale4, ALU.mult).then_inc(sems["w_xm"], 1)
                    dve.wait_ge(sems["w_xm"], v)
                    dve.tensor_tensor(dst, dst, shift4, ALU.add).then_inc(sems["w_xg_v"], 1)
                dve.wait_ge(sems["w_silu"], v)
                up_ = ps[2] if which == 1 else ps[1][:, hidden:2 * hidden]
                dve.tensor_tensor(hid[:, 0:hidden], silu_sb[:, 0:hidden], up_, ALU.mult).then_inc(sems["w_hid"], 1)
                dve.wait_ge(sems["w_y"], v)
                dve.tensor_copy(y_sb[:, 512:1024], ps[1]).then_inc(sems["w_ysb_v"], 1)

            def begin(turn):
                current(dve.tensor_copy(now, ranks[:, :, bass.ds(turn * nb, nb)]))

            each_batch(dve, at, which, round_, begin)
            dve.wait_ge(*at("moe_mm"))


        def emptied_before(at_engine, unit):
            if unit >= 4:
                who = UNITS[unit - 4][4]
                at_engine.wait_ge(sems["unit_" + who], emptied(UNITS, unit - 3, who))

        score_items = [(h, t) for h in range(4) for t in range(NT)]
        pair_items = [(h, t) for h in range(2) for t in range(NT)]

        def context_values(pe, at, h):
            pe.wait_ge(*at("c_sb"))
            o = ps[7][64 * (h % 2):64 * (h % 2) + 64, S * (h // 2):S * (h // 2) + S]
            for s in range(2):
                mm = pe.matmul(o, vbn[:, NT + s, 64 * h:64 * h + 64], ctT[:, h % 2, s, :],
                               start=(s == 0 and h < 2), stop=False, skip_group_check=True)
            mm.then_inc(sems["c_used"], 1)

        def diagonal(rows_, h, off):
            base = atT[rows_, h, :, :]
            return bass.AP(tensor=base.tensor, offset=base.offset + off, ap=[base.ap[0], (S + P, 2), (1, 32)])

        def second_block_loads(sp, plan, straight):
            for layer in range(2):
                straight(second_pieces, layer)
                gate, up, down = (ins[n][layer].rearrange("g (b e) (k p) n -> (g b) p e k n", p=P, e=4)
                                  for n in ("w_gate_2", "w_up_2", "w_down_2"))
                expert_loads(sp, plan, 2, (gate, up), down)

        def second_block_pool(pool, at):
            pool.wait_ge(*at("fin_x"))
            pool.dma_start(const2, ins["const2"]).then_inc(sems["const2"], 16)
            for layer in range(2):
                for m in range(2):
                    pool.dma_start(pool_w[64 * m:64 * m + 64, :, :], ins["pool_w_2"][layer]
                                   .rearrange("(c m) k n -> m k c n", m=2)[m]).then_inc(sems["pool_w"], 16)
                pool.wait_ge(*at("mixed"))
                for name, dst in (("w_group_2", router_w[:, :, 0:NG]), ("w_expert_2", router_w[:, :, NG:])):
                    pool.dma_start(dst, ins[name][layer].rearrange("(k p) n -> p k n", p=P)).then_inc(sems["router_w"], 16)
                for name, dst in (("b_group_2", router_b[:, 0:NG]), ("b_expert_2", router_b[:, NG:])):
                    pool.dma_start(dst, ins[name][layer:layer + 1, :].to_broadcast([P, dst.shape[1]]))\
                        .then_inc(sems["router_w"], 16)
                pool.memset(zeros, 0.0).then_inc(sems["zero_tile"], 1)
            pool.dma_start(final_g, ins["final_g_2"].rearrange("(o n) -> o n", o=1).to_broadcast([P, D]))\
                .then_inc(sems["final_gain"], 16)
            pool.wait_ge(*at("fin_x"))
            pool.dma_start(out[0].rearrange("(t p) d -> p t d", p=P), X).then_inc(sems["written"], 16)
            pool.wait_ge(sems["written"], 16)

        def second_block_pe(pe, at, plan, piece_ready):
            for layer in range(2):
                norm_pe(pe, at)
                slot = piece_ready(("win2", 0))
                w = w_cols(slot, WIN2_WIDTH[0])
                for t in range(NT):
                    for k in range(KD):
                        mm = pe.matmul(ps[t][:, 0:416], h2T[:, k, P * t:P * t + P], w[:, k, 0:416],
                                       start=(k == 0), stop=(k == KD - 1))
                    mm.then_inc(sems["p2_mm"], 1)
                pe.wait_ge(*at("p2_mm", 2))
                pe.sem_inc(sems["piece_used"], 1)
                slot = piece_ready(("win2", 1))
                w = w_cols(slot, WIN2_WIDTH[1])
                for part in range(2):
                    for t in range(NT):
                        for k in range(KD):
                            mm = pe.matmul(ps[2 + 3 * part][:, S * t:S * t + S], h2T[:, k, P * t:P * t + P],
                                           w[:, k, S * part:S * part + S], start=(k == 0), stop=(k == KD - 1))
                    mm.then_inc(sems["p2_mm"], 1)
                pe.wait_ge(*at("p2_mm", 2))
                pe.sem_inc(sems["piece_used"], 1)
                slot = piece_ready(("win2", 2))
                w = w_cols(slot, WIN2_WIDTH[2])
                for part in range(2):
                    for c in range(2):
                        for k in range(KD):
                            col = 256 * part + P * c
                            mm = pe.matmul(ps[3 + part][:, S * c:S * c + S], w[:, k, col:col + P], h2T[:, k, :],
                                           start=(k == 0), stop=(k == KD - 1))
                    mm.then_inc(sems["p2_mm"], 1)
                pe.wait_ge(*at("p2_mm", 2))
                pe.sem_inc(sems["piece_used"], 1)
                pe.wait_ge(*at("p2_v", 3))
                pe.wait_ge(*at("p2_s", 3))
                if layer == 0:
                    pe.wait_ge(sems["const2"], 16)
                for g in range(4):
                    for s in range(NT):
                        mm = pe.matmul(ps[6][64 * (g % 2):64 * (g % 2) + 64, S * (g // 2):S * (g // 2) + S],
                                       pool_u[:, s, 64 * g:64 * g + 64], pool_mat[:, g, s, :],
                                       start=(s == 0), stop=(s == 1))
                mm.then_inc(sems["pool_d"], 1)
                for t in range(NT):
                    for m in range(2):
                        for hp in range(2):
                            n = P * (t + 1)
                            r = slice(64 * m, 64 * m + 64)
                            mm = pe.matmul(ps[2 * t + m][:, n * hp:n * hp + n], bqT[r, hp, P * t:P * t + P],
                                           bkT[r, hp, 0:n], start=True, stop=True)
                mm.then_inc(sems["st_mm"], 1)
                pe.wait_ge(*at("cq_n"))
                for t in range(NT):
                    for c in range(3):
                        mm = pe.transpose(ps[4 + t][:, P * c:P * c + P], cq[:, t, P * c:P * c + P], ident)
                mm.then_inc(sems["cq_T"], 1)
                pe.wait_ge(*at("pool_ds"))
                pe.wait_ge(*at("pool_w", 32))
                for g in range(4):
                    r = slice(64 * (g % 2), 64 * (g % 2) + 64)
                    mm = pe.matmul(ps[7][r, S * (g // 2):S * (g // 2) + S], pool_w[r, g // 2, :], pool_dT[r, g // 2, :],
                                   start=True, stop=True)
                mm.then_inc(sems["pool_y"], 1)
                pe.wait_ge(*at("st_a"))
                for b, (t, c) in enumerate(((0, 0), (1, 0), (1, 1))):
                    for h in range(4):
                        mm = pe.transpose(ps[b][:, P * h:P * h + P], st_block(st_e, h, t)[:, P * c:P * c + P], ident)
                mm.then_inc(sems["st_T"], 1)
                pe.wait_ge(*at("st_Ts"))
                for h in range(4):
                    m, hp = h % 2, h // 2
                    o = ps[6][64 * m:64 * m + 64, S * hp:S * hp + S]
                    pe.matmul(o, bv[:, 0, 64 * h:64 * h + 64], st_pT[:, h, 0, :], start=True, stop=False,
                              skip_group_check=True)
                    mm = pe.matmul(o[:, P:S], bv[:, 1, 64 * h:64 * h + 64], st_pT[:, h, 1, P:S], start=False, stop=True,
                                   skip_group_check=True)
                mm.then_inc(sems["st_pv"], 1)
                pe.wait_ge(*at("st_o"))
                pe.wait_ge(*at("pool_o"))
                pe.wait_ge(*at("cq_Ts"))
                slot = piece_ready(("mla", 0))
                uq = ring[:, slot, 0:1536].rearrange("p (k n) -> p k n", k=2)
                ukv = ring[:, slot, 1536:2560]
                for t in range(NT):
                    for b, (a, n) in enumerate(((0, 512), (512, 256))):
                        for k in range(2):
                            mm = pe.matmul(ps[4 * t + b][:, 0:n], cqT[:, k, P * t:P * t + P], uq[:, k, a:a + n],
                                           start=(k == 0), stop=(k == 1))
                    mm.then_inc(sems["q_mm"], 1)
                    for b in range(2):
                        mm = pe.matmul(ps[4 * t + 2 + b], cqT[:, 2, P * t:P * t + P], ukv[:, 512 * b:512 * b + 512],
                                       start=True, stop=True)
                    mm.then_inc(sems["kv_mm"], 1)
                pe.wait_ge(*at("kv_mm", 2))
                pe.sem_inc(sems["piece_used"], 1)
                for t in range(NT):
                    pe.wait_ge(*at("q_sb"))
                    pe.wait_ge(*at("kv_sb"))
                    for b in range(4):
                        src = q_tok if b < 2 else k_tok
                        for h in range(4):
                            mm = pe.transpose(ps[4 * t + b][0:96, P * h:P * h + P], src[:, t, 4 * (b % 2) + h, :], ident)
                        mm.then_inc(sems["head_T"], 1)
                pe.wait_ge(*at("head_v", 4))
                pe.wait_ge(*at("head_s", 4))
                attention_pe(pe, at, "mla")
                out_projection_pe(pe, at, piece_ready, "wout2", mixT)
                norm_pe(pe, at)
                experts_pe(pe, at, plan, 2)

        def st_block(x, h, t):
            o = (P * (h // 2)) if t == 0 else (2 * P + S * (h // 2))
            return x[:, h % 2, o:o + P * (t + 1)]

        def second_block_act(act, at, link):
            for layer in range(2):
                norm_act(act, at, PT["norm1_g_2"][:, KD * layer:KD * layer + KD], None)
                for t in range(NT):
                    act.wait_ge(*at("p2_mm"))
                    act.activation(cq[:, t, :], ps[t][:, 0:416], ACT.Copy).then_inc(sems["p2_s"], 1)
                act.wait_ge(*at("p2_s", 2))
                for t in range(NT):
                    link(act.activation(junk[:, 0:256], cq[:, t, 0:256], ACT.Square, accum_out=cols[:, 32 + t:33 + t]))
                    link(act.activation(junk[:, 0:128], cq[:, t, 256:384], ACT.Square, accum_out=cols[:, 34 + t:35 + t]))
                act.sem_inc(sems["cq_sq"], 1)
                act.wait_ge(*at("p2_mm", 3))
                act.activation(bqT.rearrange("p h n -> p (h n)"), ps[3], ACT.Copy, scale=0.125).then_inc(sems["p2_s"], 1)
                act.wait_ge(*at("p2_s"))
                act.wait_ge(*at("cq_mean"))
                act.activation(cols[:, 32:36], cols[:, 32:36], ACT.Sqrt).then_inc(sems["cq_sqrt"], 1)
                act.wait_ge(*at("pool_d"))
                act.activation(pool_dT.rearrange("p c n -> p (c n)"), ps[6], ACT.Copy).then_inc(sems["pool_ds"], 1)
                act.wait_ge(*at("st_zb"))
                link(act.activation(st_e, st_e, ACT.Exp))
                act.activation(st_e, st_e, ACT.Ln, bias=1.0).then_inc(sems["st_ln"], 1)
                act.wait_ge(*at("st_x"))
                act.activation(st_e, st_z, ACT.Exp).then_inc(sems["st_a"], 1)
                act.wait_ge(*at("st_T"))
                for b, (t, c) in enumerate(((0, 0), (1, 0), (1, 1))):
                    ins_ = act.activation(st_pT[:, :, c, P * t:P * t + P], ps[b].rearrange("p (h n) -> p h n", h=4), ACT.Copy)
                ins_.then_inc(sems["st_Ts"], 1)
                for t in range(NT):
                    act.wait_ge(*at("kv_mm"))
                    kv = psum[:, 4 * t + 2:4 * t + 4, :].rearrange("p b n -> p (b n)").rearrange("p (h u n) -> p h u n", h=8, u=2)
                    act.activation(k_tok[:, t, :, 0:64], kv[:, :, 0, :], ACT.Copy)
                    act.activation(v2[:, t, :, :], kv[:, :, 1, :], ACT.Copy).then_inc(sems["kv_sb"], 1)
                for t in range(NT):
                    for b in range(2):
                        act.wait_ge(*at.plus("head_T", 4 * t + b + 1))
                        act.activation(q2T[0:96, 4 * b:4 * b + 4, P * t:P * t + P],
                                       ps[4 * t + b][0:96, :].rearrange("p (h n) -> p h n", h=4), ACT.Copy)\
                            .then_inc(sems["head_s"], 1)
                at("head_T", 8), at("p2_mm", 1)
                attention_act(act, at, "mla")
                norm_act(act, at, PT["norm2_g_2"][:, KD * layer:KD * layer + KD], None)
                experts_act(act, at, 2, PT["norm2_g_2"][:, KD * layer:KD * layer + KD], None)
            squares_act(act, at)

        def second_block_dve(dve, at, link):
            for layer in range(2):
                norm_dve(dve, at, link, PT["norm1_g_2"][:, KD * layer:KD * layer + KD], None)
                dve.wait_ge(*at("p2_mm", 3))
                dve.tensor_copy(pool_u.rearrange("p t n -> p (t n)"), ps[2]).then_inc(sems["p2_v"], 1)
                dve.wait_ge(*at("cq_sq"))
                link(dve.tensor_scalar(cols[:, 32:34], cols[:, 32:34], 1.0 / 256, EPS, ALU.mult, ALU.add))
                link(dve.tensor_scalar(cols[:, 34:36], cols[:, 34:36], 1.0 / 128, EPS, ALU.mult, ALU.add))
                dve.reciprocal(cols[:, 32:36], cols[:, 32:36]).then_inc(sems["cq_mean"], 1)
                dve.wait_ge(*at("p2_mm"))
                dve.tensor_copy(bv.rearrange("p t n -> p (t n)"), ps[5]).then_inc(sems["p2_v"], 1)
                dve.wait_ge(*at("p2_mm", 2))
                dve.tensor_copy(bkT.rearrange("p h n -> p (h n)"), ps[4]).then_inc(sems["p2_v"], 1)
                dve.wait_ge(*at("cq_sqrt"))
                if layer == 0:
                    dve.wait_ge(sems["const2"], 16)
                for t in range(NT):
                    dve.tensor_scalar(cq[:, t, 0:256], cq[:, t, 0:256], cols[:, 32 + t:33 + t], None, ALU.mult)
                    ins_ = dve.tensor_scalar(cq[:, t, 256:384], cq[:, t, 256:384], cols[:, 34 + t:35 + t], None, ALU.mult)
                ins_.then_inc(sems["cq_n"], 1)
                dve.wait_ge(*at("p2_v", 3))
                for t in range(NT):
                    cos = C2["rope_cos"][:, 32 * t:32 * t + 32]
                    sin = C2["rope_sin"][:, 32 * t:32 * t + 32]
                    kr = cq[:, t, 384:416]
                    for b in range(2):
                        dve.tensor_tensor(rot2b[:, t, 16 * b:16 * b + 16], kr[:, 16 - 16 * b:32 - 16 * b],
                                          sin[:, 16 * b:16 * b + 16], ALU.mult)
                    link(dve.tensor_tensor(rot2a[:, t, :], kr, cos, ALU.mult))
                    link(dve.tensor_tensor(key_rot[:, t, :], rot2a[:, t, :], rot2b[:, t, :], ALU.add))
                dve.wait_ge(*at("st_mm"))
                mask = C2["strict_mask"].unsqueeze(1).broadcast_to([P, 2, P])
                for m in range(2):
                    z0 = st_z[:, m, 0:2 * P].rearrange("p (h n) -> p h n", h=2)
                    z1 = st_z[:, m, 2 * P:].rearrange("p (h n) -> p h n", h=2)
                    p1 = ps[2 + m].rearrange("p (h n) -> p h n", h=2)
                    dve.tensor_tensor(z0, ps[m][:, 0:2 * P].rearrange("p (h n) -> p h n", h=2), mask, ALU.add)
                    dve.tensor_copy(z1[:, :, 0:P], p1[:, :, 0:P])
                    ins_ = dve.tensor_tensor(z1[:, :, P:2 * P], p1[:, :, P:2 * P], mask, ALU.add)
                link(ins_)
                dve.scalar_tensor_tensor(st_e, st_z, -1.0, st_z, ALU.mult, ALU.min).then_inc(sems["st_zb"], 1)
                dve.wait_ge(*at("cq_T"))
                for t in range(NT):
                    for c in range(3):
                        g = PT["q_norm_g_2"][:, 2 * layer + c:2 * layer + c + 1] if c < 2 else PT["kv_norm_g_2"][:, layer:layer + 1]
                        ins_ = dve.tensor_scalar(cqT[:, c, P * t:P * t + P], ps[4 + t][:, P * c:P * c + P], g, None, ALU.mult)
                ins_.then_inc(sems["cq_Ts"], 1)
                dve.wait_ge(*at("st_ln"))
                link(dve.scalar_tensor_tensor(st_e, st_z, 0.0, st_e, ALU.max, ALU.add))
                for t in range(NT):
                    for h in range(4):
                        n = P * (t + 1)
                        ins_ = dve.tensor_tensor_scan(st_block(st_s, h, t)[:, ::-1], ones[:, 0:1].broadcast_to([P, n]),
                                                      st_block(st_e, h, t)[:, ::-1], 0.0, ALU.mult, ALU.add)
                link(ins_)
                dve.tensor_tensor(st_z, st_z, st_s, ALU.subtract).then_inc(sems["st_x"], 1)
                dve.wait_ge(*at("pool_y"))
                for c in range(2):
                    ins_ = dve.tensor_scalar(mixT[:, 6 + c, :], ps[7][:, S * c:S * c + S],
                                             PT["pool_scale_2"][:, 2 * layer + c:2 * layer + c + 1], None, ALU.mult)
                ins_.then_inc(sems["pool_o"], 1)
                dve.wait_ge(*at("st_pv"))
                dve.tensor_copy(mixT[:, 4:6, :].rearrange("p c n -> p (c n)"), ps[6]).then_inc(sems["st_o"], 1)
                for t in range(NT):
                    dve.wait_ge(*at("q_mm"))
                    q = psum[:, 4 * t:4 * t + 2, :].rearrange("p b n -> p (b n)")[:, 0:768].rearrange("p (h n) -> p h n", h=8)
                    cos = C2["rope_cos"][:, 32 * t:32 * t + 32].unsqueeze(1).broadcast_to([P, 8, 32])
                    sin = C2["rope_sin"][:, 32 * t:32 * t + 32]
                    dve.tensor_copy(q_tok[:, t, :, 0:64], q[:, :, 0:64])
                    for b in range(2):
                        dve.tensor_tensor(rot2b[:, :, 16 * b:16 * b + 16], q[:, :, 80 - 16 * b:96 - 16 * b],
                                          sin[:, 16 * b:16 * b + 16].unsqueeze(1).broadcast_to([P, 8, 16]), ALU.mult)
                    dve.tensor_copy(k_tok[:, t, :, 64:96], key_rot[:, t, :].unsqueeze(1).broadcast_to([P, 8, 32]))
                    link(dve.tensor_tensor(rot2a, q[:, :, 64:96], cos, ALU.mult))
                    dve.tensor_tensor(q_tok[:, t, :, 64:96], rot2a, rot2b, ALU.add).then_inc(sems["q_sb"], 1)
                    dve.wait_ge(*at("q_sb"))
                for t in range(NT):
                    for b in range(2):
                        dve.wait_ge(*at.plus("head_T", 4 * t + 2 + b + 1))
                        dve.tensor_copy(k2T[0:96, 4 * b:4 * b + 4, P * t:P * t + P],
                                        ps[4 * t + 2 + b][0:96, :].rearrange("p (h n) -> p h n", h=4))\
                            .then_inc(sems["head_v"], 1)
                at("head_T", 8)
                attention_dve(dve, at, link, "mla")
                dve.sem_inc(sems["mixed"], 1)
                dve.wait_ge(*at("out_mm", 2))
                residual_dve(dve, at, link, 0)
                norm_dve(dve, at, link, PT["norm2_g_2"][:, KD * layer:KD * layer + KD], None)
                dve.wait_ge(*at("router_w", 64))
                route_dve(dve, at, link, 2)
                experts_dve(dve, at, link, 2, PT["norm2_g_2"][:, KD * layer:KD * layer + KD], None)
                residual_dve(dve, at, link, 4)
            dve.wait_ge(sems["final_gain"], 16)
            final_dve(dve, at, link)

        @block.sync
        def _(sp):
            plan = Ring(sems)

            def straight(pieces, layer):
                for piece in pieces:
                    if plan.n >= RING:
                        sp.wait_ge(sems["piece_used"], plan.n - RING + 1)
                    slot, sem, _ = plan.place(dmas_of(piece))
                    start_piece(sp, slot, sem, piece, layer)

            sp.dma_start(X, ins["x"][0].rearrange("(t p) d -> p t d", p=P)).then_inc(sems["loaded_x"], 16)
            straight(first_pieces, 0)
            expert_loads(sp, plan, 1, (up1,), down1)
            second_block_loads(sp, plan, straight)

        @block.gpsimd
        def _(pool):
            at = Tally(sems)
            pool.memset(cT, 0.0).then_inc(sems["zero_done"], 1)
            pool.memset(band, 0.0).then_inc(sems["zero_done"], 1)
            pool.memset(wdec, 0.0).then_inc(sems["zero_done"], 1)
            for name, (row, n) in row_places.items():
                src = ins[name]
                if name == "gla_norm_g":
                    for half in range(2):
                        pool.dma_start(rows[row:row + 1, 64 * half:64 * half + 64], src).then_inc(sems["params"], 16)
                    continue
                flat = flat_rows(src)
                pool.dma_start(rows[row:row + n, :], flat).then_inc(sems["params"], 16)
            pool.dma_start(const0, ins["const0"]).then_inc(sems["params"], 16)
            pool.wait_ge(*at("c_cols"))
            pool.dma_start(cx, ins["ctx"][0].rearrange("(t p) d -> p t d", p=P)).then_inc(sems["loaded_ctx"], 16)
            pool.dma_start(const1, ins["const1"]).then_inc(sems["params2"], 16)
            pool.dma_start(lam_row, ins["diff_lambda"][0:1].rearrange("o n d -> o (n d)").to_broadcast([P, 256])
                           .rearrange("p (n d) -> p n d", d=64)).then_inc(sems["params2"], 16)
            pool.wait_ge(sems["zero_done"], 3)
            for d in range(2):
                pool.dma_start(wdec[16 * d:16 * d + 16, d, :], ins["gla_w_decay"][0, d]).then_inc(sems["params2"], 16)
            pool.dma_start(router_b[:, 0:NG], ins["b_router_group"].to_broadcast([P, NG])).then_inc(sems["params2"], 16)
            pool.dma_start(router_b[:, NG:NG + NE], ins["b_router_expert"].to_broadcast([P, NE])).then_inc(sems["params2"], 16)
            for h in range(4):
                pool.dma_start(band[:, 7 * h:7 * h + 7, 48:79],
                               ins["na_rel_bias"][0, h:h + 1, 4:11, :].rearrange("o r c -> o (r c)")
                               .to_broadcast([GRID, 7 * 31]).rearrange("p (r c) -> p r c", c=31))\
                    .then_inc(sems["loaded_bias"], 16)
            pool.wait_ge(sems["loaded_bias"], 64)
            pool.dma_start(bias_dram[0:GRID * 28 * P].rearrange("(p n) -> p n", p=GRID), band_flat)\
                .then_inc(sems["bias_out"], 16)
            pool.wait_ge(sems["bias_out"], 16)
            pool.wait_ge(*at("mod_t", 12))
            pool.wait_ge(*at("mod_col", 12))
            pool.wait_ge(*at("lam"))
            for r in range(4):
                for h in range(4):
                    off = (7 * h + 3 - r) * P + 63
                    pitch = 28 * P - 1
                    src = bias_dram[off:off + GRID * pitch].rearrange("(q n) -> q n", n=pitch)[:, 0:4 * P]\
                        .rearrange("q (k c) -> q k c", k=4)[:, :, 0:GRID]
                    pool.dma_start(nb_bias[64 * (r % 2):64 * (r % 2) + 64, r // 2, h, :]
                                   .rearrange("q (k c) -> q k c", k=4), src).then_inc(sems["loaded_bias"], 16)
            pool.wait_ge(*at("mixed"))
            pool.dma_start(router_w[:, :, 0:NG], ins["w_router_group"][0].rearrange("(k p) n -> p k n", p=P))\
                .then_inc(sems["router_w"], 16)
            pool.dma_start(router_w[:, :, NG:], ins["w_router_expert"][0].rearrange("(k p) n -> p k n", p=P))\
                .then_inc(sems["router_w"], 16)
            pool.dma_start(final_g, ins["final_g"].rearrange("(o n) -> o n", o=1).to_broadcast([P, D]))\
                .then_inc(sems["router_w"], 16)
            pool.memset(zeros, 0.0).then_inc(sems["zero_tile"], 1)
            second_block_pool(pool, at)
        @block.tensor
        def _(pe):
            at = Tally(sems)
            plan = Ring(sems)
            windows["pe"] = counter(pe, "window_pe")

            def piece_ready(piece):
                slot, sem, value = plan.place(dmas_of(piece))
                pe.wait_ge(sem, value)
                return slot

            def turn(dst, src):
                return pe.transpose(dst, src, ident[0:src.shape[0], 0:src.shape[0]])

            pe.wait_ge(sems["params"], PARAMS)
            turn(ps[4][:, 0:n_rows], rows[0:n_rows, :]).then_inc(sems["c_T"], 1)
            pe.wait_ge(*at("c_cols", 2))

            def modulate(j):
                slot = piece_ready(("mod", j))
                w = w_cols(slot, 512)
                for k in range(KD):
                    for g in range(4):
                        mm = pe.matmul(ps[j % 2][32 * g:32 * g + 32, 0:P], cT[:, k, :], w[:, k, P * g:P * g + P],
                                       start=(k == 0), stop=(k == KD - 1))
                mm.then_inc(sems["mod_mm"], 1)
                pe.wait_ge(*at("mod_row"))
                if j >= 2:
                    pe.wait_ge(sems["mod_col"], j - 1)
                turn(ps[2 + j % 2][:, 0:P], mod_row[:, j % 2, :]).then_inc(sems["mod_t"], 1)
                pe.wait_ge(sems["mod_t"], j + 1)
                pe.sem_inc(sems["piece_used"], 1)

            for j in range(4):
                modulate(j)

            pe.wait_ge(*at("xn", 4))
            for k in range(KD):
                if k >= 4:
                    pe.wait_ge(sems["xT_v" if k % 2 == 0 else "xT_s"], (k - 4) // 2 + 1)
                for t in range(2 * NT):
                    src = (xn[:, t, :] if t < NT else cx[:, t - NT, :])[:, P * k:P * k + P]
                    mm = turn(ps[4 + k % 4][:, P * t:P * t + P], src)
                mm.then_inc(sems["x_T"], 1)
            pe.wait_ge(*at("xT_v", 4))
            pe.wait_ge(*at("xT_s", 4))

            where = {"qb": (0, 128, S), "kb": (128, 128, 2 * S), "rb": (256, 128, S), "gb": (0, 32, 2 * S),
                     "qn": (0, 128, S), "kn": (256, 128, 2 * S)}
            mods = iter(range(4, 12))
            piece = -1
            for n, (kind, of, what, i, who) in enumerate(UNITS):
                if kind != "X" and of != piece:
                    if 2 <= of <= 5:
                        modulate(next(mods))
                        modulate(next(mods))
                    piece = of
                    slot = piece_ready(("win", piece))
                    w = w_cols(slot, WIN_WIDTH[piece])
                emptied_before(pe, n)
                bank = ps[4 + n % 4]
                last = n + 1 == len(UNITS) or all(u[1] != of or u[0] == "X" for u in UNITS[n + 1:])
                if kind == "T":
                    col, m, tokens = where[what]
                    for k in range(KD):
                        mm = pe.matmul(bank[0:m, 0:tokens], w[:, k, col + P * i:col + P * i + m], hT[:, k, 0:tokens],
                                       start=(k == 0), stop=(k == KD - 1))
                elif kind == "K":
                    for k in range(KD):
                        mm = pe.matmul(bank, hT[:, k, P * i:P * i + P], w[:, k, :], start=(k == 0), stop=(k == KD - 1))
                else:
                    tile = i if what == "qa" else NT + i
                    pe.wait_ge(sems["rot_tile"], tile + 1)
                    for c in range(4):
                        mm = turn(bank[:, P * c:P * c + P], rot_o[:, tile % 2, P * c:P * c + P])
                mm.then_inc(sems["unit_mm"], 1)
                if kind != "X" and last:
                    pe.wait_ge(sems["unit_mm"], n + 1)
                    pe.sem_inc(sems["piece_used"], 1)

            pe.wait_ge(sems["params2"], PARAMS2)
            pe.wait_ge(sems["unit_s"], emptied(UNITS, len(UNITS), "s"))
            pe.wait_ge(sems["unit_v"], emptied(UNITS, len(UNITS), "v"))
            pe.wait_ge(sems["mod_row"], 12)
            for d in range(2):
                pe.matmul(ps[d], wdec[:, d, :], glow[0:32, :], start=True, stop=True).then_inc(sems["gate_z"], 1)
            pe.wait_ge(*at("gla_qk", 2))
            for h in range(4):
                if h:
                    pe.wait_ge(sems["gla_at"], h)
                r = slice(32 * h, 32 * h + 32)

                def part(d, name, a, n, _r=r):
                    o = {"base_q": 768, "base_k": 1024, "ctx_q": 1280, "ctx_k": 1536}.get(name, 256 * int(name[-1])
                                                                                     if name[0] == "l" else 0)
                    return qk[_r, d, o + a:o + a + n]

                A = ps[h].rearrange("p (s t) -> p s t", s=2)

                def block_mm(dst, d, key, query, s0, t0, n, m):
                    return pe.matmul(dst, part(d, key, s0, m), part(d, query, t0, n), start=True, stop=True)

                block_mm(A[:, 0, P:2 * P], 0, "l0", "l0", 0, P, P, P)
                block_mm(A[:, 1, 0:P], 1, "l0", "l0", P, 0, P, P)
                for u in range(2):
                    o = P * u
                    block_mm(A[0:64, u, o + 64:o + 128], 0, "l1", "l1", o, o + 64, 64, 64)
                    block_mm(A[64:128, u, o:o + 64], 1, "l1", "l1", o + 64, o, 64, 64)
                    for v in range(2):
                        a, b = 64 * v, 64 * v + 32
                        block_mm(A[a:a + 32, u, o + b:o + b + 32], 0, "l2", "l2", o + a, o + b, 32, 32)
                        block_mm(A[b:b + 32, u, o + a:o + a + 32], 1, "l2", "l2", o + b, o + a, 32, 32)
                    for j in range(4):
                        a = 32 * j
                        block_mm(A[a:a + 32, u, o + a:o + a + 32], 0, "base_k", "base_q", o + a, o + a, 32, 32)
                        mm = block_mm(ps[4][a:a + 32, 64 * h + 32 * u:64 * h + 32 * u + 32], 1, "base_k", "base_q",
                                      o + a, o + a, 32, 32)
                mm.then_inc(sems["gla_at"], 1)
                if h >= 2:
                    pe.wait_ge(sems["c_sb"], h - 1)
                for s in range(2):
                    for d in range(2):
                        mm = pe.matmul(ps[5 + h % 2][:, S * s:S * s + S], part(d, "ctx_k", P * s, P),
                                       part(d, "ctx_q", 0, S), start=(d == 0), stop=(d == 1))
                mm.then_inc(sems["gla_c"], 1)
                if h >= 1:
                    context_values(pe, at, h - 1)
            context_values(pe, at, 3)
            pe.wait_ge(*at("at_masked"))
            for h in range(4):
                o = ps[7][64 * (h % 2):64 * (h % 2) + 64, S * (h // 2):S * (h // 2) + S]
                for s in range(2):
                    mm = pe.matmul(o, vbn[:, s, 64 * h:64 * h + 64], atT[:, h, s, :], start=False,
                                   stop=(s == 1), skip_group_check=True)
            mm.then_inc(sems["gla_o"], 1)
            pe.wait_ge(*at("o_sq"))
            pe.matmul(ps[4], C0["ones64"], gl_s.rearrange("p h n -> p (h n)"), start=True, stop=True)\
                .then_inc(sems["gla_ss"], 1)

            pe.wait_ge(*at("gla_y"))
            attention_pe(pe, at, "na")
            attention_pe(pe, at, "diff")
            pe.wait_ge(*at("a_sq"))
            for b in range(2):
                mm = pe.matmul(ps[b], ones, oS[:, 2 * b:2 * b + 2, :].rearrange("p h n -> p (h n)"), start=True, stop=True)
            mm.then_inc(sems["a_ss"], 1)

            pe.wait_ge(*at("mixed"))
            out_projection_pe(pe, at, piece_ready, "wout", mixT)
            gate_broadcast_pe(pe, at, 4)
            norm_pe(pe, at)
            experts_pe(pe, at, plan, 1)
            gate_broadcast_pe(pe, at, 0)
            second_block_pe(pe, at, plan, piece_ready)


        @block.scalar
        def _(act):
            at = Tally(sems)
            windows["act"] = counter(act, "window_act")

            def link(ins):
                ins.then_inc(sems["scalar_step"], 1)
                act.wait_ge(*at("scalar_step"))

            act.wait_ge(*at("c_cols"))
            act.wait_ge(*at("zero_done", 3))
            act.activation(cT[:, :, 0:2], rowsT[:, 0:16].rearrange("p (i k) -> p k i", i=2), ACT.Silu)\
                .then_inc(sems["c_cols"], 1)
            act.wait_ge(sems["loaded_x"], 16)
            act.wait_ge(sems["loaded_ctx"], 16)
            for t in range(2 * NT):
                src = X[:, t, :] if t < NT else cx[:, t - NT, :]
                link(act.activation(hTf[:, D * t:D * t + D], src, ACT.Square, accum_out=ss[:, t:t + 1]))
            act.sem_inc(sems["sumsq"], 1)
            act.wait_ge(*at("mean"))
            act.activation(rstd, ss, ACT.Sqrt).then_inc(sems["sqrt_done"], 1)

            def mod_copy(j):
                act.wait_ge(*at("mod_mm"))
                if j >= 2:
                    act.wait_ge(sems["mod_t"], j - 1)
                act.activation(mod_row[:, j % 2, :], ps[j % 2][:, 0:P], ACT.Copy).then_inc(sems["mod_row"], 1)

            for j in range(4):
                mod_copy(j)
            act.wait_ge(*at("scale"))
            for k in range(1, KD, 2):
                act.wait_ge(sems["x_T"], k + 1)
                link(act.activation(hT[:, k, 0:S], ps[4 + k % 4][:, 0:S], ACT.Identity,
                                    bias=modT[:, k, 0:1], scale=scaleT[:, 0, k:k + 1]))
                act.activation(hT[:, k, S:2 * S], ps[4 + k % 4][:, S:2 * S], ACT.Identity,
                               bias=modT[:, k, 1:2], scale=scaleT[:, 1, k:k + 1]).then_inc(sems["xT_s"], 1)
            at("x_T", KD)
            mods = iter(range(4, 12))
            piece = -1
            act.wait_ge(sems["bias_out"], 16)
            for n, (kind, of, what, i, who) in enumerate(UNITS):
                if kind != "X" and of != piece:
                    if 2 <= of <= 5:
                        mod_copy(next(mods))
                        mod_copy(next(mods))
                    piece = of
                if who != "s":
                    continue
                act.wait_ge(sems["unit_mm"], n + 1)
                bank = ps[4 + n % 4]
                if kind == "X":
                    dst = qaT if what == "qa" else kaT
                    ins_ = act.activation(dst[:, :, P * i:P * i + P], bank.rearrange("p (c n) -> p c n", c=4), ACT.Copy)
                elif what == "qb":
                    ins_ = act.activation(qbT, bank[:, 0:S], ACT.Copy, scale=32.0 ** -0.5)
                elif what == "gb":
                    ins_ = act.activation(glow[0:32, :], bank[0:32, :], ACT.Copy)
                elif what == "rb":
                    ins_ = act.activation(rT[:, i, :], bank[:, 0:S], ACT.Silu)
                elif what == "qn":
                    ins_ = act.activation(qnT[:, i, :], bank[:, 0:S], ACT.Copy, scale=0.125)
                elif what == "kn":
                    ins_ = act.activation(knT[:, i, :], bank, ACT.Copy)
                else:
                    ins_ = act.activation(va[:, i, :], bank, ACT.Copy)
                ins_.then_inc(sems["unit_s"], 1)

            act.wait_ge(*at("z_bias"))
            link(act.activation(ze, ze, ACT.Exp))
            act.activation(ze, ze, ACT.Ln, bias=1.0).then_inc(sems["z_ln"], 1)
            for d in range(2):
                act.wait_ge(*at("gla_d"))
                link(act.activation(qk[:, d, 0:768], qk[:, d, 0:768], ACT.Exp))
                link(act.activation(qk[:, d, 768:1024], dif[:, 3, :], ACT.Exp, scale=1.0 if d == 0 else -1.0))
                link(act.activation(qk[:, d, 1024:1280], dif[:, 3, :], ACT.Exp, scale=-1.0 if d == 0 else 1.0))
                if d == 0:
                    link(act.activation(qk[:, d, 1280:1536], pre[:, d, 0, :], ACT.Exp))
                    link(act.activation(qk[:, d, 1536:1792], pre[:, d, 1, :], ACT.Exp, bias=pre[:, d, 1, S - 1:S], scale=-1.0))
                else:
                    link(act.activation(qk[:, d, 1280:1536], pre[:, d, 0, :], ACT.Exp, bias=cols[:, 0:1], scale=-1.0))
                    link(act.activation(qk[:, d, 1536:1792], pre[:, d, 1, :], ACT.Exp))
                act.sem_inc(sems["gla_e"], 1)
            for h in range(4):
                act.wait_ge(*at("gla_c"))
                if h >= 2:
                    act.wait_ge(sems["c_used"], h - 1)
                act.activation(ctT[:, h % 2, :, :].rearrange("p s n -> p (s n)"), ps[5 + h % 2], ACT.Copy)\
                    .then_inc(sems["c_sb"], 1)
            act.wait_ge(*at("o_sb"))
            act.activation(gl_s, gl_o, ACT.Square).then_inc(sems["o_sq"], 1)
            act.wait_ge(*at("gla_mean"))
            act.activation(gl_s, gl_s, ACT.Sqrt).then_inc(sems["gla_sqrt"], 1)
            act.wait_ge(*at("lam_sums"))
            act.activation(cols[:, 8:10], cols[:, 8:10], ACT.Exp).then_inc(sems["lam_exp"], 1)
            attention_act(act, at, "na")
            attention_act(act, at, "diff")
            act.wait_ge(*at("pv_sb", 2 + 4))
            act.activation(oS, oA, ACT.Square).then_inc(sems["a_sq"], 1)
            act.wait_ge(*at("a_mean"))
            act.activation(oS, oS, ACT.Sqrt).then_inc(sems["a_sqrt"], 1)
            norm_act(act, at, scaleT[:, 2, :], modT[:, 3 * KD:4 * KD, :])
            experts_act(act, at, 1, scaleT[:, 2, :], modT[:, 3 * KD:4 * KD, :])
            squares_act(act, at)
            second_block_act(act, at, link)

        @block.vector
        def _(dve):
            at = Tally(sems)
            windows["dve"] = counter(dve, "window_dve")
            windows["cur"] = counter(dve, "experts_dve")

            def link(ins):
                ins.then_inc(sems["vector_step"], 1)
                dve.wait_ge(*at("vector_step"))

            dve.wait_ge(*at("c_T"))
            dve.tensor_copy(rowsT[:, 0:n_rows], ps[4][:, 0:n_rows]).then_inc(sems["c_cols"], 1)
            dve.wait_ge(*at("c_cols", 2))
            dve.wait_ge(*at("sumsq"))
            link(dve.tensor_scalar(ss, ss, 1.0 / D, EPS, ALU.mult, ALU.add))
            dve.reciprocal(ss, ss).then_inc(sems["mean"], 1)
            dve.wait_ge(*at("sqrt_done"))
            for t in range(2 * NT):
                src = X[:, t, :] if t < NT else cx[:, t - NT, :]
                dst = xn[:, t, :] if t < NT else cx[:, t - NT, :]
                dve.tensor_scalar(dst, src, rstd[:, t:t + 1], None, ALU.mult).then_inc(sems["xn"], 1)

            def mod_columns(j):
                dve.wait_ge(*at("mod_t"))
                dve.tensor_tensor(modT[:, 4 * j:4 * j + 4, :],
                                  ps[2 + j % 2][:, 0:P].rearrange("p (g i) -> p g i", i=32)[:, :, 0:2],
                                  PT["b_mod"][:, 4 * j:4 * j + 4].unsqueeze(2).broadcast_to([P, 4, 2]), ALU.add)\
                    .then_inc(sems["mod_col"], 1)

            for j in range(4):
                mod_columns(j)
            dve.wait_ge(*at("mod_col", 4))
            for i in range(2):
                link(dve.tensor_scalar(scaleT[:, i, :], modT[:, KD:2 * KD, i], 1.0, None, ALU.add))
                link(dve.tensor_tensor(scaleT[:, i, :], scaleT[:, i, :], PT["norm1_g"], ALU.mult))
            dve.sem_inc(sems["scale"], 1)
            for k in range(0, KD, 2):
                dve.wait_ge(sems["x_T"], k + 1)
                link(dve.tensor_scalar(hT[:, k, 0:S], ps[4 + k % 4][:, 0:S], scaleT[:, 0, k:k + 1], modT[:, k, 0:1],
                                       ALU.mult, ALU.add))
                dve.tensor_scalar(hT[:, k, S:2 * S], ps[4 + k % 4][:, S:2 * S], scaleT[:, 1, k:k + 1],
                                  modT[:, k, 1:2], ALU.mult, ALU.add).then_inc(sems["xT_v"], 1)
            at("x_T", KD)
            dve.wait_ge(sems["params2"], PARAMS2)
            link(dve.tensor_tensor(lam_row[:, 0:3:2, :], lam_row[:, 0:3:2, :], lam_row[:, 1:4:2, :], ALU.mult))
            dve.tensor_reduce(cols[:, 8:10], lam_row[:, 0:3:2, :], AX, ALU.add).then_inc(sems["lam"], 1)
            dve.wait_ge(*at("lam"))
            dve.sem_inc(sems["lam_sums"], 1)

            def rotate(bank, tile):
                cos = C1["rope_cos"][:, 64 * tile:64 * tile + 64].unsqueeze(1).broadcast_to([P, 8, 64])
                x4 = bank.rearrange("p (h a b f) -> p h a b f", h=8, a=2, b=2)
                s4 = C1["rope_sin"][:, 64 * tile:64 * tile + 64].rearrange("p (a b f) -> p a b f", a=2, b=2)
                b4 = rot_b.rearrange("p (h a b f) -> p h a b f", h=8, a=2, b=2)
                for b in range(2):
                    dve.tensor_tensor(b4[:, :, :, b, :], x4[:, :, :, 1 - b, :],
                                      s4[:, :, b, :].unsqueeze(1).broadcast_to([P, 8, 2, 16]), ALU.mult)
                return cos

            tiles = 0
            mods = iter(range(4, 12))
            piece = -1
            dve.wait_ge(sems["bias_out"], 16)
            for n, (kind, of, what, i, who) in enumerate(UNITS):
                if kind != "X" and of != piece:
                    if 2 <= of <= 5:
                        mod_columns(next(mods))
                        mod_columns(next(mods))
                    piece = of
                if who != "v":
                    continue
                dve.wait_ge(sems["unit_mm"], n + 1)
                bank = ps[4 + n % 4]
                if what == "kb":
                    dve.tensor_copy(kbT, bank).then_inc(sems["unit_v"], 1)
                elif what == "vbn":
                    dve.tensor_copy(vbn[:, i, :], bank).then_inc(sems["unit_v"], 1)
                elif what == "qn":
                    dve.tensor_scalar(qnT[:, i, :], bank[:, 0:S], 0.125, None, ALU.mult).then_inc(sems["unit_v"], 1)
                elif what == "kn":
                    dve.tensor_copy(knT[:, i, :], bank).then_inc(sems["unit_v"], 1)
                elif what == "va":
                    dve.tensor_copy(va[:, i, :], bank).then_inc(sems["unit_v"], 1)
                else:
                    if tiles >= 2:
                        turned = [m for m, u in enumerate(UNITS) if u[0] == "X"][tiles - 2]
                        dve.wait_ge(sems["unit_mm"], turned + 1)
                    o = rot_o[:, tiles % 2, :]
                    if i < NT:
                        if tiles:
                            dve.wait_ge(sems["rot_tile"], tiles)
                        cos = rotate(bank, i)
                        x3 = bank.rearrange("p (h n) -> p h n", h=8)
                        dve.tensor_tensor(o.rearrange("p (h n) -> p h n", h=8), x3, cos, ALU.mult)\
                            .then_inc(sems["unit_v"], 1)
                        dve.wait_ge(sems["unit_v"], emptied(UNITS, n + 1, "v"))
                        dve.tensor_tensor(o, o, rot_b, ALU.add).then_inc(sems["rot_tile"], 1)
                    else:
                        dve.tensor_copy(o, bank).then_inc(sems["unit_v"], 1)
                        dve.wait_ge(sems["unit_v"], emptied(UNITS, n + 1, "v"))
                        dve.sem_inc(sems["rot_tile"], 1)
                    tiles += 1

            dve.wait_ge(*at("gate_z", 2))
            for d in range(2):
                link(dve.tensor_scalar(zg[:, d, :], ps[d], PT["gla_b_decay"][:, d:d + 1], None, ALU.add))
            dve.scalar_tensor_tensor(ze, zg, -1.0, zg, ALU.mult, ALU.min).then_inc(sems["z_bias"], 1)
            dve.wait_ge(*at("z_ln"))
            link(dve.scalar_tensor_tensor(zg, zg, 0.0, ze, ALU.min, ALU.subtract))
            link(dve.tensor_scalar(zg, zg, 1.0 / 16.0, None, ALU.mult))
            for d in range(2):
                for s in range(2):
                    ins_ = dve.tensor_tensor_scan(pre[:, d, s, :], ones[:, 0:1].broadcast_to([P, S]),
                                                  zg[:, d, S * s:S * s + S], 0.0, ALU.mult, ALU.add)
            link(ins_)
            link(dve.tensor_copy(cols[:, 0:1], pre[:, 1, 0, S - 1:S]))
            link(dve.tensor_tensor(pre[:, 1, :, :].rearrange("p s n -> p (s n)"),
                                   pre[:, 1, :, :].rearrange("p s n -> p (s n)"), zg[:, 1, :], ALU.subtract))

            def decayed(d):
                p = pre[:, d, 0, :]
                if d == 1:
                    dve.wait_ge(*at("gla_e"))
                for lv in range(4):
                    blk = S >> lv
                    v = p.rearrange("p (b n) -> p b n", n=blk)
                    mid = blk // 2 if (d == 1 or lv == 3) else blk // 2 - 1
                    link(dve.tensor_tensor(dif[:, lv, :].rearrange("p (b n) -> p b n", n=blk), v,
                                           v[:, :, mid:mid + 1].broadcast_to([P, S // blk, blk]), ALU.subtract))
                flat = dif[:, 0:3, :].rearrange("p l n -> p (l n)")
                dve.scalar_tensor_tensor(qk[:, d, 0:768], flat, -1.0, flat, ALU.mult, ALU.min)\
                    .then_inc(sems["gla_d"], 1)

            def products(d):
                for lv in range(3):
                    blk = S >> lv
                    view = lambda x: x.rearrange("p (b u n) -> p b u n", u=2, n=blk // 2)
                    e = view(qk[:, d, S * lv:S * lv + S])
                    for u in range(2):
                        who = view(qbT if (u == 1) == (d == 0) else kbT[:, 0:S])
                        dve.tensor_tensor(e[:, :, u, :], e[:, :, u, :], who[:, :, u, :], ALU.mult)
                for o, who in ((768, qbT), (1024, kbT[:, 0:S]), (1280, qbT), (1536, kbT[:, S:2 * S])):
                    e = qk[:, d, o:o + S]
                    ins_ = dve.tensor_tensor(e, e, who, ALU.mult)
                ins_.then_inc(sems["gla_qk"], 1)

            decayed(0)
            decayed(1)
            products(0)
            dve.wait_ge(*at("gla_e"))
            products(1)
            lim = 3.0e38
            dve.wait_ge(*at("gla_at", 4))
            for h in range(4):
                link(dve.tensor_scalar(atT[:, h, :, :].rearrange("p s n -> p (s n)"), ps[h], lim, -lim, ALU.min, ALU.max))
            link(dve.tensor_scalar(at_b, ps[4][:, 0:S], lim, -lim, ALU.min, ALU.max))
            b3 = at_b.rearrange("p (g n) -> p g n", n=32)
            link(dve.tensor_tensor(b3, b3, C1["mask_bwd"].unsqueeze(1).broadcast_to([P, 8, 32]), ALU.mult))
            for j in range(4):
                rows_ = slice(32 * j, 32 * j + 32)
                for h in range(4):
                    dg = diagonal(rows_, h, 32 * j)
                    dve.tensor_tensor(dg, dg, C1["mask_fwd"][rows_, :].unsqueeze(1).broadcast_to([32, 2, 32]), ALU.mult)
            link(dve.tensor_copy(cols[:, 1:2], cols[:, 0:1]))
            for j in range(4):
                rows_ = slice(32 * j, 32 * j + 32)
                for h in range(4):
                    dg = diagonal(rows_, h, 32 * j)
                    ins_ = dve.tensor_tensor(dg, dg, b3[rows_, 2 * h:2 * h + 2, :], ALU.add)
            ins_.then_inc(sems["at_masked"], 1)
            dve.wait_ge(*at("gla_o"))
            dve.tensor_copy(gl_o.rearrange("p h n -> p (h n)"), ps[7]).then_inc(sems["o_sb"], 1)
            dve.wait_ge(*at("gla_ss"))
            g2 = gl_s.rearrange("p h n -> p (h n)")
            link(dve.tensor_scalar(g2, ps[4], 1.0 / 64, EPS, ALU.mult, ALU.add))
            dve.reciprocal(g2, g2).then_inc(sems["gla_mean"], 1)
            dve.wait_ge(*at("gla_sqrt"))
            link(dve.scalar_tensor_tensor(gl_o, gl_o, PT["gla_norm_g"], gl_s, ALU.mult, ALU.mult))
            dve.tensor_tensor(mixT[:, 4:6, :], gl_o, rT, ALU.mult).then_inc(sems["gla_y"], 1)
            dve.wait_ge(*at("gla_y"))

            dve.wait_ge(sems["loaded_bias"], 64 + 16 * 16)
            for t in range(NT):
                b4 = nb_bias[:, t, :, :].rearrange("p h (k c) -> p (h k) c", c=GRID)
                ins_ = dve.tensor_tensor(b4, b4, C1["nb_mask"].unsqueeze(1).broadcast_to([P, 16, GRID]), ALU.add)
            link(ins_)
            dve.wait_ge(*at("lam_exp"))
            link(dve.tensor_tensor(cols[:, 10:11], cols[:, 9:10], cols[:, 8:9], ALU.subtract))
            link(dve.tensor_scalar(cols[:, 10:11], cols[:, 10:11], -LAM_INIT, None, ALU.add))
            link(dve.tensor_scalar(cols[:, 11:12], PT["diff_sub_g"], 1.0 - LAM_INIT, None, ALU.mult))
            attention_dve(dve, at, link, "na")
            attention_dve(dve, at, link, "diff")
            dve.wait_ge(*at("a_ss"))
            for b in range(2):
                half = oS[:, 2 * b:2 * b + 2, :].rearrange("p h n -> p (h n)")
                link(dve.tensor_scalar(half, ps[b], 1.0 / P, EPS, ALU.mult, ALU.add))
            dve.reciprocal(oS, oS).then_inc(sems["a_mean"], 1)
            dve.wait_ge(*at("a_sqrt"))
            dve.scalar_tensor_tensor(mixT[:, 0:4, :], oA, cols[:, 11:12], oS, ALU.mult, ALU.mult)\
                .then_inc(sems["mixed"], 1)
            dve.wait_ge(*at("mixed"))
            gate_diagonals_dve(dve, at, 2)
            link(dve.tensor_scalar(scaleT[:, 2, :], modT[:, 4 * KD:5 * KD, 0], 1.0, None, ALU.add))
            link(dve.tensor_tensor(scaleT[:, 2, :], scaleT[:, 2, :], PT["norm2_g"], ALU.mult))
            dve.wait_ge(*at("out_mm", 2))
            residual_dve(dve, at, link, 0, 4)
            norm_dve(dve, at, link, scaleT[:, 2, :], modT[:, 3 * KD:4 * KD, :])
            route_dve(dve, at, link, 1)
            experts_dve(dve, at, link, 1, scaleT[:, 2, :], modT[:, 3 * KD:4 * KD, :])
            gate_diagonals_dve(dve, at, 5)
            residual_dve(dve, at, link, 4, 0)
            dve.wait_ge(*at("router_w", 48))
            final_dve(dve, at, link)
            second_block_dve(dve, at, link)



INS = ["x", "ctx", "c", "c_ctx", "w_mod", "b_mod", "norm1_g", "norm2_g", "w_in", "w_out", "diff_lambda", "diff_sub_g",
       "gla_w_decay", "gla_b_decay", "gla_norm_g", "na_rel_bias", "w_router_group", "b_router_group",
       "w_router_expert", "b_router_expert", "w_expert_up", "w_expert_down", "final_g", "norm1_g_2", "w_in_2",
       "q_norm_g_2", "w_uq_2", "kv_norm_g_2", "w_ukv_2", "pool_w_2", "pool_scale_2", "w_out_2", "norm2_g_2",
       "w_group_2", "b_group_2", "w_expert_2", "b_expert_2", "w_gate_2", "w_up_2", "w_down_2", "final_g_2"]
SCRATCH = GRID * 28 * P + 32 * P


def kernel(**inputs):
    import concourse.bacc as bacc
    from concourse.bass_utils import run_bass_kernel_spmd

    arrays = {n: np.ascontiguousarray(inputs[n]) for n in INS}
    arrays.update(shape_constants())
    nc = bacc.Bacc("TRN2", target_bir_lowering=False, num_devices=1)
    ins = {n: nc.dram_tensor(f"in_{n}", a.shape, F32, kind="ExternalInput").ap() for n, a in arrays.items()}
    ins["bias_scratch"] = nc.dram_tensor("bias_scratch", [SCRATCH], F32, kind="Internal").ap()
    out = nc.dram_tensor("out", [1, S, D], F32, kind="ExternalOutput").ap()
    hybrid_kernel(nc, ins, out)
    result = run_bass_kernel_spmd(nc, [{f"in_{n}": a for n, a in arrays.items()}], core_ids=[0])
    return result.results[0]["out"]
```

```python
from contextlib import ExitStack

import numpy as np
import concourse.bass as bass
from concourse import mybir

F32 = mybir.dt.float32
I32 = mybir.dt.int32
ALU = mybir.AluOpType
ACT = mybir.ActivationFunctionType
AX = mybir.AxisListType.X

P = 128
D = 1024
KD = D // P
S = 256
NT = S // P
SLOT = 4096
RING = 6
NE = 32
NG = 4
EG = NE // NG
GRID = 64
BIG = 1e30
EPS = 1e-6
LAM_INIT = 0.2

CONST_COLS = {"ident": P, "ones": P, "tri": P, "ones64": P, "slot64": P, "slot32": P, "slot128": P, "iota8": 8,
              "step1": 8, "step2": 8}
CONST1_COLS = {"rope_cos": 2 * 64, "rope_sin": 2 * 64, "nb_mask": GRID, "mask_fwd": 32, "mask_bwd": 32}
CONST2_COLS = {"rope_cos": 2 * 32, "rope_sin": 2 * 32, "chunk_mask": P, "strict_mask": P, "pool": 4 * 2 * S}


def offsets(cols):
    at, out = 0, {}
    for name, n in cols.items():
        out[name] = (at, n)
        at += n
    return out, at


def rope_table(n_tokens, dim, positions):
    inv = np.float32(10000.0) ** (-np.arange(16, dtype=np.float32) / np.float32(16))
    cos, sin = [], []
    for pos in positions:
        ang = pos.astype(np.float32)[:, None] * inv.astype(np.float32)
        cos += [np.cos(ang), np.cos(ang)]
        sin += [-np.sin(ang), np.sin(ang)]
    cos, sin = (np.concatenate(x, axis=1).astype(np.float32) for x in (cos, sin))
    tile = lambda t: t.reshape(n_tokens // P, P, dim).transpose(1, 0, 2).reshape(P, -1)
    return tile(cos), tile(sin)


def shape_constants():
    r = np.arange(P)
    t = np.arange(S)
    c = {
        "ident": np.eye(P),
        "ones": np.ones((P, P)),
        "tri": r[:, None] < r[None, :],
        "ones64": (r[:, None] // 64) == (r[None, :] // 64),
        "slot64": np.broadcast_to(r % 64, (P, P)),
        "slot32": np.broadcast_to(r % 32, (P, P)),
        "iota8": np.broadcast_to(np.arange(8), (P, 8)),
        "slot128": np.broadcast_to(r, (P, P)),
        "step1": np.broadcast_to(2 * np.arange(8) + 1, (P, 8)),
        "step2": np.broadcast_to(np.arange(8) + 1, (P, 8)),
    }
    cos, sin = rope_table(S, 64, [t // GRID, t % GRID])
    q = r % GRID
    start = np.clip(q - 8, 0, GRID - 16)
    k = np.arange(GRID)
    inside = (k[None, :] >= start[:, None]) & (k[None, :] < start[:, None] + 16)
    s32, t32 = r[:, None] % 32, np.arange(32)[None, :]
    c1 = {
        "rope_cos": cos, "rope_sin": sin, "nb_mask": np.where(inside, 0.0, -BIG),
        "mask_fwd": t32 >= s32, "mask_bwd": s32 >= t32,
    }
    cos, sin = rope_table(S, 32, [t])
    pool = np.zeros((4, S, S))
    for g, w in enumerate((2, 4, 8, 16)):
        for tt in range(S):
            lo = max(0, tt - w + 1)
            pool[g, lo:tt + 1, tt] = np.float32(1.0) / np.float32(min(tt + 1, w))
            pool[g, tt, tt] -= 1.0
    pool = pool.reshape(4, 2, P, S).transpose(2, 0, 1, 3).reshape(P, -1)
    c2 = {
        "rope_cos": cos, "rope_sin": sin,
        "chunk_mask": np.where(r[None, :] // 64 <= r[:, None] // 64, 0.0, -BIG),
        "strict_mask": np.where(r[None, :] < r[:, None], 0.0, -BIG),
        "pool": pool,
    }
    pack = lambda d, cols: np.concatenate([np.asarray(d[n], np.float32).reshape(P, -1) for n in cols], axis=1)
    return {"const0": pack(c, CONST_COLS), "const1": pack(c1, CONST1_COLS), "const2": pack(c2, CONST2_COLS)}


QB, KB, VB, RB, GB, QN, KN, VN = 1536, 1664, 1792, 2048, 2304, 2336, 2592, 2848

def straight_pieces():
    mods = [("mod", j) for j in range(12)]
    wins = [("win", j) for j in range(7)]
    first = mods[:4] + wins[:2]
    for j in range(4):
        first += mods[4 + 2 * j:6 + 2 * j] + [wins[2 + j]]
    first += [wins[6], ("wout", 1), ("wout", 0)]
    second = [("win2", 0), ("win2", 1), ("win2", 2), ("mla", 0), ("wout2", 1), ("wout2", 0)]
    return first, second


def projection_units():
    u = [("T", 0, "qb", 0, "s"), ("T", 0, "kb", 0, "v"), ("T", 0, "rb", 0, "s"), ("T", 0, "rb", 1, "s"),
         ("T", 1, "gb", 0, "s")]
    u += [("K", 2, "vbn", t, "v") for t in range(4)]
    u += [("T", 3, "qn", 0, "s"), ("T", 3, "qn", 1, "v"), ("T", 3, "kn", 0, "s"), ("T", 3, "kn", 1, "v")]
    u += [("K", 4, "qa", 0, "v"), ("K", 4, "qa", 1, "v"), ("X", 4, "qa", 0, "s")]
    u += [("K", 5, "ka", 0, "v"), ("X", 4, "qa", 1, "s"), ("K", 5, "ka", 1, "v"), ("X", 5, "ka", 0, "s"),
          ("K", 5, "ka", 2, "v"), ("X", 5, "ka", 1, "s"), ("K", 5, "ka", 3, "v"), ("X", 5, "ka", 2, "s")]
    u += [("K", 6, "va", 0, "s"), ("X", 5, "ka", 3, "s")]
    u += [("K", 6, "va", t, "v" if t % 2 else "s") for t in range(1, 4)]
    return u


UNITS = projection_units()
LAST_TURN = max(n for n, u in enumerate(UNITS) if u[0] == "X")


def emptied(units, n, engine):
    return sum(1 for u in units[:n] if u[4] == engine)


SEMS = """params loaded_x loaded_ctx loaded_bias bias_out piece0 piece1 piece2 piece3 piece4 piece5 piece_used
vector_step scalar_step c_T c_cols mod_mm mod_row mod_t mod_col
sumsq mean sqrt_done xn x_T xT_v xT_s unit_mm unit_v unit_s rot_tile zero_done
gate_z z_bias z_ln gla_d gla_e gla_qk gla_at gla_c c_sb at_masked gla_o o_sb o_sq gla_ss gla_mean gla_sqrt gla_y
score neg_max exps probs q_padded zero_pad tr tr_sb pv pv_sb a_sq a_ss a_mean a_sqrt mixed
diag gate_bc out_mm resid
logits lg lg_exp route rank_mm 
w_sel w_g0 w_g1 w_ct w_ct_sb w_comb_sb w_up w_silu w_hid w_ht0 w_ht1 w_y w_got_s w_got_v w_gt0 w_gt1 w_xg_v w_xg_s w_ysb_s w_ysb_v w_selg p2_mm p2_s p2_v st_mm pool_w head_s head_v final_gain moe_mm
fin_x
cq_sq cq_mean cq_sqrt cq_n cq_T cq_Ts q_mm q_sb kv_mm kv_sb head_T 
st_zb st_ln st_x st_a st_T st_Ts st_pv st_o pool_d pool_ds pool_y pool_o
w_hsb0 w_hsb1 const2 params2 written scale lam lam_sums lam_exp router_w zero_tile ranked w_cur c_used """.split()


ROWS = {"c": 8, "c_ctx": 8, "b_mod": 48, "norm1_g": 8, "norm2_g": 8, "norm1_g_2": 16, "norm2_g_2": 16,
        "q_norm_g_2": 4, "kv_norm_g_2": 2, "pool_scale_2": 4, "diff_sub_g": 1, "gla_b_decay": 2, "gla_norm_g": 1}
PARAMS = 16 * (len(ROWS) + 2)
PARAMS2 = 16 * 6


def flat_rows(src):
    names = "abcd"[:len(src.shape)]
    flat = src if len(names) == 1 else src.rearrange(f"{' '.join(names)} -> ({' '.join(names)})")
    return flat.rearrange("(r n) -> r n", n=P)


class Tally:

    def __init__(self, sems):
        self.sems, self.n = sems, {name: 0 for name in sems}

    def __call__(self, name, k=1):
        self.n[name] += k
        return self.sems[name], self.n[name]

    def plus(self, name, k):
        return self.sems[name], self.n[name] + k


class Ring:

    def __init__(self, sems):
        self.sems, self.n, self.loads = sems, 0, [0] * RING

    def place(self, dmas):
        slot = self.n % RING
        self.n += 1
        self.loads[slot] += 16 * dmas
        return slot, self.sems[f"piece{slot}"], self.loads[slot]

    def loop(self, turns, per_turn, dmas, dmas_down):
        assert per_turn == RING
        out = []
        for j in range(per_turn):
            slot, step = (self.n + j) % RING, 16 * (dmas if j < 4 else dmas_down)
            out.append((slot, self.sems[f"piece{slot}"], self.loads[slot], step))
            self.loads[slot] += step * turns
        self.n += turns * per_turn
        return out


DMAS = {"mod": 1, "win": 1, "wout": 1, "win2": 1, "mla": 2, "wout2": 1}
WIN_COLS = [[(QB, 256), (RB, 256)], [(GB, 32)], [(VB, 256), (VN, 256)], [(QN, 512)], [(0, 512)], [(512, 512)],
            [(1024, 512)]]
WIN_WIDTH = [sum(n for _, n in cols) for cols in WIN_COLS]
WIN2_COLS = [[(416, 512)], [(1184, 256), (928, 256)], [(0, 416)]]
WIN2_WIDTH = [sum(n for _, n in cols) for cols in WIN2_COLS]


def dmas_of(piece):
    kind, j = piece
    if kind == "win":
        return len(WIN_COLS[j])
    if kind == "win2":
        return len(WIN2_COLS[j])
    return DMAS[kind]


def hybrid_kernel(nc, ins, out):
    first_pieces, second_pieces = straight_pieces()
    row_places, n_rows = offsets(ROWS)
    c0, n_c0 = offsets(CONST_COLS)
    c1, n_c1 = offsets(CONST1_COLS)
    c2, n_c2 = offsets(CONST2_COLS)

    with ExitStack() as ctx:
        def sb(name, cols, dt=F32, rows=P):
            return ctx.enter_context(nc.sbuf_tensor(name, [rows, cols], dt))[:, :]

        sems = {name: ctx.enter_context(nc.semaphore(name)) for name in SEMS}

        ring = sb("ring", RING * SLOT).rearrange("p (r n) -> p r n", r=RING)
        X = sb("X", NT * D).rearrange("p (t d) -> p t d", t=NT)
        xn = sb("xn", NT * D).rearrange("p (t d) -> p t d", t=NT)
        hTf = sb("hT", KD * 2 * S)
        hT = hTf.rearrange("p (k n) -> p k n", k=KD)
        h2T = hTf[:, 0:KD * S].rearrange("p (k n) -> p k n", k=KD)
        const0 = sb("const0_sb", n_c0)
        C0 = {n: const0[:, a:a + w] for n, (a, w) in c0.items()}
        ident, ones, tri = C0["ident"], C0["ones"], C0["tri"]
        small = sb("small", 400)
        modT = small[:, 0:96].rearrange("p (j i) -> p j i", i=2)
        scaleT = small[:, 96:120].rearrange("p (n k) -> p n k", k=KD)
        ss = small[:, 120:124]
        rstd = small[:, 124:128]
        rowsT = small[:, 128:256]
        PT = {n: rowsT[:, a:a + w] for n, (a, w) in row_places.items()}
        router_b = small[:, 256:292]
        cols = small[:, 292:400]
        psum = ctx.enter_context(nc.psum_tensor("psum", [P, 8, 512], F32))
        ps = [psum[:, b, :] for b in range(8)]
        bias_dram = ins["bias_scratch"]

        arena = sb("arena", 18944)
        at_col = [0]

        def area(n):
            at_col[0] += n
            return arena[:, at_col[0] - n:at_col[0]]

        cxf = area(2048)
        rotf = area(1536)
        cx = cxf.rearrange("p (t d) -> p t d", t=NT)
        rot_b, rot_o = rotf[:, 0:512], rotf[:, 512:1536].rearrange("p (b n) -> p b n", b=2)
        qk = arena[:, 0:3584].rearrange("p (d n) -> p d n", d=2)
        q_pad = rotf[:, 0:512].rearrange("p (b m n) -> p b m n", b=2, m=2)
        probs1 = cxf.rearrange("p (b m n) -> p b m n", b=2, m=2)
        qaT = area(1024).rearrange("p (h n) -> p h n", h=4)
        kaT = area(2048).rearrange("p (h n) -> p h n", h=4)
        va = area(2048).rearrange("p (t n) -> p t n", t=4)
        vbn = area(2048).rearrange("p (t n) -> p t n", t=4)
        qnT = area(512).rearrange("p (h n) -> p h n", h=2)
        knT = area(1024).rearrange("p (h n) -> p h n", h=2)
        qbT = area(256)
        kbT = area(512)
        rT = area(512).rearrange("p (h n) -> p h n", h=2)
        glow = area(512)
        nb_biasf = area(2048)
        nb_bias = nb_biasf.rearrange("p (t h n) -> p t h n", t=2, h=4)
        const1 = area(n_c1)
        C1 = {n: const1[:, a:a + w] for n, (a, w) in c1.items()}
        mixf = area(2048)
        mixT = mixf.rearrange("p (k n) -> p k n", k=KD)
        wdec = area(256)[0:32, :].rearrange("p (d n) -> p d n", d=2)
        rows = knT[:, 0, 0:P]
        cT = nb_biasf[:, 0:256].rearrange("p (k i) -> p k i", i=32)
        mod_row = nb_biasf[:, 256:512].rearrange("p (b n) -> p b n", b=2)
        lam_row = nb_biasf[:, 512:768].rearrange("p (n d) -> p n d", d=64)
        zg = xn[:, 0, :].rearrange("p (d n) -> p d n", d=2)
        ze = xn[:, 1, :].rearrange("p (d n) -> p d n", d=2)
        pre = mixf[:, 0:1024].rearrange("p (d s n) -> p d s n", d=2, s=2)
        dif = nb_biasf[:, 1024:2048].rearrange("p (l n) -> p l n", l=4)
        atT = hTf[:, 1024:3072].rearrange("p (h s n) -> p h s n", h=4, s=2)
        ctT = hTf[:, 3072:4096].rearrange("p (b s n) -> p b s n", b=2, s=2)
        gl_o = hTf[:, 0:512].rearrange("p (h n) -> p h n", h=2)
        gl_s = hTf[:, 512:1024].rearrange("p (h n) -> p h n", h=2)
        at_b = rotf[:, 0:256]
        prT = hTf.rearrange("p (b m k n) -> p b m k n", b=2, m=2, k=4)
        oA = xn[:, 0, :].rearrange("p (h n) -> p h n", h=4)
        oS = xn[:, 1, :].rearrange("p (h n) -> p h n", h=4)
        band_flat = arena[0:GRID, 3584:7168]
        band = band_flat.rearrange("p (r u) -> p r u", u=P)
        work = arena[:, 0:3584]
        sel_gate = work[:, 0:256].rearrange("p (t n) -> p t n", t=NT)
        sel = work[:, 256:512].rearrange("p (t n) -> p t n", t=NT)
        comb = work[:, 512:768]
        comb_next = arena[:, 13056:13312]
        cur = work[:, 768:784]
        silu_sb, hid = work[:, 784:1296], work[:, 1296:1808]
        hidT = work[:, 1808:2320].rearrange("p (c n) -> p c n", c=4)
        gotT = work[:, 2320:3344].rearrange("p (k n) -> p k n", k=KD)
        got = arena[:, 11008:12032]
        y_sb = arena[:, 12032:13056]
        junk = arena[:, 3584:4608]
        router_w = kaT.rearrange("p h n -> p (h n)")[:, 0:288].rearrange("p (k n) -> p k n", k=KD)
        rt = kaT.rearrange("p h n -> p (h n)")[:, 288:2048]
        ranks = rt[:, 0:128].rearrange("p (r e) -> p r e", e=NE)
        chosen = rt[:, 128:192].rearrange("p (t e) -> p t e", t=NT)
        lg = rt[:, 192:272].rearrange("p (t n) -> p t n", t=NT)
        r8 = rt[:, 272:272 + 16 * 12].rearrange("p (n t e) -> p n t e", t=NT, e=EG)
        r4 = rt[:, 480:480 + 8 * 6].rearrange("p (n t g) -> p n t g", t=NT, g=NG)
        r1 = rt[:, 544:544 + 2 * 16].rearrange("p (n t) -> p n t", t=NT)
        r32 = rt[:, 600:664].rearrange("p (t e) -> p t e", t=NT)
        extra_f = rt[0:1, 664:696]
        extra_cmp = rt[0:1, 704:960].rearrange("p (e j) -> p e j", j=8)
        extra = ctx.enter_context(nc.sbuf_tensor("extra", [1, NE], I32))
        zeros = rt[:, 960:1088]
        extra_m = rt[0:1, 1088:1104]
        final_g = va.rearrange("p t n -> p (t n)")[:, 0:D]
        vbf = vbn.rearrange("p t n -> p (t n)")
        gate_diag = vbf[:, 0:D].rearrange("p (k n) -> p k n", k=KD)
        gate_sb = vbf[:, D:2 * D]
        res_tmp = vbf[:, 0:D]
        junk2 = arena[:, 2560:3584]
        def lie(start, n):
            return arena[:, start:start + n]

        const2 = lie(7680, n_c2)
        C2 = {n: const2[:, a:a + w] for n, (a, w) in c2.items()}
        low = 7680 + n_c2
        cq = lie(low, 832).rearrange("p (t n) -> p t n", t=NT)
        pool_u = lie(low + 832, 512).rearrange("p (t n) -> p t n", t=NT)
        bqT = lie(low + 1344, 512).rearrange("p (h n) -> p h n", h=2)
        bkT = lie(low + 1856, 512).rearrange("p (h n) -> p h n", h=2)
        bv = lie(low + 2368, 512).rearrange("p (t n) -> p t n", t=NT)
        pool_dT = lie(low + 2880, 512).rearrange("p (c n) -> p c n", c=2)
        pool_w = lie(low + 3392, 128).rearrange("p (c n) -> p c n", c=2)
        st_z = lie(low + 3520, 1536).rearrange("p (m n) -> p m n", m=2)
        rot2a = lie(low + 5056, 256).rearrange("p (h n) -> p h n", h=8)
        rot2b = lie(low + 5312, 256).rearrange("p (h n) -> p h n", h=8)
        key_rot = lie(low + 5568, 64).rearrange("p (t n) -> p t n", t=NT)
        st_e = work[:, 0:1536].rearrange("p (m n) -> p m n", m=2)
        st_s = work[:, 1536:3072].rearrange("p (m n) -> p m n", m=2)
        q_tok = work[:, 0:1536].rearrange("p (t h n) -> p t h n", t=NT, h=8)
        k_tok = work[:, 1536:3072].rearrange("p (t h n) -> p t h n", t=NT, h=8)
        v2 = lie(4608, 1024).rearrange("p (t h n) -> p t h n", t=NT, h=8)
        cqT = lie(5632, 768).rearrange("p (c n) -> p c n", c=3)
        q2T = hTf[:, 0:2048].rearrange("p (h n) -> p h n", h=8)
        k2T = hTf[:, 2048:4096].rearrange("p (h n) -> p h n", h=8)
        probs2 = lie(3584, 1024).rearrange("p (b m n) -> p b m n", b=2, m=2)
        xnf = xn.rearrange("p t d -> p (t d)")
        st_pT = xnf.rearrange("p (h c n) -> p h c n", h=4, c=2)
        prT2 = xnf.rearrange("p (b m c n) -> p b m c n", b=2, m=2, c=2)
        pool_mat = C2["pool"].rearrange("p (g s n) -> p g s n", g=4, s=NT)

        def pr_of(kind):
            return probs1 if kind != "mla" else probs2

        def prT_of(kind):
            return prT if kind != "mla" else prT2

        def mix_of(kind):
            return mixT

        def junk_of(t):
            return junk if t == 0 else junk2
        windows = {}

        def counter(eng, name):
            reg = ctx.enter_context(eng.register(name))
            eng.reg_mov(reg, 0)
            return reg

        block = ctx.enter_context(nc.Block())

        def w_cols(slot, width):
            return ring[:, slot, 0:KD * width].rearrange("p (k n) -> p k n", k=KD)

        def start_piece(sp, slot, sem, piece, layer):
            kind, j = piece
            if kind == "mod":
                src = ins["w_mod"][0].rearrange("(k p) n -> p k n", p=P)[:, :, 512 * j:512 * j + 512]
                sp.dma_start(w_cols(slot, 512), src).then_inc(sem, 16)
            elif kind in ("win", "win2"):
                cols_, width = (WIN_COLS, WIN_WIDTH) if kind == "win" else (WIN2_COLS, WIN2_WIDTH)
                w = ins["w_in"][0] if kind == "win" else ins["w_in_2"][layer]
                at = 0
                for col, n in cols_[j]:
                    sp.dma_start(w_cols(slot, width[j])[:, :, at:at + n],
                                 w.rearrange("(k p) n -> p k n", p=P)[:, :, col:col + n]).then_inc(sem, 16)
                    at += n
            elif kind in ("wout", "wout2"):
                w = ins["w_out"][0] if kind == "wout" else ins["w_out_2"][layer]
                sp.dma_start(ring[:, slot, 0:4 * D].rearrange("p (k n) -> p k n", k=4),
                             w[512 * j:512 * j + 512, :].rearrange("(k p) n -> p k n", p=P)).then_inc(sem, 16)
            elif kind == "mla":
                sp.dma_start(ring[:, slot, 0:1536].rearrange("p (k n) -> p k n", k=2),
                             ins["w_uq_2"][layer].rearrange("(k p) n -> p k n", p=P)).then_inc(sem, 16)
                sp.dma_start(ring[:, slot, 1536:2560], ins["w_ukv_2"][layer]).then_inc(sem, 16)

        up1 = ins["w_expert_up"][0].rearrange("(b e) (k p) n -> b p e k n", e=2, p=P)
        down1 = ins["w_expert_down"][0].rearrange("(b e) (k p) n -> b p e k n", e=2, p=P)

        def expert_loads(sp, plan, which, ups, down):
            nb, _, hidden = batch_of(which)
            base, turns = plan.n, NE // nb
            slots = plan.loop(turns, RING, 2 * len(ups), hidden // P // 2)
            with sp.Fori(0, turns) as turn:
                for j, (slot, sem, _, _) in enumerate(slots):
                    sp.wait_ge(sems["piece_used"], turn * RING + (base + j - RING + 1))
                    if j < 4:
                        v = piece_view(slot, which, False)
                        for u, src in enumerate(ups):
                            for kk in range(2):
                                sp.dma_start(v[:, :, kk, :] if which == 1 else v[:, u, :, kk, :],
                                             src[bass.ds(turn, 1)][0][:, :, 2 * j + kk, :]).then_inc(sem, 16)
                    else:
                        per = hidden // P // 2
                        for kk in range(per):
                            sp.dma_start(piece_view(slot, which, True)[:, :, kk, :],
                                         down[bass.ds(turn, 1)][0][:, :, per * (j - 4) + kk, :]).then_inc(sem, 16)


        def items_of(kind):
            return [(g, t) for g in range(2 if kind == "na" else 4) for t in range(NT)]

        def keys_of(kind, t):
            return P * (t + 1) if kind == "mla" else 4 * P

        def attention_pool(pool, at, kind):
            items = items_of(kind)
            for i, (g, t) in enumerate(items):
                if i >= 2:
                    pool.wait_ge(*at.plus("score", i - 1))
                for m in range(2):
                    r = slice(64 * m, 64 * m + 64)
                    ins_ = pool.tensor_copy(q_pad[r, i % 2, m, :], (qnT if kind == "na" else qaT)[r, g, P * t:P * t + P])
                ins_.then_inc(sems["q_padded"], 1)
            pool.wait_ge(*at("score", len(items)))

        def attention_pe(pe, at, kind):
            items = items_of(kind)

            def scores(i):
                g, t = items[i]
                if i >= 2:
                    pe.wait_ge(*at.plus("exps", i - 1))
                if kind != "mla":
                    pe.wait_ge(*at.plus("q_padded", i + 1))
                for m in range(2):
                    if kind == "mla":
                        q, k = q2T[0:96, 2 * g + m, P * t:P * t + P], k2T[0:96, 2 * g + m, 0:P * (t + 1)]
                    else:
                        k_all = knT if kind == "na" else kaT
                        q, k = q_pad[:, i % 2, m, :], k_all[:, g, :]
                    mm = pe.matmul(ps[2 * (i % 2) + m][:, 0:keys_of(kind, t)], q, k, start=True, stop=True)
                mm.then_inc(sems["score"], 1)

            def turns(i):
                g, t = items[i]
                pe.wait_ge(*at.plus("probs", i + 1))
                lag = 2 if kind == "diff" else 1
                if i >= lag:
                    pe.wait_ge(*at.plus("tr_sb", i + 1 - lag))
                for m in range(1 if kind == "diff" else 2):
                    bank = ps[4 + (i % 2 if kind == "diff" else m)]
                    for c in range(keys_of(kind, t) // P):
                        mm = pe.transpose(bank[:, P * c:P * c + P], pr_of(kind)[:, i % 2, m, P * c:P * c + P], ident)
                mm.then_inc(sems["tr"], 1)

            def values(i):
                g, _ = items[i]
                pe.wait_ge(*at.plus("tr_sb", i + 1))
                if g >= 2:
                    pe.wait_ge(*at.plus("pv_sb", g - 1))
                bank = ps[6 + g % 2]
                for m in range(1 if kind == "diff" else 2):
                    for c in range(2 if kind == "mla" else 4):
                        if kind == "diff":
                            dst, v = bank[:, 0:S], va[:, c, P * g:P * g + P]
                        elif kind == "na":
                            dst, v = bank[64 * m:64 * m + 64, 0:S], vbn[:, c, S + 64 * (2 * g + m):S + 64 * (2 * g + m) + 64]
                        else:
                            dst, v = bank[64 * m:64 * m + 64, P * c:S], v2[:, c, 2 * g + m, :]
                        rhs = prT_of(kind)[:, g % 2, m, c, :]
                        if kind == "mla":
                            rhs = rhs[:, P * c:S]
                        mm = pe.matmul(dst, v, rhs, start=(c == 0), stop=(c == (1 if kind == "mla" else 3)))
                mm.then_inc(sems["pv"], 1)

            scores(0)
            scores(1)
            if kind == "na":
                pe.wait_ge(*at("gla_y"))
            for i in range(len(items)):
                if i + 2 < len(items):
                    scores(i + 2)
                turns(i)
                if i and items[i - 1][1] == NT - 1:
                    values(i - 1)
            values(len(items) - 1)
            for name, n in (("exps", len(items)), ("probs", len(items)), ("tr_sb", len(items)), ("pv_sb", len(items) // 2)):
                pe.wait_ge(*at(name, n))
            if kind != "mla":
                at("q_padded", len(items))

        def attention_act(act, at, kind):
            items = items_of(kind)
            scale = {"na": 1.0, "diff": 0.125, "mla": 96.0 ** -0.5}[kind]

            def exps(i):
                g, t = items[i]
                act.wait_ge(*at.plus("neg_max", i + 1))
                if i >= 2:
                    act.wait_ge(*at.plus("tr", i - 1))
                n = keys_of(kind, t)
                for m in range(2):
                    a = 16 + 2 * (i % 2) + m
                    ins_ = act.activation(pr_of(kind)[:, i % 2, m, 0:n], ps[2 * (i % 2) + m][:, 0:n], ACT.Exp,
                                          bias=cols[:, a:a + 1], scale=scale, accum_out=cols[:, a + 4:a + 5])
                ins_.then_inc(sems["exps"], 1)

            def copies(i):
                g, t = items[i]
                act.wait_ge(*at.plus("tr", i + 1))
                if g >= 2 and t == 0:
                    act.wait_ge(*at.plus("pv", g - 1))
                c = keys_of(kind, t) // P
                for m in range(1 if kind == "diff" else 2):
                    bank = ps[4 + (i % 2 if kind == "diff" else m)]
                    ins_ = act.activation(prT_of(kind)[:, g % 2, m, 0:c, P * t:P * t + P],
                                          bank[:, 0:P * c].rearrange("p (c n) -> p c n", c=c), ACT.Copy)
                ins_.then_inc(sems["tr_sb"], 1)

            exps(0)
            exps(1)
            for i in range(len(items)):
                copies(i)
                if i + 2 < len(items):
                    exps(i + 2)
            at("neg_max", len(items)), at("tr", len(items)), at("pv", len(items) // 2)

        def attention_dve(dve, at, link, kind):
            items = items_of(kind)
            scale = {"na": 1.0, "diff": 0.125, "mla": 96.0 ** -0.5}[kind]

            def maxima(i):
                g, t = items[i]
                dve.wait_ge(*at.plus("score", i + 1))
                b, n = 2 * (i % 2), keys_of(kind, t)
                if kind == "na":
                    link(dve.tensor_tensor(psum[:, b:b + 2, 0:S], psum[:, b:b + 2, 0:S],
                                           nb_bias[:, t, 2 * g:2 * g + 2, :], ALU.add))
                if kind == "mla":
                    link(dve.tensor_tensor(psum[:, b:b + 2, n - P:n], psum[:, b:b + 2, n - P:n],
                                           C2["chunk_mask"].unsqueeze(1).broadcast_to([P, 2, P]), ALU.add))
                a = 16 + b
                link(dve.tensor_reduce(cols[:, a:a + 2], psum[:, b:b + 2, 0:n], AX, ALU.max))
                dve.tensor_scalar(cols[:, a:a + 2], cols[:, a:a + 2], -scale, None, ALU.mult).then_inc(sems["neg_max"], 1)

            def normalise(i):
                dve.wait_ge(*at.plus("exps", i + 1))
                a = 20 + 2 * (i % 2)
                n = keys_of(kind, items[i][1])
                pr = pr_of(kind)[:, i % 2, :, :]
                link(dve.reciprocal(cols[:, a:a + 2], cols[:, a:a + 2]))
                if kind == "diff":
                    link(dve.tensor_scalar(cols[:, a + 1:a + 2], cols[:, a + 1:a + 2], cols[:, 10:11], None, ALU.mult))
                    link(dve.tensor_scalar(pr[:, 0, :], pr[:, 0, :], cols[:, a:a + 1], None, ALU.mult))
                    ins_ = dve.scalar_tensor_tensor(pr[:, 0, :], pr[:, 1, :], cols[:, a + 1:a + 2], pr[:, 0, :],
                                                    ALU.mult, ALU.add)
                else:
                    for m in range(2):
                        ins_ = dve.tensor_scalar(pr[:, m, 0:n], pr[:, m, 0:n], cols[:, a + m:a + m + 1], None, ALU.mult)
                ins_.then_inc(sems["probs"], 1)

            def outputs(g):
                dve.wait_ge(*at.plus("pv", g + 1))
                dst = oA[:, g, :] if kind == "diff" else mix_of(kind)[:, (6 if kind == "na" else 0) + g, :]
                dve.tensor_copy(dst, ps[6 + g % 2][:, 0:S]).then_inc(sems["pv_sb"], 1)

            maxima(0)
            maxima(1)
            for i in range(len(items)):
                normalise(i)
                if i + 2 < len(items):
                    maxima(i + 2)
                if items[i][1] == NT - 1 and items[i][0] >= 1:
                    outputs(items[i][0] - 1)
            outputs(items[-1][0])
            at("score", len(items)), at("exps", len(items)), at("pv", len(items) // 2)

        def out_projection_pe(pe, at, piece_ready, kind, mix):
            for j in (1, 0):
                slot = piece_ready((kind, j))
                w = ring[:, slot, 0:4 * D].rearrange("p (k n) -> p k n", k=4)
                if j == 0:
                    pe.wait_ge(*at("mixed"))
                for t in range(NT):
                    for n in range(2):
                        for k in range(4):
                            mm = pe.matmul(ps[2 * t + n], mix[:, 4 * j + k, P * t:P * t + P],
                                           w[:, k, 512 * n:512 * n + 512], start=(j == 1 and k == 0),
                                           stop=(j == 0 and k == 3))
                    mm.then_inc(sems["out_mm"], 1)
                pe.wait_ge(*at("out_mm", 2))
                pe.sem_inc(sems["piece_used"], 1)

        def gate_diagonals_dve(dve, at, part):
            for k in range(KD):
                ins_ = dve.tensor_scalar(gate_diag[:, k, :], ident, modT[:, KD * part + k, 0:1], None, ALU.mult)
            ins_.then_inc(sems["diag"], 1)

        def gate_broadcast_pe(pe, at, bank):
            pe.wait_ge(*at("diag"))
            for n in range(2):
                mm = pe.matmul(ps[bank + n], ones, gate_diag[:, 4 * n:4 * n + 4, :].rearrange("p k n -> p (k n)"),
                               start=True, stop=True)
            mm.then_inc(sems["gate_bc"], 1)

        def gate_dve(dve, at, link, bank):
            dve.wait_ge(*at("gate_bc"))
            link(dve.tensor_copy(gate_sb, psum[:, bank:bank + 2, :].rearrange("p b n -> p (b n)")))

        def residual_dve(dve, at, link, bank, done, gated=False):
            if done == "out_mm":
                at(done, 2)
            for t in range(NT):
                dve.wait_ge(*at(done))
                src = psum[:, bank + 2 * t:bank + 2 * t + 2, :].rearrange("p b n -> p (b n)")
                if gated:
                    link(dve.tensor_tensor(res_tmp, src, gate_sb, ALU.mult))
                    src = res_tmp
                dve.tensor_tensor(X[:, t, :], X[:, t, :], src, ALU.add).then_inc(sems["resid"], 1)
                dve.wait_ge(*at("resid"))

        def squares_act(act, at):
            for t in range(NT):
                act.wait_ge(*at("resid"))
                ins_ = act.activation(junk_of(t), X[:, t, :], ACT.Square, accum_out=ss[:, t:t + 1])
            ins_.then_inc(sems["sumsq"], 1)
            act.wait_ge(*at("sumsq"))
            act.wait_ge(*at("mean"))
            act.activation(rstd[:, 0:NT], ss[:, 0:NT], ACT.Sqrt).then_inc(sems["sqrt_done"], 1)

        def rstd_dve(dve, at, link):
            dve.wait_ge(*at("sumsq"))
            link(dve.tensor_scalar(ss[:, 0:NT], ss[:, 0:NT], 1.0 / D, EPS, ALU.mult, ALU.add))
            dve.reciprocal(ss[:, 0:NT], ss[:, 0:NT]).then_inc(sems["mean"], 1)
            dve.wait_ge(*at("sqrt_done"))

        def norm_dve(dve, at, link, scale, shift):
            rstd_dve(dve, at, link)
            for t in range(NT):
                dve.tensor_scalar(xn[:, t, :], X[:, t, :], rstd[:, t:t + 1], None, ALU.mult).then_inc(sems["xn"], 1)
            for b in range(2):
                dve.wait_ge(*at.plus("x_T", b + 1))
                for k in (2 * b, 2 * b + 1):
                    src = ps[4 + b][:, S * (k % 2):S * (k % 2) + S]
                    if shift is None:
                        ins_ = dve.tensor_scalar(h2T[:, k, :], src, scale[:, k:k + 1], None, ALU.mult)
                    else:
                        ins_ = dve.tensor_scalar(h2T[:, k, :], src, scale[:, k:k + 1], shift[:, k, 0:1], ALU.mult, ALU.add)
                ins_.then_inc(sems["xT_v"], 1)
            at("x_T", 4)

        def norm_act(act, at, scale, shift):
            squares_act(act, at)
            for b in range(2, 4):
                act.wait_ge(*at.plus("x_T", b + 1))
                for k in (2 * b, 2 * b + 1):
                    src = ps[4 + b][:, S * (k % 2):S * (k % 2) + S]
                    ins_ = act.activation(h2T[:, k, :], src, ACT.Identity, scale=scale[:, k:k + 1],
                                          bias=0.0 if shift is None else shift[:, k, 0:1])
                ins_.then_inc(sems["xT_s"], 1)
            at("x_T", 4)

        def norm_pe(pe, at):
            for t in range(NT):
                pe.wait_ge(*at("xn"))
                for b in range(4):
                    for k in (2 * b, 2 * b + 1):
                        o = S * (k % 2) + P * t
                        mm = pe.transpose(ps[4 + b][:, o:o + P], xn[:, t, P * k:P * k + P], ident)
                    if t == NT - 1:
                        mm.then_inc(sems["x_T"], 1)
            pe.wait_ge(*at("xT_v", 2))
            pe.wait_ge(*at("xT_s", 2))

        def final_dve(dve, at, link):
            rstd_dve(dve, at, link)
            for t in range(NT):
                dve.scalar_tensor_tensor(X[:, t, :], X[:, t, :], rstd[:, t:t + 1], final_g, ALU.mult, ALU.mult)\
                    .then_inc(sems["resid"], 1)
            dve.wait_ge(*at("resid", 2))
            dve.sem_inc(sems["fin_x"], 1)

        def route_pe(pe, at, which):
            pe.wait_ge(*at("router_w", 48 if which == 1 else 64))
            for t in range(NT):
                for k in range(KD):
                    mm = pe.matmul(ps[0][:, 64 * t:64 * t + NG + NE], h2T[:, k, P * t:P * t + P], router_w[:, k, :],
                                   start=(k == 0), stop=(k == KD - 1))
            mm.then_inc(sems["logits"], 1)
            if which == 1:
                gate_broadcast_pe(pe, at, 2)
            pe.wait_ge(*at("route"))
            r = ps[1][:, 0:3 * NE].rearrange("p (n e) -> p n e", e=NE)
            pe.matmul(r[:, 0, :], tri, chosen[:, 0, :], start=True, stop=True)
            pe.matmul(r[:, 1, :], tri, chosen[:, 1, :], start=True, stop=False)
            pe.matmul(r[:, 1, :], ones, chosen[:, 0, :], start=False, stop=True)
            for t in range(NT):
                mm = pe.matmul(r[:, 2, :], ones, chosen[:, t, :], start=(t == 0), stop=(t == 1))
            mm.then_inc(sems["rank_mm"], 1)
            pe.wait_ge(*at("zero_tile"))
            for b in range(4, 8):
                pe.matmul(ps[b], zeros, xn[:, 0, 0:512], start=True, stop=True)

        def route_act(act, at):
            act.wait_ge(*at("lg"))
            act.activation(r4[:, 1, :, :], r4[:, 1, :, :], ACT.Exp).then_inc(sems["lg_exp"], 1)
            act.wait_ge(*at("lg"))
            act.activation(r1[:, 6, :], r1[:, 6, :], ACT.Exp).then_inc(sems["lg_exp"], 1)

        def route_dve(dve, at, link, which):
            spread = lambda x, n: x.unsqueeze(2).broadcast_to([P, NT, n])

            def first_of(x, n, top, mark, where):
                link(dve.tensor_reduce(top, x, AX, ALU.max))
                link(dve.tensor_tensor(where, x, spread(top, n), ALU.is_equal))
                link(dve.scalar_tensor_tensor(where, where, -16.0, iota_of(n), ALU.mult, ALU.add))
                link(dve.tensor_reduce(mark, where, AX, ALU.min))
                link(dve.tensor_tensor(where, where, spread(mark, n), ALU.is_equal))

            def iota_of(n):
                return C0["iota8"][:, 0:n].unsqueeze(1).broadcast_to([P, NT, n])

            if which == 1:
                gate_diagonals_dve(dve, at, 5)
            dve.wait_ge(*at("logits"))
            src = ps[0][:, 0:128].rearrange("p (t n) -> p t n", t=NT)[:, :, 0:NG + NE]
            link(dve.tensor_tensor(lg[:, :, 0:NG + NE], src, router_b.unsqueeze(1).broadcast_to([P, NT, NG + NE]), ALU.add))
            groups = lg[:, :, 0:NG]
            first_of(groups, NG, r1[:, 0, :], r1[:, 1, :], r4[:, 0, :, :])
            dve.tensor_tensor(r4[:, 1, :, :], groups, spread(r1[:, 0, :], NG), ALU.subtract).then_inc(sems["lg"], 1)
            for t in range(NT):
                e3 = lg[:, t, NG:NG + NE].rearrange("p (g e) -> p g e", g=NG)
                ins_ = dve.tensor_tensor(r32[:, t, :].rearrange("p (g e) -> p g e", g=NG), e3,
                                         r4[:, 0, t, :].unsqueeze(2).broadcast_to([P, NG, EG]), ALU.mult)
            link(ins_)
            for t in range(NT):
                ins_ = dve.tensor_reduce(r8[:, 0, t, :], r32[:, t, :].rearrange("p (g e) -> p e g", g=NG), AX, ALU.add)
            link(ins_)
            first_of(r8[:, 0, :, :], EG, r1[:, 3, :], r1[:, 4, :], r8[:, 1, :, :])
            link(dve.scalar_tensor_tensor(r8[:, 2, :, :], r8[:, 1, :, :], -BIG, r8[:, 0, :, :], ALU.mult, ALU.add))
            first_of(r8[:, 2, :, :], EG, r1[:, 5, :], r1[:, 4, :], r8[:, 3, :, :])
            dve.tensor_tensor(r1[:, 6, :], r1[:, 5, :], r1[:, 3, :], ALU.subtract).then_inc(sems["lg"], 1)
            link(dve.tensor_tensor(r8[:, 4, :, :], r8[:, 1, :, :], r8[:, 3, :, :], ALU.add))

            def by_group(dst, t, src):
                return dve.tensor_tensor(dst.rearrange("p (g e) -> p g e", g=NG),
                                         r4[:, 0, t, :].unsqueeze(2).broadcast_to([P, NG, EG]),
                                         src.unsqueeze(1).broadcast_to([P, NG, EG]), ALU.mult)

            for t in range(NT):
                ins_ = by_group(chosen[:, t, :], t, r8[:, 4, t, :])
            ins_.then_inc(sems["route"], 1)
            dve.wait_ge(*at("lg", 2))
            dve.wait_ge(*at("lg_exp", 2))
            link(dve.tensor_reduce(r1[:, 2, :], r4[:, 1, :, :], AX, ALU.add))
            link(dve.reciprocal(r1[:, 2, :], r1[:, 2, :]))
            link(dve.tensor_scalar(r1[:, 7, :], r1[:, 6, :], 1.0, None, ALU.add))
            link(dve.reciprocal(r1[:, 7, :], r1[:, 7, :]))
            link(dve.tensor_tensor(r1[:, 7, :], r1[:, 7, :], r1[:, 2, :], ALU.mult))
            link(dve.tensor_tensor(r1[:, 8, :], r1[:, 7, :], r1[:, 6, :], ALU.mult))
            link(dve.tensor_tensor(r8[:, 5, :, :], r8[:, 1, :, :], spread(r1[:, 7, :], EG), ALU.mult))
            link(dve.tensor_tensor(r8[:, 6, :, :], r8[:, 3, :, :], spread(r1[:, 8, :], EG), ALU.mult))
            link(dve.tensor_tensor(r8[:, 5, :, :], r8[:, 5, :, :], r8[:, 6, :, :], ALU.add))
            for t in range(NT):
                ins_ = by_group(ranks[:, NT + t, :], t, r8[:, 5, t, :])
            link(ins_)
            dve.wait_ge(*at("route"))
            if which == 1:
                gate_dve(dve, at, link, 2)
            dve.wait_ge(*at("rank_mm"))
            r = ps[1][:, 0:3 * NE].rearrange("p (n e) -> p n e", e=NE)
            link(dve.scalar_tensor_tensor(ranks[:, 0:NT, :], r[:, 0:NT, :], 1.0, chosen, ALU.add, ALU.mult))
            link(dve.tensor_scalar(ranks[:, 0:NT, :], ranks[:, 0:NT, :], -1.0, None, ALU.add))
            nb, w, _ = batch_of(which)
            link(dve.tensor_scalar(extra_f, r[0:1, 2, :], 1.0 / w, None, ALU.mult))
            link(dve.tensor_tensor(extra_cmp, extra_f.unsqueeze(2).broadcast_to([1, NE, 8]),
                                   C0[f"step{which}"][0:1, :].unsqueeze(1).broadcast_to([1, NE, 8]), ALU.is_gt))
            link(dve.tensor_reduce(extra_f, extra_cmp, AX, ALU.add))
            if which == 1:
                link(dve.tensor_copy(extra[:, 0:NE], extra_f))
            else:
                link(dve.tensor_reduce(extra_m[:, 0:NE // nb], extra_f.rearrange("p (b e) -> p b e", e=nb), AX, ALU.max))
                link(dve.tensor_copy(extra[:, 0:NE // nb], extra_m[:, 0:NE // nb]))
            dve.sem_inc(sems["ranked"], 1)

        def batch_of(which):
            return (2, P // 2, 512) if which == 1 else (4, P // 4, 256)

        def each_batch(eng, at, which, round_, before=None):
            nb = batch_of(which)[0]
            eng.wait_ge(*at("ranked"))
            with eng.Fori(0, NE // nb) as turn:
                for alone in range(nb) if which == 1 else (None,):
                    if before:
                        before(turn, alone)
                    at_ = turn if alone is None else turn * nb + alone
                    n = eng.value_load(extra[0:1, bass.ds(at_, 1)], min_val=0, max_val=7)
                    with eng.If(n > 0):
                        with eng.Fori(0, n):
                            round_(turn, False, alone)
                round_(turn, True, None)

        def piece_view(slot, which, down):
            nb = batch_of(which)[0]
            v = ring[:, slot, :]
            if down:
                return v.rearrange("p (e k n) -> p e k n", e=nb, n=D)
            if which == 1:
                return v.rearrange("p (e k n) -> p e k n", e=nb, k=2)
            return v.rearrange("p (u e k n) -> p u e k n", u=2, e=nb, k=2)

        def experts_pe(pe, at, plan, which, part):
            route_pe(pe, at, which)
            win = windows["pe"]
            nb, w, hidden = batch_of(which)
            chunks = hidden // P
            slots = plan.loop(NE // nb, RING, 2 if which == 1 else 4, chunks // 2)
            pe.sem_inc(sems["w_y"], 1)

            def combine(n, t):
                return pe.matmul(ps[4 + 2 * t + n], comb[:, P * t:P * t + P], y_sb[:, 512 * n:512 * n + 512],
                                 start=False, stop=True, skip_group_check=True)

            def round_(turn, last, alone):
                who = [(e, slice(w * e, w * e + w)) for e in range(nb)] if alone is None else [(alone, slice(0, P))]
                pe.reg_add(win, win, 1)
                v = pe.snap(win)
                pe.wait_ge(sems["w_sel"], v)
                for n in range(2):
                    for t in range(NT):
                        mm = pe.matmul(ps[2 + n], sel[:, t, :], xn[:, t, 512 * n:512 * n + 512],
                                       start=(t == 0), stop=(t == NT - 1))
                    mm.then_inc(sems["w_g0" if n == 0 else "w_g1"], 1)
                pe.wait_ge(sems["w_ysb_s"], v + part)
                pe.wait_ge(sems["w_got_s"], v)
                for k in range(4):
                    mm = pe.transpose(ps[0][:, P * k:P * k + P], got[:, P * k:P * k + P], ident)
                mm.then_inc(sems["w_gt0"], 1)
                pe.wait_ge(sems["w_selg"], v)
                for t in range(NT):
                    mm = pe.transpose(ps[2][:, P * t:P * t + P], sel_gate[:, t, :], ident)
                mm.then_inc(sems["w_ct"], 1)
                pe.wait_ge(sems["w_ysb_v"], v + part)
                pe.wait_ge(sems["w_got_v"], v)
                for k in range(4, KD):
                    mm = pe.transpose(ps[1][:, P * (k - 4):P * (k - 4) + P], got[:, P * k:P * k + P], ident)
                mm.then_inc(sems["w_gt1"], 1)
                pe.wait_ge(sems["w_comb_sb"], v + part)
                combine(0, 0)
                pe.wait_ge(sems["w_ct_sb"], v + (part + 1))
                for i, (slot, sem, base, step) in enumerate(slots[0:4]):
                    if i % 2 == 0:
                        pe.wait_ge(sems["w_xg_v" if i == 0 else "w_xg_s"], v)
                    pe.wait_ge(sem, turn * step + (base + step))
                    view = piece_view(slot, which, False)
                    for kk in range(2):
                        k = 2 * i + kk
                        for n in range(2 if which == 1 else 1):
                            for e, its in who:
                                out_ = ps[2 + n][its, :]
                                if which == 1:
                                    rhs = view[:, e, kk, 512 * n:512 * n + 512]
                                else:
                                    rhs = view[:, :, e, kk, :]
                                    out_ = out_.rearrange("p (u n) -> p u n", u=2)
                                mm = pe.matmul(out_, gotT[:, k, its], rhs, start=(k == 0), stop=(k == KD - 1))
                    if i < 3:
                        if last:
                            mm.then_inc(sems["piece_used"], 1)
                    else:
                        mm.then_inc(sems["w_up"], 1)
                combine(0, 1)
                combine(1, 0)
                pe.wait_ge(sems["w_hid"], v)
                for c in range(chunks):
                    mm = pe.transpose(ps[2 + 2 * c // chunks][:, P * c:P * c + P], hid[:, P * c:P * c + P], ident)
                    if c == chunks // 2 - 1:
                        mm.then_inc(sems["w_ht0"], 1)
                mm.then_inc(sems["w_ht1"], 1)
                if last:
                    pe.sem_inc(sems["piece_used"], 1)
                for i, (slot, sem, base, step) in enumerate(slots[4:6]):
                    pe.wait_ge(sems[f"w_hsb{i}"], v)
                    pe.wait_ge(sem, turn * step + (base + step))
                    view = piece_view(slot, which, True)
                    per = chunks // 2
                    for kk in range(per):
                        k = per * i + kk
                        for n in range(2):
                            for e, its in who:
                                mm = pe.matmul(ps[n][its, :], hidT[:, k, its],
                                               view[:, e, kk, 512 * n:512 * n + 512], start=(k == 0), stop=(k == chunks - 1))
                    if last:
                        mm.then_inc(sems["piece_used"], 1)
                combine(1, 1).then_inc(sems["w_y"], 1)

            each_batch(pe, at, which, round_)
            v = pe.snap(win)
            for name in ("w_ysb_s", "w_ysb_v", "w_comb_sb"):
                pe.wait_ge(sems[name], v + (part + 1))
            for t in range(NT):
                for n in range(2):
                    mm = combine(n, t)
                mm.then_inc(sems["moe_mm"], 1)

        def experts_act(act, at, which, part, scale, shift):
            route_act(act, at)
            win = windows["act"]
            hidden = batch_of(which)[2]

            def outputs(value):
                act.wait_ge(sems["w_y"], value)
                act.activation(y_sb[:, 0:512], ps[0], ACT.Copy).then_inc(sems["w_ysb_s"], 1)

            def round_(turn, last, alone):
                act.reg_add(win, win, 1)
                v = act.snap(win)
                outputs(v + part)
                act.wait_ge(sems["w_g0"], v)
                act.activation(got[:, 0:512], ps[2], ACT.Copy).then_inc(sems["w_got_s"], 1)
                act.wait_ge(sems["w_gt1"], v)
                for k in range(4, KD):
                    ins_ = act.activation(gotT[:, k, :], ps[1][:, P * (k - 4):P * (k - 4) + P], ACT.Identity,
                                          scale=scale[:, k:k + 1], bias=0.0 if shift is None else shift[:, k, 0:1])
                ins_.then_inc(sems["w_xg_s"], 1)
                act.wait_ge(sems["w_up"], v)
                act.activation(silu_sb[:, 0:hidden], ps[2][:, 0:hidden], ACT.Silu).then_inc(sems["w_silu"], 1)
                half = hidden // 2
                for i in range(2):
                    act.wait_ge(sems[f"w_ht{i}"], v)
                    act.activation(hidT.rearrange("p c n -> p (c n)")[:, half * i:half * i + half],
                                   ps[2 + i][:, half * i:half * i + half], ACT.Copy).then_inc(sems[f"w_hsb{i}"], 1)

            each_batch(act, at, which, round_)
            outputs(act.snap(win) + (part + 1))

        def experts_dve(dve, at, link, which, part, scale, shift):
            win, currents = windows["dve"], windows["cur"]
            nb, w, hidden = batch_of(which)
            now = cur[:, 0:4 * nb].rearrange("p (r e) -> p r e", e=nb)
            now1 = cur[:, 12:16].rearrange("p (r e) -> p r e", e=1)
            slot_ids = C0["slot64" if which == 1 else "slot32"].rearrange("p (e s) -> p e s", e=nb)
            dve.memset(comb_next, 0.0).then_inc(sems["w_ct_sb"], 1)

            def outputs(value):
                dve.wait_ge(sems["w_y"], value)
                dve.tensor_copy(y_sb[:, 512:1024], ps[1]).then_inc(sems["w_ysb_v"], 1)
                dve.wait_ge(sems["w_ct_sb"], value)
                dve.tensor_copy(comb, comb_next).then_inc(sems["w_comb_sb"], 1)

            def current(ins_):
                ins_.then_inc(sems["w_cur"], 1)
                dve.reg_add(currents, currents, 1)
                dve.wait_ge(sems["w_cur"], dve.snap(currents))

            def round_(turn, last, alone):
                dve.reg_add(win, win, 1)
                v = dve.snap(win)
                n, width = (nb, w) if alone is None else (1, P)
                it = now if alone is None else now1
                ids = slot_ids if alone is None else C0["slot128"].unsqueeze(1)
                if last:
                    current(dve.tensor_copy(now, ranks[:, :, bass.ds(turn * nb, nb)]))
                else:
                    current(dve.tensor_scalar(it[:, 0:NT, :], it[:, 0:NT, :], -float(width), None, ALU.add))
                for t in range(NT):
                    s3 = sel[:, t, :].rearrange("p (e s) -> p e s", e=n)
                    ins_ = dve.tensor_tensor(s3, ids, it[:, t, :].unsqueeze(2).broadcast_to([P, n, width]), ALU.is_equal)
                ins_.then_inc(sems["w_sel"], 1)
                dve.wait_ge(sems["w_sel"], v)
                for t in range(NT):
                    s3 = sel[:, t, :].rearrange("p (e s) -> p e s", e=n)
                    g3 = sel_gate[:, t, :].rearrange("p (e s) -> p e s", e=n)
                    ins_ = dve.tensor_tensor(g3, s3, it[:, NT + t, :].unsqueeze(2).broadcast_to([P, n, width]), ALU.mult)
                ins_.then_inc(sems["w_selg"], 1)
                outputs(v + part)
                dve.wait_ge(sems["w_g1"], v)
                dve.tensor_copy(got[:, 512:1024], ps[3]).then_inc(sems["w_got_v"], 1)
                dve.wait_ge(sems["w_gt0"], v)
                for k in range(4):
                    src = ps[0][:, P * k:P * k + P]
                    if shift is None:
                        ins_ = dve.tensor_scalar(gotT[:, k, :], src, scale[:, k:k + 1], None, ALU.mult)
                    else:
                        ins_ = dve.tensor_scalar(gotT[:, k, :], src, scale[:, k:k + 1], shift[:, k, 0:1], ALU.mult, ALU.add)
                ins_.then_inc(sems["w_xg_v"], 1)
                dve.wait_ge(sems["w_ct"], v)
                dve.wait_ge(sems["w_comb_sb"], v + part)
                dve.tensor_copy(comb_next, ps[2][:, 0:S]).then_inc(sems["w_ct_sb"], 1)
                dve.wait_ge(sems["w_silu"], v)
                up_ = ps[3] if which == 1 else ps[2][:, hidden:2 * hidden]
                dve.tensor_tensor(hid[:, 0:hidden], silu_sb[:, 0:hidden], up_, ALU.mult).then_inc(sems["w_hid"], 1)

            def begin(turn, alone):
                if alone is None:
                    current(dve.tensor_copy(now, ranks[:, :, bass.ds(turn * nb, nb)]))
                else:
                    one = bass.ds(turn * nb + alone, 1)
                    dve.tensor_copy(now1[:, NT:, :], ranks[:, NT:, one])
                    current(dve.tensor_scalar(now1[:, 0:NT, :], ranks[:, 0:NT, one], float(P - w), None, ALU.add))

            each_batch(dve, at, which, round_, begin)
            outputs(dve.snap(win) + (part + 1))


        def emptied_before(at_engine, unit):
            if unit >= 4:
                who = UNITS[unit - 4][4]
                at_engine.wait_ge(sems["unit_" + who], emptied(UNITS, unit - 3, who))

        score_items = [(h, t) for h in range(4) for t in range(NT)]
        pair_items = [(h, t) for h in range(2) for t in range(NT)]

        def context_values(pe, at, h):
            pe.wait_ge(*at("c_sb"))
            o = ps[7][64 * (h % 2):64 * (h % 2) + 64, S * (h // 2):S * (h // 2) + S]
            for s in range(2):
                mm = pe.matmul(o, vbn[:, NT + s, 64 * h:64 * h + 64], ctT[:, h % 2, s, :],
                               start=(s == 0 and h < 2), stop=False, skip_group_check=True)
            mm.then_inc(sems["c_used"], 1)

        def diagonal(rows_, h, off):
            base = atT[rows_, h, :, :]
            return bass.AP(tensor=base.tensor, offset=base.offset + off, ap=[base.ap[0], (S + P, 2), (1, 32)])

        def second_block_loads(sp, plan, straight):
            for layer in range(2):
                straight(second_pieces, layer)
                gate, up, down = (ins[n][layer].rearrange("g (b e) (k p) n -> (g b) p e k n", p=P, e=4)
                                  for n in ("w_gate_2", "w_up_2", "w_down_2"))
                expert_loads(sp, plan, 2, (gate, up), down)

        def second_block_pool(pool, at):
            pool.wait_ge(*at("fin_x"))
            pool.dma_start(const2, ins["const2"]).then_inc(sems["const2"], 16)
            for layer in range(2):
                for m in range(2):
                    pool.dma_start(pool_w[64 * m:64 * m + 64, :, :], ins["pool_w_2"][layer]
                                   .rearrange("(c m) k n -> m k c n", m=2)[m]).then_inc(sems["pool_w"], 16)
                pool.wait_ge(*at("mixed"))
                for name, dst in (("w_group_2", router_w[:, :, 0:NG]), ("w_expert_2", router_w[:, :, NG:])):
                    pool.dma_start(dst, ins[name][layer].rearrange("(k p) n -> p k n", p=P)).then_inc(sems["router_w"], 16)
                for name, dst in (("b_group_2", router_b[:, 0:NG]), ("b_expert_2", router_b[:, NG:])):
                    pool.dma_start(dst, ins[name][layer:layer + 1, :].to_broadcast([P, dst.shape[1]]))\
                        .then_inc(sems["router_w"], 16)
                pool.memset(zeros, 0.0).then_inc(sems["zero_tile"], 1)
            pool.dma_start(final_g, ins["final_g_2"].rearrange("(o n) -> o n", o=1).to_broadcast([P, D]))\
                .then_inc(sems["final_gain"], 16)
            pool.wait_ge(*at("fin_x"))
            pool.dma_start(out[0].rearrange("(t p) d -> p t d", p=P), X).then_inc(sems["written"], 16)
            pool.wait_ge(sems["written"], 16)

        def second_block_pe(pe, at, plan, piece_ready):
            for layer in range(2):
                norm_pe(pe, at)
                slot = piece_ready(("win2", 0))
                w = w_cols(slot, WIN2_WIDTH[0])
                for part in range(2):
                    for c in range(2):
                        for k in range(KD):
                            col = 256 * part + P * c
                            mm = pe.matmul(ps[4 + part][:, S * c:S * c + S], w[:, k, col:col + P], h2T[:, k, :],
                                           start=(k == 0), stop=(k == KD - 1))
                    mm.then_inc(sems["p2_mm"], 1)
                pe.wait_ge(*at("p2_mm", 2))
                pe.sem_inc(sems["piece_used"], 1)
                slot = piece_ready(("win2", 1))
                w = w_cols(slot, WIN2_WIDTH[1])

                def tokens_mm(part):
                    for t in range(NT):
                        for k in range(KD):
                            mm = pe.matmul(ps[6 + part][:, S * t:S * t + S], h2T[:, k, P * t:P * t + P],
                                           w[:, k, S * part:S * part + S], start=(k == 0), stop=(k == KD - 1))
                    mm.then_inc(sems["p2_mm"], 1)

                tokens_mm(0)
                pe.wait_ge(*at("p2_s"))
                pe.wait_ge(*at("p2_v"))
                for t in range(NT):
                    for m in range(2):
                        for hp in range(2):
                            n = P * (t + 1)
                            r = slice(64 * m, 64 * m + 64)
                            mm = pe.matmul(ps[2 * t + m][:, n * hp:n * hp + n], bqT[r, hp, P * t:P * t + P],
                                           bkT[r, hp, 0:n], start=True, stop=True)
                mm.then_inc(sems["st_mm"], 1)
                tokens_mm(1)
                pe.wait_ge(*at("p2_mm", 2))
                pe.sem_inc(sems["piece_used"], 1)
                pe.wait_ge(*at("p2_v"))
                if layer == 0:
                    pe.wait_ge(sems["const2"], 16)
                for g in range(4):
                    for s in range(NT):
                        mm = pe.matmul(ps[6][64 * (g % 2):64 * (g % 2) + 64, S * (g // 2):S * (g // 2) + S],
                                       pool_u[:, s, 64 * g:64 * g + 64], pool_mat[:, g, s, :],
                                       start=(s == 0), stop=(s == 1))
                mm.then_inc(sems["pool_d"], 1)
                slot = piece_ready(("win2", 2))
                w = w_cols(slot, WIN2_WIDTH[2])
                for t in range(NT):
                    for k in range(KD):
                        mm = pe.matmul(ps[4 + t][:, 0:416], h2T[:, k, P * t:P * t + P], w[:, k, 0:416],
                                       start=(k == 0), stop=(k == KD - 1))
                    mm.then_inc(sems["p2_mm"], 1)
                pe.wait_ge(*at("p2_mm", 2))
                pe.sem_inc(sems["piece_used"], 1)
                pe.wait_ge(*at("st_a"))
                for b, (t, c) in enumerate(((0, 0), (1, 0), (1, 1))):
                    for h in range(4):
                        mm = pe.transpose(ps[b][:, P * h:P * h + P], st_block(st_e, h, t)[:, P * c:P * c + P], ident)
                mm.then_inc(sems["st_T"], 1)
                pe.wait_ge(*at("p2_v"))
                pe.wait_ge(*at("pool_ds"))
                pe.wait_ge(*at("pool_w", 32))
                for g in range(4):
                    r = slice(64 * (g % 2), 64 * (g % 2) + 64)
                    mm = pe.matmul(ps[7][r, S * (g // 2):S * (g // 2) + S], pool_w[r, g // 2, :], pool_dT[r, g // 2, :],
                                   start=True, stop=True)
                mm.then_inc(sems["pool_y"], 1)
                pe.wait_ge(*at("st_Ts"))
                for h in range(4):
                    m, hp = h % 2, h // 2
                    o = ps[6][64 * m:64 * m + 64, S * hp:S * hp + S]
                    pe.matmul(o, bv[:, 0, 64 * h:64 * h + 64], st_pT[:, h, 0, :], start=True, stop=False,
                              skip_group_check=True)
                    mm = pe.matmul(o[:, P:S], bv[:, 1, 64 * h:64 * h + 64], st_pT[:, h, 1, P:S], start=False, stop=True,
                                   skip_group_check=True)
                mm.then_inc(sems["st_pv"], 1)
                pe.wait_ge(*at("p2_s", 2))
                pe.wait_ge(*at("cq_n"))
                for t in range(NT):
                    for c in range(3):
                        mm = pe.transpose(ps[4 + t][:, P * c:P * c + P], cq[:, t, P * c:P * c + P], ident)
                mm.then_inc(sems["cq_T"], 1)
                pe.wait_ge(*at("st_o"))
                pe.wait_ge(*at("pool_o"))
                pe.wait_ge(*at("cq_Ts"))
                slot = piece_ready(("mla", 0))
                uq = ring[:, slot, 0:1536].rearrange("p (k n) -> p k n", k=2)
                ukv = ring[:, slot, 1536:2560]
                for t in range(NT):
                    for b, (a, n) in enumerate(((0, 512), (512, 256))):
                        for k in range(2):
                            mm = pe.matmul(ps[4 * t + b][:, 0:n], cqT[:, k, P * t:P * t + P], uq[:, k, a:a + n],
                                           start=(k == 0), stop=(k == 1))
                    mm.then_inc(sems["q_mm"], 1)
                    for b in range(2):
                        mm = pe.matmul(ps[4 * t + 2 + b], cqT[:, 2, P * t:P * t + P], ukv[:, 512 * b:512 * b + 512],
                                       start=True, stop=True)
                    mm.then_inc(sems["kv_mm"], 1)
                pe.wait_ge(*at("kv_mm", 2))
                pe.sem_inc(sems["piece_used"], 1)
                for t in range(NT):
                    pe.wait_ge(*at("q_sb"))
                    pe.wait_ge(*at("kv_sb"))
                    for b in range(4):
                        src = q_tok if b < 2 else k_tok
                        for h in range(4):
                            mm = pe.transpose(ps[4 * t + b][0:96, P * h:P * h + P], src[:, t, 4 * (b % 2) + h, :], ident)
                        mm.then_inc(sems["head_T"], 1)
                pe.wait_ge(*at("head_v", 4))
                pe.wait_ge(*at("head_s", 4))
                attention_pe(pe, at, "mla")
                out_projection_pe(pe, at, piece_ready, "wout2", mixT)
                norm_pe(pe, at)
                experts_pe(pe, at, plan, 2, 1 + layer)

        def st_block(x, h, t):
            o = (P * (h // 2)) if t == 0 else (2 * P + S * (h // 2))
            return x[:, h % 2, o:o + P * (t + 1)]

        def second_block_act(act, at, link):
            for layer in range(2):
                norm_act(act, at, PT["norm1_g_2"][:, KD * layer:KD * layer + KD], None)
                act.wait_ge(*at("p2_mm"))
                act.activation(bqT.rearrange("p h n -> p (h n)"), ps[4], ACT.Copy, scale=0.125).then_inc(sems["p2_s"], 1)
                act.wait_ge(*at("p2_s"))
                act.wait_ge(*at("st_zb"))
                link(act.activation(st_e, st_e, ACT.Exp))
                act.activation(st_e, st_e, ACT.Ln, bias=1.0).then_inc(sems["st_ln"], 1)
                act.wait_ge(*at("st_x"))
                act.activation(st_e, st_z, ACT.Exp).then_inc(sems["st_a"], 1)
                act.wait_ge(*at("pool_d"))
                act.activation(pool_dT.rearrange("p c n -> p (c n)"), ps[6], ACT.Copy).then_inc(sems["pool_ds"], 1)
                at("p2_mm", 3)
                for t in range(NT):
                    act.wait_ge(*at("p2_mm"))
                    act.activation(cq[:, t, :], ps[4 + t][:, 0:416], ACT.Copy).then_inc(sems["p2_s"], 1)
                    act.wait_ge(*at("p2_s"))
                    link(act.activation(junk[:, 0:256], cq[:, t, 0:256], ACT.Square, accum_out=cols[:, 32 + t:33 + t]))
                    link(act.activation(junk[:, 0:128], cq[:, t, 256:384], ACT.Square, accum_out=cols[:, 34 + t:35 + t]))
                act.sem_inc(sems["cq_sq"], 1)
                act.wait_ge(*at("st_T"))
                for b, (t, c) in enumerate(((0, 0), (1, 0), (1, 1))):
                    ins_ = act.activation(st_pT[:, :, c, P * t:P * t + P], ps[b].rearrange("p (h n) -> p h n", h=4), ACT.Copy)
                ins_.then_inc(sems["st_Ts"], 1)
                act.wait_ge(*at("cq_mean"))
                act.activation(cols[:, 32:36], cols[:, 32:36], ACT.Sqrt).then_inc(sems["cq_sqrt"], 1)
                for t in range(NT):
                    act.wait_ge(*at("kv_mm"))
                    kv = psum[:, 4 * t + 2:4 * t + 4, :].rearrange("p b n -> p (b n)").rearrange("p (h u n) -> p h u n", h=8, u=2)
                    act.activation(k_tok[:, t, :, 0:64], kv[:, :, 0, :], ACT.Copy)
                    act.activation(v2[:, t, :, :], kv[:, :, 1, :], ACT.Copy).then_inc(sems["kv_sb"], 1)
                for t in range(NT):
                    for b in range(2):
                        act.wait_ge(*at.plus("head_T", 4 * t + b + 1))
                        act.activation(q2T[0:96, 4 * b:4 * b + 4, P * t:P * t + P],
                                       ps[4 * t + b][0:96, :].rearrange("p (h n) -> p h n", h=4), ACT.Copy)\
                            .then_inc(sems["head_s"], 1)
                at("head_T", 8)
                attention_act(act, at, "mla")
                norm_act(act, at, PT["norm2_g_2"][:, KD * layer:KD * layer + KD], None)
                experts_act(act, at, 2, 1 + layer, PT["norm2_g_2"][:, KD * layer:KD * layer + KD], None)
            squares_act(act, at)

        def second_block_dve(dve, at, link):
            for layer in range(2):
                norm_dve(dve, at, link, PT["norm1_g_2"][:, KD * layer:KD * layer + KD], None)
                dve.wait_ge(*at("p2_mm", 2))
                dve.tensor_copy(bkT.rearrange("p h n -> p (h n)"), ps[5]).then_inc(sems["p2_v"], 1)
                dve.wait_ge(*at("p2_mm"))
                dve.tensor_copy(pool_u.rearrange("p t n -> p (t n)"), ps[6]).then_inc(sems["p2_v"], 1)
                if layer == 0:
                    dve.wait_ge(sems["const2"], 16)
                dve.wait_ge(*at("st_mm"))
                mask = C2["strict_mask"].unsqueeze(1).broadcast_to([P, 2, P])
                for m in range(2):
                    z0 = st_z[:, m, 0:2 * P].rearrange("p (h n) -> p h n", h=2)
                    z1 = st_z[:, m, 2 * P:].rearrange("p (h n) -> p h n", h=2)
                    p1 = ps[2 + m].rearrange("p (h n) -> p h n", h=2)
                    dve.tensor_tensor(z0, ps[m][:, 0:2 * P].rearrange("p (h n) -> p h n", h=2), mask, ALU.add)
                    dve.tensor_copy(z1[:, :, 0:P], p1[:, :, 0:P])
                    ins_ = dve.tensor_tensor(z1[:, :, P:2 * P], p1[:, :, P:2 * P], mask, ALU.add)
                link(ins_)
                dve.scalar_tensor_tensor(st_e, st_z, -1.0, st_z, ALU.mult, ALU.min).then_inc(sems["st_zb"], 1)
                dve.wait_ge(*at("st_ln"))
                link(dve.scalar_tensor_tensor(st_e, st_z, 0.0, st_e, ALU.max, ALU.add))
                for t in range(NT):
                    for h in range(4):
                        n = P * (t + 1)
                        ins_ = dve.tensor_tensor_scan(st_block(st_s, h, t)[:, ::-1], ones[:, 0:1].broadcast_to([P, n]),
                                                      st_block(st_e, h, t)[:, ::-1], 0.0, ALU.mult, ALU.add)
                link(ins_)
                dve.tensor_tensor(st_z, st_z, st_s, ALU.subtract).then_inc(sems["st_x"], 1)
                dve.wait_ge(*at("p2_mm"))
                dve.tensor_copy(bv.rearrange("p t n -> p (t n)"), ps[7]).then_inc(sems["p2_v"], 1)
                at("p2_mm", 2)
                dve.wait_ge(*at("cq_sq"))
                link(dve.tensor_scalar(cols[:, 32:34], cols[:, 32:34], 1.0 / 256, EPS, ALU.mult, ALU.add))
                link(dve.tensor_scalar(cols[:, 34:36], cols[:, 34:36], 1.0 / 128, EPS, ALU.mult, ALU.add))
                dve.reciprocal(cols[:, 32:36], cols[:, 32:36]).then_inc(sems["cq_mean"], 1)
                for t in range(NT):
                    cos = C2["rope_cos"][:, 32 * t:32 * t + 32]
                    sin = C2["rope_sin"][:, 32 * t:32 * t + 32]
                    kr = cq[:, t, 384:416]
                    for b in range(2):
                        dve.tensor_tensor(rot2b[:, t, 16 * b:16 * b + 16], kr[:, 16 - 16 * b:32 - 16 * b],
                                          sin[:, 16 * b:16 * b + 16], ALU.mult)
                    link(dve.tensor_tensor(rot2a[:, t, :], kr, cos, ALU.mult))
                    link(dve.tensor_tensor(key_rot[:, t, :], rot2a[:, t, :], rot2b[:, t, :], ALU.add))
                dve.wait_ge(*at("cq_sqrt"))
                for t in range(NT):
                    dve.tensor_scalar(cq[:, t, 0:256], cq[:, t, 0:256], cols[:, 32 + t:33 + t], None, ALU.mult)
                    ins_ = dve.tensor_scalar(cq[:, t, 256:384], cq[:, t, 256:384], cols[:, 34 + t:35 + t], None, ALU.mult)
                ins_.then_inc(sems["cq_n"], 1)
                dve.wait_ge(*at("pool_y"))
                for c in range(2):
                    ins_ = dve.tensor_scalar(mixT[:, 6 + c, :], ps[7][:, S * c:S * c + S],
                                             PT["pool_scale_2"][:, 2 * layer + c:2 * layer + c + 1], None, ALU.mult)
                ins_.then_inc(sems["pool_o"], 1)
                dve.wait_ge(*at("st_pv"))
                dve.tensor_copy(mixT[:, 4:6, :].rearrange("p c n -> p (c n)"), ps[6]).then_inc(sems["st_o"], 1)
                dve.wait_ge(*at("cq_T"))
                for t in range(NT):
                    for c in range(3):
                        g = PT["q_norm_g_2"][:, 2 * layer + c:2 * layer + c + 1] if c < 2 else PT["kv_norm_g_2"][:, layer:layer + 1]
                        ins_ = dve.tensor_scalar(cqT[:, c, P * t:P * t + P], ps[4 + t][:, P * c:P * c + P], g, None, ALU.mult)
                ins_.then_inc(sems["cq_Ts"], 1)
                for t in range(NT):
                    dve.wait_ge(*at("q_mm"))
                    q = psum[:, 4 * t:4 * t + 2, :].rearrange("p b n -> p (b n)")[:, 0:768].rearrange("p (h n) -> p h n", h=8)
                    cos = C2["rope_cos"][:, 32 * t:32 * t + 32].unsqueeze(1).broadcast_to([P, 8, 32])
                    sin = C2["rope_sin"][:, 32 * t:32 * t + 32]
                    dve.tensor_copy(q_tok[:, t, :, 0:64], q[:, :, 0:64])
                    for b in range(2):
                        dve.tensor_tensor(rot2b[:, :, 16 * b:16 * b + 16], q[:, :, 80 - 16 * b:96 - 16 * b],
                                          sin[:, 16 * b:16 * b + 16].unsqueeze(1).broadcast_to([P, 8, 16]), ALU.mult)
                    dve.tensor_copy(k_tok[:, t, :, 64:96], key_rot[:, t, :].unsqueeze(1).broadcast_to([P, 8, 32]))
                    link(dve.tensor_tensor(rot2a, q[:, :, 64:96], cos, ALU.mult))
                    dve.tensor_tensor(q_tok[:, t, :, 64:96], rot2a, rot2b, ALU.add).then_inc(sems["q_sb"], 1)
                    dve.wait_ge(*at("q_sb"))
                for t in range(NT):
                    for b in range(2):
                        dve.wait_ge(*at.plus("head_T", 4 * t + 2 + b + 1))
                        dve.tensor_copy(k2T[0:96, 4 * b:4 * b + 4, P * t:P * t + P],
                                        ps[4 * t + 2 + b][0:96, :].rearrange("p (h n) -> p h n", h=4))\
                            .then_inc(sems["head_v"], 1)
                at("head_T", 8)
                attention_dve(dve, at, link, "mla")
                dve.sem_inc(sems["mixed"], 1)
                residual_dve(dve, at, link, 0, "out_mm")
                norm_dve(dve, at, link, PT["norm2_g_2"][:, KD * layer:KD * layer + KD], None)
                dve.wait_ge(*at("router_w", 64))
                route_dve(dve, at, link, 2)
                experts_dve(dve, at, link, 2, 1 + layer, PT["norm2_g_2"][:, KD * layer:KD * layer + KD], None)
                residual_dve(dve, at, link, 4, "moe_mm")
            dve.wait_ge(sems["final_gain"], 16)
            final_dve(dve, at, link)

        @block.sync
        def _(sp):
            plan = Ring(sems)

            def straight(pieces, layer):
                for piece in pieces:
                    if plan.n >= RING:
                        sp.wait_ge(sems["piece_used"], plan.n - RING + 1)
                    slot, sem, _ = plan.place(dmas_of(piece))
                    start_piece(sp, slot, sem, piece, layer)

            sp.dma_start(X, ins["x"][0].rearrange("(t p) d -> p t d", p=P)).then_inc(sems["loaded_x"], 16)
            straight(first_pieces[:1], 0)
            sp.wait_ge(sems["params"], PARAMS)
            straight(first_pieces[1:], 0)
            expert_loads(sp, plan, 1, (up1,), down1)
            second_block_loads(sp, plan, straight)

        @block.gpsimd
        def _(pool):
            at = Tally(sems)
            pool.memset(cT, 0.0).then_inc(sems["zero_done"], 1)
            pool.memset(band, 0.0).then_inc(sems["zero_done"], 1)
            pool.memset(wdec, 0.0).then_inc(sems["zero_done"], 1)
            pool.dma_start(const1, ins["const1"]).then_inc(sems["params2"], 16)
            pool.dma_start(lam_row, ins["diff_lambda"][0:1].rearrange("o n d -> o (n d)").to_broadcast([P, 256])
                           .rearrange("p (n d) -> p n d", d=64)).then_inc(sems["params2"], 16)
            pool.wait_ge(sems["zero_done"], 3)
            for d in range(2):
                pool.dma_start(wdec[16 * d:16 * d + 16, d, :], ins["gla_w_decay"][0, d]).then_inc(sems["params2"], 16)
            pool.dma_start(router_b[:, 0:NG], ins["b_router_group"].to_broadcast([P, NG])).then_inc(sems["params2"], 16)
            pool.dma_start(router_b[:, NG:NG + NE], ins["b_router_expert"].to_broadcast([P, NE])).then_inc(sems["params2"], 16)
            for h in range(4):
                pool.dma_start(band[:, 7 * h:7 * h + 7, 48:79],
                               ins["na_rel_bias"][0, h:h + 1, 4:11, :].rearrange("o r c -> o (r c)")
                               .to_broadcast([GRID, 7 * 31]).rearrange("p (r c) -> p r c", c=31))\
                    .then_inc(sems["loaded_bias"], 16)
            pool.wait_ge(sems["loaded_bias"], 64)
            pool.dma_start(bias_dram[0:GRID * 28 * P].rearrange("(p n) -> p n", p=GRID), band_flat)\
                .then_inc(sems["bias_out"], 16)
            pool.wait_ge(sems["bias_out"], 16)
            pool.wait_ge(*at("mod_t", 12))
            pool.wait_ge(*at("mod_col", 12))
            pool.wait_ge(*at("lam"))
            pool.wait_ge(*at("gla_e", 2))
            for r in range(4):
                for h in range(4):
                    off = (7 * h + 3 - r) * P + 63
                    pitch = 28 * P - 1
                    src = bias_dram[off:off + GRID * pitch].rearrange("(q n) -> q n", n=pitch)[:, 0:4 * P]\
                        .rearrange("q (k c) -> q k c", k=4)[:, :, 0:GRID]
                    pool.dma_start(nb_bias[64 * (r % 2):64 * (r % 2) + 64, r // 2, h, :]
                                   .rearrange("q (k c) -> q k c", k=4), src).then_inc(sems["loaded_bias"], 16)
            pool.wait_ge(*at("at_masked"))
            pool.wait_ge(*at("c_used", 4))
            pool.memset(rotf[:, 0:512], 0.0).then_inc(sems["zero_pad"], 1)
            pool.wait_ge(*at("zero_pad"))
            attention_pool(pool, at, "na")
            attention_pool(pool, at, "diff")
            pool.wait_ge(*at("mixed"))
            pool.dma_start(router_w[:, :, 0:NG], ins["w_router_group"][0].rearrange("(k p) n -> p k n", p=P))\
                .then_inc(sems["router_w"], 16)
            pool.dma_start(router_w[:, :, NG:], ins["w_router_expert"][0].rearrange("(k p) n -> p k n", p=P))\
                .then_inc(sems["router_w"], 16)
            pool.dma_start(final_g, ins["final_g"].rearrange("(o n) -> o n", o=1).to_broadcast([P, D]))\
                .then_inc(sems["router_w"], 16)
            pool.memset(zeros, 0.0).then_inc(sems["zero_tile"], 1)
            second_block_pool(pool, at)
        @block.tensor
        def _(pe):
            at = Tally(sems)
            plan = Ring(sems)
            windows["pe"] = counter(pe, "window_pe")

            def piece_ready(piece):
                slot, sem, value = plan.place(dmas_of(piece))
                pe.wait_ge(sem, value)
                return slot

            def turn(dst, src):
                return pe.transpose(dst, src, ident[0:src.shape[0], 0:src.shape[0]])

            pe.wait_ge(sems["params"], PARAMS)
            turn(ps[4][:, 0:n_rows], rows[0:n_rows, :]).then_inc(sems["c_T"], 1)
            pe.wait_ge(*at("c_cols", 2))

            def modulate_mm(j):
                slot = piece_ready(("mod", j))
                w = w_cols(slot, 512)
                for k in range(KD):
                    for g in range(4):
                        mm = pe.matmul(ps[j % 2][32 * g:32 * g + 32, 0:P], cT[:, k, :], w[:, k, P * g:P * g + P],
                                       start=(k == 0), stop=(k == KD - 1))
                mm.then_inc(sems["mod_mm"], 1)

            def modulate_turn(j):
                pe.wait_ge(*at("mod_row"))
                pe.sem_inc(sems["piece_used"], 1)
                if j >= 2:
                    pe.wait_ge(sems["mod_col"], j - 1)
                turn(ps[2 + j % 2][:, 0:P], mod_row[:, j % 2, :]).then_inc(sems["mod_t"], 1)

            def modulate(j):
                modulate_mm(j)
                modulate_mm(j + 1)
                modulate_turn(j)
                modulate_turn(j + 1)

            def tokens_turn(chunks):
                for k in chunks:
                    if k >= 4:
                        pe.wait_ge(sems["xT_v" if k % 2 == 0 else "xT_s"], (k - 4) // 2 + 1)
                    for t in range(2 * NT):
                        src = (xn[:, t, :] if t < NT else cx[:, t - NT, :])[:, P * k:P * k + P]
                        mm = turn(ps[4 + k % 4][:, P * t:P * t + P], src)
                    mm.then_inc(sems["x_T"], 1)

            modulate(0)
            pe.wait_ge(*at("xn", 4))
            tokens_turn(range(4))
            modulate(2)
            tokens_turn(range(4, KD))
            pe.wait_ge(*at("xT_v", 4))
            pe.wait_ge(*at("xT_s", 4))

            where = {"qb": (0, 128, S), "kb": (128, 128, 2 * S), "rb": (256, 128, S), "gb": (0, 32, 2 * S),
                     "qn": (0, 128, S), "kn": (256, 128, 2 * S)}
            mods = iter(range(4, 12, 2))
            piece = -1
            for n, (kind, of, what, i, who) in enumerate(UNITS):
                if kind != "X" and of != piece:
                    if 2 <= of <= 5:
                        modulate(next(mods))
                    if of == 5:
                        pe.wait_ge(sems["params2"], PARAMS2)
                        pe.wait_ge(sems["unit_s"], emptied(UNITS, 5, "s"))
                        pe.wait_ge(sems["mod_row"], 12)
                        for d in range(2):
                            pe.matmul(ps[d], wdec[:, d, :], glow[0:32, :], start=True, stop=True).then_inc(sems["gate_z"], 1)
                    piece = of
                    slot = piece_ready(("win", piece))
                    w = w_cols(slot, WIN_WIDTH[piece])
                emptied_before(pe, n)
                bank = ps[4 + n % 4]
                last = n + 1 == len(UNITS) or all(u[1] != of or u[0] == "X" for u in UNITS[n + 1:])
                if kind == "T":
                    col, m, tokens = where[what]
                    for k in range(KD):
                        mm = pe.matmul(bank[0:m, 0:tokens], w[:, k, col + P * i:col + P * i + m], hT[:, k, 0:tokens],
                                       start=(k == 0), stop=(k == KD - 1))
                elif kind == "K":
                    for k in range(KD):
                        mm = pe.matmul(bank, hT[:, k, P * i:P * i + P], w[:, k, :], start=(k == 0), stop=(k == KD - 1))
                else:
                    tile = i if what == "qa" else NT + i
                    pe.wait_ge(sems["rot_tile"], tile + 1)
                    for c in range(4):
                        mm = turn(bank[:, P * c:P * c + P], rot_o[:, tile % 2, P * c:P * c + P])
                mm.then_inc(sems["unit_mm"], 1)
                if kind != "X" and last:
                    pe.wait_ge(sems["unit_mm"], n + 1)
                    pe.sem_inc(sems["piece_used"], 1)

            pe.wait_ge(sems["unit_s"], emptied(UNITS, len(UNITS), "s"))
            pe.wait_ge(sems["unit_v"], emptied(UNITS, len(UNITS), "v"))
            pe.wait_ge(*at("gla_qk", 2))
            for h in range(4):
                if h:
                    pe.wait_ge(sems["gla_at"], h)
                r = slice(32 * h, 32 * h + 32)

                def part(d, name, a, n, _r=r):
                    o = {"base_q": 768, "base_k": 1024, "ctx_q": 1280, "ctx_k": 1536}.get(name, 256 * int(name[-1])
                                                                                     if name[0] == "l" else 0)
                    return qk[_r, d, o + a:o + a + n]

                A = ps[h].rearrange("p (s t) -> p s t", s=2)

                def block_mm(dst, d, key, query, s0, t0, n, m):
                    return pe.matmul(dst, part(d, key, s0, m), part(d, query, t0, n), start=True, stop=True)

                block_mm(A[:, 0, P:2 * P], 0, "l0", "l0", 0, P, P, P)
                block_mm(A[:, 1, 0:P], 1, "l0", "l0", P, 0, P, P)
                for u in range(2):
                    o = P * u
                    block_mm(A[0:64, u, o + 64:o + 128], 0, "l1", "l1", o, o + 64, 64, 64)
                    block_mm(A[64:128, u, o:o + 64], 1, "l1", "l1", o + 64, o, 64, 64)
                    for v in range(2):
                        a, b = 64 * v, 64 * v + 32
                        block_mm(A[a:a + 32, u, o + b:o + b + 32], 0, "l2", "l2", o + a, o + b, 32, 32)
                        block_mm(A[b:b + 32, u, o + a:o + a + 32], 1, "l2", "l2", o + b, o + a, 32, 32)
                    for j in range(4):
                        a = 32 * j
                        block_mm(A[a:a + 32, u, o + a:o + a + 32], 0, "base_k", "base_q", o + a, o + a, 32, 32)
                        mm = block_mm(ps[4][a:a + 32, 64 * h + 32 * u:64 * h + 32 * u + 32], 1, "base_k", "base_q",
                                      o + a, o + a, 32, 32)
                mm.then_inc(sems["gla_at"], 1)
                if h >= 2:
                    pe.wait_ge(sems["c_sb"], h - 1)
                for s in range(2):
                    for d in range(2):
                        mm = pe.matmul(ps[5 + h % 2][:, S * s:S * s + S], part(d, "ctx_k", P * s, P),
                                       part(d, "ctx_q", 0, S), start=(d == 0), stop=(d == 1))
                mm.then_inc(sems["gla_c"], 1)
                if h >= 1:
                    context_values(pe, at, h - 1)
            context_values(pe, at, 3)
            pe.wait_ge(*at("at_masked"))
            for h in range(4):
                o = ps[7][64 * (h % 2):64 * (h % 2) + 64, S * (h // 2):S * (h // 2) + S]
                for s in range(2):
                    mm = pe.matmul(o, vbn[:, s, 64 * h:64 * h + 64], atT[:, h, s, :], start=False,
                                   stop=(s == 1), skip_group_check=True)
            mm.then_inc(sems["gla_o"], 1)
            pe.wait_ge(*at("o_sq"))
            pe.matmul(ps[4], C0["ones64"], gl_s.rearrange("p h n -> p (h n)"), start=True, stop=True)\
                .then_inc(sems["gla_ss"], 1)

            attention_pe(pe, at, "na")
            attention_pe(pe, at, "diff")
            gate_broadcast_pe(pe, at, 4)
            pe.wait_ge(*at("a_sq"))
            for b in range(2):
                mm = pe.matmul(ps[6 + b], ones, oS[:, 2 * b:2 * b + 2, :].rearrange("p h n -> p (h n)"), start=True, stop=True)
            mm.then_inc(sems["a_ss"], 1)

            out_projection_pe(pe, at, piece_ready, "wout", mixT)
            norm_pe(pe, at)
            experts_pe(pe, at, plan, 1, 0)
            second_block_pe(pe, at, plan, piece_ready)


        @block.scalar
        def _(act):
            at = Tally(sems)
            windows["act"] = counter(act, "window_act")

            def link(ins):
                ins.then_inc(sems["scalar_step"], 1)
                act.wait_ge(*at("scalar_step"))

            for name, (row, n) in row_places.items():
                src = ins[name]
                if name == "gla_norm_g":
                    for half in range(2):
                        act.dma_start(rows[row:row + 1, 64 * half:64 * half + 64], src).then_inc(sems["params"], 16)
                    continue
                act.dma_start(rows[row:row + n, :], flat_rows(src)).then_inc(sems["params"], 16)
            act.dma_start(const0, ins["const0"]).then_inc(sems["params"], 16)
            act.dma_start(cx, ins["ctx"][0].rearrange("(t p) d -> p t d", p=P)).then_inc(sems["loaded_ctx"], 16)

            act.wait_ge(*at("c_cols"))
            act.wait_ge(*at("zero_done", 3))
            act.activation(cT[:, :, 0:2], rowsT[:, 0:16].rearrange("p (i k) -> p k i", i=2), ACT.Silu)\
                .then_inc(sems["c_cols"], 1)
            act.wait_ge(sems["loaded_x"], 16)
            act.wait_ge(sems["loaded_ctx"], 16)
            for t in range(2 * NT):
                src = X[:, t, :] if t < NT else cx[:, t - NT, :]
                link(act.activation(hTf[:, D * t:D * t + D], src, ACT.Square, accum_out=ss[:, t:t + 1]))
            act.sem_inc(sems["sumsq"], 1)
            act.wait_ge(*at("mean"))
            act.activation(rstd, ss, ACT.Sqrt).then_inc(sems["sqrt_done"], 1)

            def mod_copy(j):
                act.wait_ge(*at("mod_mm"))
                if j >= 2:
                    act.wait_ge(sems["mod_t"], j - 1)
                act.activation(mod_row[:, j % 2, :], ps[j % 2][:, 0:P], ACT.Copy).then_inc(sems["mod_row"], 1)

            for j in range(4):
                mod_copy(j)
            act.wait_ge(*at("scale"))
            for k in range(1, KD, 2):
                act.wait_ge(sems["x_T"], k + 1)
                link(act.activation(hT[:, k, 0:S], ps[4 + k % 4][:, 0:S], ACT.Identity,
                                    bias=modT[:, k, 0:1], scale=scaleT[:, 0, k:k + 1]))
                act.activation(hT[:, k, S:2 * S], ps[4 + k % 4][:, S:2 * S], ACT.Identity,
                               bias=modT[:, k, 1:2], scale=scaleT[:, 1, k:k + 1]).then_inc(sems["xT_s"], 1)
            at("x_T", KD)
            def gates():
                act.wait_ge(*at("z_bias"))
                link(act.activation(ze, ze, ACT.Exp))
                act.activation(ze, ze, ACT.Ln, bias=1.0).then_inc(sems["z_ln"], 1)

            def decays():
                for d in range(2):
                    act.wait_ge(*at("gla_d"))
                    link(act.activation(qk[:, d, 0:768], qk[:, d, 0:768], ACT.Exp))
                    link(act.activation(qk[:, d, 768:1024], dif[:, 3, :], ACT.Exp, scale=1.0 if d == 0 else -1.0))
                    link(act.activation(qk[:, d, 1024:1280], dif[:, 3, :], ACT.Exp, scale=-1.0 if d == 0 else 1.0))
                    if d == 0:
                        link(act.activation(qk[:, d, 1280:1536], pre[:, d, 0, :], ACT.Exp))
                        link(act.activation(qk[:, d, 1536:1792], pre[:, d, 1, :], ACT.Exp, bias=pre[:, d, 1, S - 1:S], scale=-1.0))
                    else:
                        link(act.activation(qk[:, d, 1280:1536], pre[:, d, 0, :], ACT.Exp, bias=cols[:, 0:1], scale=-1.0))
                        link(act.activation(qk[:, d, 1536:1792], pre[:, d, 1, :], ACT.Exp))
                    act.sem_inc(sems["gla_e"], 1)

            mods = iter(range(4, 12))
            piece = -1
            act.wait_ge(sems["bias_out"], 16)
            for n, (kind, of, what, i, who) in enumerate(UNITS):
                if kind != "X" and of != piece:
                    if 2 <= of <= 5:
                        mod_copy(next(mods))
                        mod_copy(next(mods))
                    if of == 5:
                        gates()
                    piece = of
                if n == LAST_TURN + 1:
                    decays()
                if who != "s":
                    continue
                act.wait_ge(sems["unit_mm"], n + 1)
                bank = ps[4 + n % 4]
                if kind == "X":
                    dst = qaT if what == "qa" else kaT
                    ins_ = act.activation(dst[:, :, P * i:P * i + P], bank.rearrange("p (c n) -> p c n", c=4), ACT.Copy)
                elif what == "qb":
                    ins_ = act.activation(qbT, bank[:, 0:S], ACT.Copy, scale=32.0 ** -0.5)
                elif what == "gb":
                    ins_ = act.activation(glow[0:32, :], bank[0:32, :], ACT.Copy)
                elif what == "rb":
                    ins_ = act.activation(rT[:, i, :], bank[:, 0:S], ACT.Silu)
                elif what == "qn":
                    ins_ = act.activation(qnT[:, i, :], bank[:, 0:S], ACT.Copy, scale=0.125)
                elif what == "kn":
                    ins_ = act.activation(knT[:, i, :], bank, ACT.Copy)
                else:
                    ins_ = act.activation(va[:, i, :], bank, ACT.Copy)
                ins_.then_inc(sems["unit_s"], 1)

            for h in range(4):
                act.wait_ge(*at("gla_c"))
                if h >= 2:
                    act.wait_ge(sems["c_used"], h - 1)
                act.activation(ctT[:, h % 2, :, :].rearrange("p s n -> p (s n)"), ps[5 + h % 2], ACT.Copy)\
                    .then_inc(sems["c_sb"], 1)
            act.wait_ge(*at("o_sb"))
            act.activation(gl_s, gl_o, ACT.Square).then_inc(sems["o_sq"], 1)
            act.wait_ge(*at("gla_mean"))
            act.activation(gl_s, gl_s, ACT.Sqrt).then_inc(sems["gla_sqrt"], 1)
            act.wait_ge(*at("lam_sums"))
            act.activation(cols[:, 8:10], cols[:, 8:10], ACT.Exp).then_inc(sems["lam_exp"], 1)
            attention_act(act, at, "na")
            attention_act(act, at, "diff")
            act.wait_ge(*at("pv_sb", 2 + 4))
            act.activation(oS, oA, ACT.Square).then_inc(sems["a_sq"], 1)
            act.wait_ge(*at("a_mean"))
            act.activation(oS, oS, ACT.Sqrt).then_inc(sems["a_sqrt"], 1)
            norm_act(act, at, scaleT[:, 2, :], modT[:, 3 * KD:4 * KD, :])
            experts_act(act, at, 1, 0, scaleT[:, 2, :], modT[:, 3 * KD:4 * KD, :])
            squares_act(act, at)
            second_block_act(act, at, link)

        @block.vector
        def _(dve):
            at = Tally(sems)
            windows["dve"] = counter(dve, "window_dve")
            windows["cur"] = counter(dve, "experts_dve")

            def link(ins):
                ins.then_inc(sems["vector_step"], 1)
                dve.wait_ge(*at("vector_step"))

            dve.wait_ge(*at("c_T"))
            dve.tensor_copy(rowsT[:, 0:n_rows], ps[4][:, 0:n_rows]).then_inc(sems["c_cols"], 1)
            dve.wait_ge(*at("c_cols", 2))
            dve.wait_ge(*at("sumsq"))
            link(dve.tensor_scalar(ss, ss, 1.0 / D, EPS, ALU.mult, ALU.add))
            dve.reciprocal(ss, ss).then_inc(sems["mean"], 1)
            dve.wait_ge(*at("sqrt_done"))
            for t in range(2 * NT):
                src = X[:, t, :] if t < NT else cx[:, t - NT, :]
                dst = xn[:, t, :] if t < NT else cx[:, t - NT, :]
                dve.tensor_scalar(dst, src, rstd[:, t:t + 1], None, ALU.mult).then_inc(sems["xn"], 1)

            def mod_columns(j):
                dve.wait_ge(*at("mod_t"))
                dve.tensor_tensor(modT[:, 4 * j:4 * j + 4, :],
                                  ps[2 + j % 2][:, 0:P].rearrange("p (g i) -> p g i", i=32)[:, :, 0:2],
                                  PT["b_mod"][:, 4 * j:4 * j + 4].unsqueeze(2).broadcast_to([P, 4, 2]), ALU.add)\
                    .then_inc(sems["mod_col"], 1)

            for j in range(4):
                mod_columns(j)
            dve.wait_ge(*at("mod_col", 4))
            for i in range(2):
                link(dve.tensor_scalar(scaleT[:, i, :], modT[:, KD:2 * KD, i], 1.0, None, ALU.add))
                link(dve.tensor_tensor(scaleT[:, i, :], scaleT[:, i, :], PT["norm1_g"], ALU.mult))
            dve.sem_inc(sems["scale"], 1)
            for k in range(0, KD, 2):
                dve.wait_ge(sems["x_T"], k + 1)
                link(dve.tensor_scalar(hT[:, k, 0:S], ps[4 + k % 4][:, 0:S], scaleT[:, 0, k:k + 1], modT[:, k, 0:1],
                                       ALU.mult, ALU.add))
                dve.tensor_scalar(hT[:, k, S:2 * S], ps[4 + k % 4][:, S:2 * S], scaleT[:, 1, k:k + 1],
                                  modT[:, k, 1:2], ALU.mult, ALU.add).then_inc(sems["xT_v"], 1)
            at("x_T", KD)
            dve.wait_ge(sems["params2"], PARAMS2)
            link(dve.tensor_tensor(lam_row[:, 0:3:2, :], lam_row[:, 0:3:2, :], lam_row[:, 1:4:2, :], ALU.mult))
            dve.tensor_reduce(cols[:, 8:10], lam_row[:, 0:3:2, :], AX, ALU.add).then_inc(sems["lam"], 1)
            dve.wait_ge(*at("lam"))
            dve.sem_inc(sems["lam_sums"], 1)

            def rotate(bank, tile):
                cos = C1["rope_cos"][:, 64 * tile:64 * tile + 64].unsqueeze(1).broadcast_to([P, 8, 64])
                x4 = bank.rearrange("p (h a b f) -> p h a b f", h=8, a=2, b=2)
                s4 = C1["rope_sin"][:, 64 * tile:64 * tile + 64].rearrange("p (a b f) -> p a b f", a=2, b=2)
                b4 = rot_b.rearrange("p (h a b f) -> p h a b f", h=8, a=2, b=2)
                for b in range(2):
                    dve.tensor_tensor(b4[:, :, :, b, :], x4[:, :, :, 1 - b, :],
                                      s4[:, :, b, :].unsqueeze(1).broadcast_to([P, 8, 2, 16]), ALU.mult)
                return cos

            def gates():
                dve.wait_ge(*at("gate_z", 2))
                for d in range(2):
                    link(dve.tensor_scalar(zg[:, d, :], ps[d], PT["gla_b_decay"][:, d:d + 1], None, ALU.add))
                dve.scalar_tensor_tensor(ze, zg, -1.0, zg, ALU.mult, ALU.min).then_inc(sems["z_bias"], 1)
                dve.wait_ge(*at("z_ln"))
                link(dve.scalar_tensor_tensor(zg, zg, 0.0, ze, ALU.min, ALU.subtract))
                link(dve.tensor_scalar(zg, zg, 1.0 / 16.0, None, ALU.mult))
                for d in range(2):
                    for s in range(2):
                        ins_ = dve.tensor_tensor_scan(pre[:, d, s, :], ones[:, 0:1].broadcast_to([P, S]),
                                                      zg[:, d, S * s:S * s + S], 0.0, ALU.mult, ALU.add)
                link(ins_)
                link(dve.tensor_copy(cols[:, 0:1], pre[:, 1, 0, S - 1:S]))
                link(dve.tensor_tensor(pre[:, 1, :, :].rearrange("p s n -> p (s n)"),
                                       pre[:, 1, :, :].rearrange("p s n -> p (s n)"), zg[:, 1, :], ALU.subtract))

            def decayed(d):
                p = pre[:, d, 0, :]
                if d == 1:
                    dve.wait_ge(*at("gla_e"))
                for lv in range(4):
                    blk = S >> lv
                    v = p.rearrange("p (b n) -> p b n", n=blk)
                    mid = blk // 2 if (d == 1 or lv == 3) else blk // 2 - 1
                    link(dve.tensor_tensor(dif[:, lv, :].rearrange("p (b n) -> p b n", n=blk), v,
                                           v[:, :, mid:mid + 1].broadcast_to([P, S // blk, blk]), ALU.subtract))
                flat = dif[:, 0:3, :].rearrange("p l n -> p (l n)")
                dve.scalar_tensor_tensor(qk[:, d, 0:768], flat, -1.0, flat, ALU.mult, ALU.min)\
                    .then_inc(sems["gla_d"], 1)

            def products(d):
                for lv in range(3):
                    blk = S >> lv
                    view = lambda x: x.rearrange("p (b u n) -> p b u n", u=2, n=blk // 2)
                    e = view(qk[:, d, S * lv:S * lv + S])
                    for u in range(2):
                        who = view(qbT if (u == 1) == (d == 0) else kbT[:, 0:S])
                        dve.tensor_tensor(e[:, :, u, :], e[:, :, u, :], who[:, :, u, :], ALU.mult)
                for o, who in ((768, qbT), (1024, kbT[:, 0:S]), (1280, qbT), (1536, kbT[:, S:2 * S])):
                    e = qk[:, d, o:o + S]
                    ins_ = dve.tensor_tensor(e, e, who, ALU.mult)
                ins_.then_inc(sems["gla_qk"], 1)

            def decayed_parts():
                decayed(0)
                dve.wait_ge(sems["unit_mm"], LAST_TURN + 1)
                decayed(1)
                products(0)
                dve.wait_ge(*at("gla_e"))
                products(1)

            tiles = 0
            mods = iter(range(4, 12))
            piece = -1
            dve.wait_ge(sems["bias_out"], 16)
            for n, (kind, of, what, i, who) in enumerate(UNITS):
                if kind != "X" and of != piece:
                    if 2 <= of <= 5:
                        mod_columns(next(mods))
                        mod_columns(next(mods))
                    if of == 5:
                        gates()
                    piece = of
                if n == LAST_TURN + 1:
                    decayed_parts()
                if who != "v":
                    continue
                dve.wait_ge(sems["unit_mm"], n + 1)
                bank = ps[4 + n % 4]
                if what == "kb":
                    dve.tensor_copy(kbT, bank).then_inc(sems["unit_v"], 1)
                elif what == "vbn":
                    dve.tensor_copy(vbn[:, i, :], bank).then_inc(sems["unit_v"], 1)
                elif what == "qn":
                    dve.tensor_scalar(qnT[:, i, :], bank[:, 0:S], 0.125, None, ALU.mult).then_inc(sems["unit_v"], 1)
                elif what == "kn":
                    dve.tensor_copy(knT[:, i, :], bank).then_inc(sems["unit_v"], 1)
                elif what == "va":
                    dve.tensor_copy(va[:, i, :], bank).then_inc(sems["unit_v"], 1)
                else:
                    if tiles >= 2:
                        turned = [m for m, u in enumerate(UNITS) if u[0] == "X"][tiles - 2]
                        dve.wait_ge(sems["unit_mm"], turned + 1)
                    o = rot_o[:, tiles % 2, :]
                    if i < NT:
                        if tiles:
                            dve.wait_ge(sems["rot_tile"], tiles)
                        cos = rotate(bank, i)
                        x3 = bank.rearrange("p (h n) -> p h n", h=8)
                        dve.tensor_tensor(o.rearrange("p (h n) -> p h n", h=8), x3, cos, ALU.mult)\
                            .then_inc(sems["unit_v"], 1)
                        dve.wait_ge(sems["unit_v"], emptied(UNITS, n + 1, "v"))
                        dve.tensor_tensor(o, o, rot_b, ALU.add).then_inc(sems["rot_tile"], 1)
                    else:
                        dve.tensor_copy(o, bank).then_inc(sems["unit_v"], 1)
                        dve.wait_ge(sems["unit_v"], emptied(UNITS, n + 1, "v"))
                        dve.sem_inc(sems["rot_tile"], 1)
                    tiles += 1

            lim = 3.0e38
            for h in range(4):
                dve.wait_ge(*at("gla_at"))
                link(dve.tensor_scalar(atT[:, h, :, :].rearrange("p s n -> p (s n)"), ps[h], lim, -lim, ALU.min, ALU.max))
                for j in range(4):
                    rows_ = slice(32 * j, 32 * j + 32)
                    dg = diagonal(rows_, h, 32 * j)
                    dve.tensor_tensor(dg, dg, C1["mask_fwd"][rows_, :].unsqueeze(1).broadcast_to([32, 2, 32]), ALU.mult)
            link(dve.tensor_scalar(at_b, ps[4][:, 0:S], lim, -lim, ALU.min, ALU.max))
            b3 = at_b.rearrange("p (g n) -> p g n", n=32)
            link(dve.tensor_tensor(b3, b3, C1["mask_bwd"].unsqueeze(1).broadcast_to([P, 8, 32]), ALU.mult))
            for j in range(4):
                rows_ = slice(32 * j, 32 * j + 32)
                for h in range(4):
                    dg = diagonal(rows_, h, 32 * j)
                    ins_ = dve.tensor_tensor(dg, dg, b3[rows_, 2 * h:2 * h + 2, :], ALU.add)
            ins_.then_inc(sems["at_masked"], 1)
            dve.wait_ge(sems["loaded_bias"], 64 + 16 * 16)
            for t in range(NT):
                b4 = nb_bias[:, t, :, :].rearrange("p h (k c) -> p (h k) c", c=GRID)
                ins_ = dve.tensor_tensor(b4, b4, C1["nb_mask"].unsqueeze(1).broadcast_to([P, 16, GRID]), ALU.add)
            link(ins_)
            dve.wait_ge(*at("gla_o"))
            dve.tensor_copy(gl_o.rearrange("p h n -> p (h n)"), ps[7]).then_inc(sems["o_sb"], 1)
            dve.wait_ge(*at("gla_ss"))
            g2 = gl_s.rearrange("p h n -> p (h n)")
            link(dve.tensor_scalar(g2, ps[4], 1.0 / 64, EPS, ALU.mult, ALU.add))
            dve.reciprocal(g2, g2).then_inc(sems["gla_mean"], 1)
            dve.wait_ge(*at("gla_sqrt"))
            link(dve.scalar_tensor_tensor(gl_o, gl_o, PT["gla_norm_g"], gl_s, ALU.mult, ALU.mult))
            dve.tensor_tensor(mixT[:, 4:6, :], gl_o, rT, ALU.mult).then_inc(sems["gla_y"], 1)
            dve.wait_ge(*at("gla_y"))

            dve.wait_ge(*at("lam_exp"))
            link(dve.tensor_tensor(cols[:, 10:11], cols[:, 9:10], cols[:, 8:9], ALU.subtract))
            link(dve.tensor_scalar(cols[:, 10:11], cols[:, 10:11], -LAM_INIT, None, ALU.add))
            link(dve.tensor_scalar(cols[:, 11:12], PT["diff_sub_g"], 1.0 - LAM_INIT, None, ALU.mult))
            attention_dve(dve, at, link, "na")
            attention_dve(dve, at, link, "diff")
            gate_diagonals_dve(dve, at, 2)
            dve.wait_ge(*at("a_ss"))
            for b in range(2):
                half = oS[:, 2 * b:2 * b + 2, :].rearrange("p h n -> p (h n)")
                link(dve.tensor_scalar(half, ps[6 + b], 1.0 / P, EPS, ALU.mult, ALU.add))
            dve.reciprocal(oS, oS).then_inc(sems["a_mean"], 1)
            dve.wait_ge(*at("a_sqrt"))
            dve.scalar_tensor_tensor(mixT[:, 0:4, :], oA, cols[:, 11:12], oS, ALU.mult, ALU.mult)\
                .then_inc(sems["mixed"], 1)
            dve.wait_ge(*at("mixed"))
            gate_dve(dve, at, link, 4)
            link(dve.tensor_scalar(scaleT[:, 2, :], modT[:, 4 * KD:5 * KD, 0], 1.0, None, ALU.add))
            link(dve.tensor_tensor(scaleT[:, 2, :], scaleT[:, 2, :], PT["norm2_g"], ALU.mult))
            residual_dve(dve, at, link, 0, "out_mm", gated=True)
            norm_dve(dve, at, link, scaleT[:, 2, :], modT[:, 3 * KD:4 * KD, :])
            route_dve(dve, at, link, 1)
            experts_dve(dve, at, link, 1, 0, scaleT[:, 2, :], modT[:, 3 * KD:4 * KD, :])
            residual_dve(dve, at, link, 4, "moe_mm", gated=True)
            dve.wait_ge(*at("router_w", 48))
            final_dve(dve, at, link)
            second_block_dve(dve, at, link)



INS = ["x", "ctx", "c", "c_ctx", "w_mod", "b_mod", "norm1_g", "norm2_g", "w_in", "w_out", "diff_lambda", "diff_sub_g",
       "gla_w_decay", "gla_b_decay", "gla_norm_g", "na_rel_bias", "w_router_group", "b_router_group",
       "w_router_expert", "b_router_expert", "w_expert_up", "w_expert_down", "final_g", "norm1_g_2", "w_in_2",
       "q_norm_g_2", "w_uq_2", "kv_norm_g_2", "w_ukv_2", "pool_w_2", "pool_scale_2", "w_out_2", "norm2_g_2",
       "w_group_2", "b_group_2", "w_expert_2", "b_expert_2", "w_gate_2", "w_up_2", "w_down_2", "final_g_2"]
SCRATCH = GRID * 28 * P + 32 * P


def kernel(**inputs):
    import concourse.bacc as bacc
    from concourse.bass_utils import run_bass_kernel_spmd

    arrays = {n: np.ascontiguousarray(inputs[n]) for n in INS}
    arrays.update(shape_constants())
    nc = bacc.Bacc("TRN2", target_bir_lowering=False, num_devices=1)
    ins = {n: nc.dram_tensor(f"in_{n}", a.shape, F32, kind="ExternalInput").ap() for n, a in arrays.items()}
    ins["bias_scratch"] = nc.dram_tensor("bias_scratch", [SCRATCH], F32, kind="Internal").ap()
    out = nc.dram_tensor("out", [1, S, D], F32, kind="ExternalOutput").ap()
    hybrid_kernel(nc, ins, out)
    result = run_bass_kernel_spmd(nc, [{f"in_{n}": a for n, a in arrays.items()}], core_ids=[0])
    return result.results[0]["out"]
```
